# Optimizing a Trainium2 kernel written in Bass

```python
import jax, jax.numpy as jnp
from jax import lax
import numpy as np

D_MODEL = 1024
BATCH = 1
SEQ = 1024
DEPTH = 2
DEC_BATCH = 8
DEC_SEQ = 8
PAST_LEN = 8192
PAGE_SIZE = 128

N_MIXERS = 2
N_POOL_LAYERS = (DEPTH + 1) // 2
N_GLA_LAYERS = DEPTH // 2
EXPAND = 2
D_INNER = EXPAND * D_MODEL
POOL_WINDOWS = (2, 4, 8, 16)
N_POOL_GROUPS = len(POOL_WINDOWS)
POOL_GROUP = D_INNER // N_POOL_GROUPS
POOL_BUF = max(POOL_WINDOWS) - 1
GLA_HEADS = 4
GLA_DK = D_MODEL // 2
GLA_DV = D_INNER
GLA_HK = GLA_DK // GLA_HEADS
GLA_HV = GLA_DV // GLA_HEADS
GLA_RANK = 16
GLA_GATE_NORM = 16.0
GLA_CHUNK = 32
GLA_IN = 2 * GLA_DK + 2 * GLA_DV + GLA_RANK
EPS = 1e-6
F32 = jnp.float32

kernel_name = 'hybrid_pool_gla_adaln_step'

def rmsnorm(x, g):
    xf = x.astype(F32)
    y = xf * lax.rsqrt(jnp.mean(xf * xf, axis=-1, keepdims=True) + EPS)
    return (y * g.astype(F32)).astype(x.dtype)

def pool_mix(u, buf, pos0, w_grp, scale):
    b, L, _ = u.shape
    ext = jnp.concatenate([buf.astype(F32), u.astype(F32)], axis=1)
    cs = jnp.concatenate([jnp.zeros((b, 1, D_INNER), F32), jnp.cumsum(ext, axis=1)], axis=1)
    cs = cs.reshape(b, POOL_BUF + L + 1, N_POOL_GROUPS, POOL_GROUP)
    pos = pos0 + jnp.arange(L)
    hi = POOL_BUF + 1
    means = []
    for gi, w in enumerate(POOL_WINDOWS):
        s = cs[:, hi:hi + L, gi] - cs[:, hi - w:hi - w + L, gi]
        cnt = jnp.minimum(pos + 1, w).astype(F32)
        means.append(s / cnt[None, :, None])
    mean = jnp.stack(means, axis=2)
    diff = mean - ext[:, POOL_BUF:].reshape(b, L, N_POOL_GROUPS, POOL_GROUP)
    mixed = jnp.einsum('blgc,gcd->blgd', diff, w_grp.astype(F32)).reshape(b, L, D_INNER)
    return mixed * scale.astype(F32), ext[:, -POOL_BUF:]

def pool_branch(h, buf, pos0, w_in, w_grp, scale, w_out):
    uz = h @ w_in
    u, z = jnp.split(uz, 2, axis=-1)
    mixed, new_buf = pool_mix(u, buf, pos0, w_grp, scale)
    y = (mixed * jax.nn.silu(z.astype(F32))).astype(h.dtype) @ w_out
    return y, new_buf.astype(buf.dtype)

def gla_recurrence(q, k, v, lg, s0):
    b, L, H, _ = q.shape
    C = GLA_CHUNK
    n = -(-L // C)
    pad = n * C - L

    def chunks(a):
        a = jnp.pad(a.astype(F32), ((0, 0), (0, pad), (0, 0), (0, 0)))
        return a.reshape(b, n, C, H, a.shape[-1]).transpose(1, 0, 3, 2, 4)

    q, k, v, lg = chunks(q), chunks(k), chunks(v), chunks(lg)
    bcum = jnp.cumsum(lg, axis=3)
    blast = bcum[:, :, :, -1:]
    q_dec = q * jnp.exp(bcum)
    k_intra = k * jnp.exp(-bcum)
    k_state = k * jnp.exp(blast - bcum)
    causal = jnp.tril(jnp.ones((C, C), bool))
    att = jnp.where(causal, jnp.einsum('nbhid,nbhjd->nbhij', q_dec, k_intra), 0.0)
    o_intra = jnp.einsum('nbhij,nbhje->nbhie', att, v)

    def step(s, inp):
        qc, kc, vc, dc = inp
        o_inter = jnp.einsum('bhid,bhde->bhie', qc, s)
        s = dc[..., None] * s + jnp.einsum('bhjd,bhje->bhde', kc, vc)
        return s, o_inter

    s_fin, o_inter = lax.scan(step, s0.astype(F32), (q_dec, k_state, v, jnp.exp(blast[:, :, :, 0])))
    o = (o_intra + o_inter).transpose(1, 0, 3, 2, 4).reshape(b, n * C, H, -1)[:, :L]
    return o, s_fin

def gla_branch(h, s0, w_in, w_gate_up, b_gate, norm_g, w_out):
    b, L, _ = h.shape
    proj = h @ w_in
    q, k, v, z, gl = jnp.split(proj, [GLA_DK, 2 * GLA_DK, 2 * GLA_DK + GLA_DV, 2 * GLA_DK + 2 * GLA_DV], axis=-1)
    lg = jax.nn.log_sigmoid((gl @ w_gate_up + b_gate).astype(F32)) / GLA_GATE_NORM
    q = q.astype(F32).reshape(b, L, GLA_HEADS, GLA_HK) * (GLA_HK ** -0.5)
    k = k.reshape(b, L, GLA_HEADS, GLA_HK)
    v = v.reshape(b, L, GLA_HEADS, GLA_HV)
    lg = lg.reshape(b, L, GLA_HEADS, GLA_HK)
    o, s_new = gla_recurrence(q, k, v, lg, s0)
    o = o * lax.rsqrt(jnp.mean(o * o, axis=-1, keepdims=True) + EPS)
    o = o.reshape(b, L, GLA_DV) * norm_g.astype(F32)
    y = (o * jax.nn.silu(z.astype(F32))).astype(h.dtype) @ w_out
    return y, s_new.astype(s0.dtype)

def run_trunk(x, c, pool_bufs, gla_states, pos0, ada_w, ada_b, norm_g, pool_w_in, pool_w_grp, pool_scale,
              pool_w_out, gla_w_in, gla_w_gate_up, gla_b_gate, gla_norm_g, gla_w_out, final_g):
    new_pool, new_gla = [], []
    cs = jax.nn.silu(c)
    for li in range(DEPTH):
        mod = cs @ ada_w[li] + ada_b[li]
        shift, scale, gate = jnp.split(mod, 3, axis=-1)
        h = rmsnorm(x, norm_g[li]) * (1.0 + scale[:, None]) + shift[:, None]
        j = li // N_MIXERS
        if li % N_MIXERS == 0:
            y, st = pool_branch(h, pool_bufs[j], pos0, pool_w_in[j], pool_w_grp[j], pool_scale[j], pool_w_out[j])
            new_pool.append(st)
        else:
            y, st = gla_branch(h, gla_states[j], gla_w_in[j], gla_w_gate_up[j], gla_b_gate[j], gla_norm_g[j], gla_w_out[j])
            new_gla.append(st)
        x = x + gate[:, None] * y
    return rmsnorm(x, final_g), jnp.stack(new_pool), jnp.stack(new_gla)

def setup_inputs(seed: int = 0) -> dict:
    key = jax.random.key(seed)
    ks = jax.random.split(key, 20)
    nrm = lambda k, s, sc: jax.random.normal(k, s, F32) * sc
    return {
        'x_prompt': nrm(ks[0], (BATCH, SEQ, D_MODEL), 1.0),
        'x_sample': nrm(ks[1], (DEC_BATCH, DEC_SEQ, D_MODEL), 1.0),
        'c_prompt': nrm(ks[2], (BATCH, D_MODEL), 1.0),
        'c_sample': nrm(ks[3], (DEC_BATCH, D_MODEL), 1.0),
        'state_pool': nrm(ks[4], (N_POOL_LAYERS, DEC_BATCH, POOL_BUF, D_INNER), 1.0),
        'state_gla': nrm(ks[5], (N_GLA_LAYERS, DEC_BATCH, GLA_HEADS, GLA_HK, GLA_HV), 1.0),
        'ada_w': nrm(ks[6], (DEPTH, D_MODEL, 3 * D_MODEL), 0.5 * D_MODEL ** -0.5),
        'ada_b': nrm(ks[7], (DEPTH, 3 * D_MODEL), 0.02),
        'norm_g': 1.0 + nrm(ks[8], (DEPTH, D_MODEL), 0.02),
        'pool_w_in': nrm(ks[9], (N_POOL_LAYERS, D_MODEL, 2 * D_INNER), D_MODEL ** -0.5),
        'pool_w_grp': nrm(ks[10], (N_POOL_LAYERS, N_POOL_GROUPS, POOL_GROUP, POOL_GROUP), POOL_GROUP ** -0.5),
        'pool_scale': 1.0 + nrm(ks[11], (N_POOL_LAYERS, D_INNER), 0.02),
        'pool_w_out': nrm(ks[12], (N_POOL_LAYERS, D_INNER, D_MODEL), D_INNER ** -0.5),
        'gla_w_in': nrm(ks[13], (N_GLA_LAYERS, D_MODEL, GLA_IN), D_MODEL ** -0.5),
        'gla_w_gate_up': nrm(ks[14], (N_GLA_LAYERS, GLA_RANK, GLA_DK), GLA_RANK ** -0.5),
        'gla_b_gate': nrm(ks[15], (N_GLA_LAYERS, GLA_DK), 0.1),
        'gla_norm_g': 1.0 + nrm(ks[16], (N_GLA_LAYERS, GLA_DV), 0.02),
        'gla_w_out': nrm(ks[17], (N_GLA_LAYERS, GLA_DV, D_MODEL), GLA_DV ** -0.5),
        'final_g': 1.0 + nrm(ks[18], (D_MODEL,), 0.02),
    }

def reference(x_prompt, x_sample, c_prompt, c_sample, state_pool, state_gla, ada_w, ada_b, norm_g,
              pool_w_in, pool_w_grp, pool_scale, pool_w_out, gla_w_in, gla_w_gate_up, gla_b_gate,
              gla_norm_g, gla_w_out, final_g):
    weights = (ada_w, ada_b, norm_g, pool_w_in, pool_w_grp, pool_scale, pool_w_out,
               gla_w_in, gla_w_gate_up, gla_b_gate, gla_norm_g, gla_w_out, final_g)
    pool0 = jnp.zeros((N_POOL_LAYERS, BATCH, POOL_BUF, D_INNER), x_prompt.dtype)
    gla0 = jnp.zeros((N_GLA_LAYERS, BATCH, GLA_HEADS, GLA_HK, GLA_HV), x_prompt.dtype)
    y_prompt, pool_prompt, gla_prompt = run_trunk(x_prompt, c_prompt, pool0, gla0, 0, *weights)
    y_sample, pool_sample, gla_sample = run_trunk(x_sample, c_sample, state_pool, state_gla, PAST_LEN, *weights)
    return (y_prompt, y_sample, pool_prompt, gla_prompt, pool_sample, gla_sample)


_drawn_inputs = setup_inputs


def setup_inputs(seed=0):
    import zlib

    import numpy as np

    out = dict(_drawn_inputs(seed))
    spreads = {}
    factors = {'pool_scale': 8.0, 'gla_norm_g': 8.0, 'final_g': 2.896}
    for name, (base, spread) in spreads.items():
        noise = np.random.default_rng([zlib.crc32(name.encode()), seed]).standard_normal(out[name].shape)
        drawn = base * np.exp(spread * noise) if base else spread * noise
        out[name] = __import__('jax').numpy.asarray(drawn.astype(out[name].dtype))
    for name, factor in factors.items():
        out[name] = (out[name] * factor).astype(out[name].dtype)
    return out
```

```python
import concourse.bass as bass
from concourse import mybir
from contextlib import ExitStack

P = 128
D = 1024
DI = 2048
KD = D // P
NG = 4
GW = DI // NG
KG = GW // P
TP = 1024
NB = 8
TS = 8
NS = NB * TS
T = TP + NS
BUF = 15
SEG = BUF + TS
WE = BUF + TP + NB * SEG
SE0 = BUF + TP
RANK = 16
CH = 32
SUP = 4 * CH
NSUP = TP // SUP
EPS = 1e-6
NC_ = 1 + NB
NT = [(0, 364), (364, 362), (726, 362)]
N2P = TP - NT[2][0]
V_ADAB, V_NG, V_PS, V_BG, V_GN, V_FG = 0, 48, 64, 80, 84, 100
NVEC = 108

POOL_PLAN = [("U0", 1, 1), ("U1", 1, 1), ("U2", 1, 1), ("U3", 1, 1), ("Z0", 1, 1),
             ("G01", 1, 2), ("G23", 1, 2), ("Z1", 1, 1), ("Z2", 1, 1), ("Z3", 1, 1),
             ("O01", 1, 2), ("O23", 1, 2), ("O45", 1, 2), ("O67", 1, 2)]
GLA_PLAN = [("Q", 1, 1), ("K", 1, 1), ("LG", 0, 1), ("V0", 1, 1), ("V1", 1, 1), ("VT0", 0, 1),
            ("V2", 1, 1), ("VT1", 0, 1), ("V3", 1, 1), ("VT2", 0, 1), ("Z0", 1, 1), ("VT3", 0, 1),
            ("ATT", 0, 2), ("Z1", 1, 1), ("NRM", 0, 1), ("Z2", 1, 1), ("Z3", 1, 1),
            ("O01", 1, 2), ("O23", 1, 2), ("O45", 1, 2), ("O67", 1, 2)]


class Plan:

    def __init__(self, rows):
        self.unit, self.slot, self.names, self.after = {}, {}, [], []
        u = 0
        for name, slots, units in rows:
            self.unit[name] = u
            u += units
            if slots:
                self.slot[name] = len(self.names)
                self.names.append(name)
                self.after.append(u)
        self.units, self.slots = u, len(self.names)


def trunk(nc, x_prompt, x_sample, c_prompt, c_sample, state_pool, state_gla, ada_w, ada_b, norm_g,
          pool_w_in, pool_w_grp, pool_scale, pool_w_out, gla_w_in, gla_w_gate_up, gla_b_gate,
          gla_norm_g, gla_w_out, final_g, y_prompt, y_sample, new_pool_prompt, new_gla_prompt,
          new_pool_sample, new_gla_sample):
    f32, f32r, i8 = mybir.dt.float32, mybir.dt.float32r, mybir.dt.int8
    ACT, ALU = mybir.ActivationFunctionType, mybir.AluOpType
    ds = bass.ds
    PP, GP = Plan(POOL_PLAN), Plan(GLA_PLAN)
    ctx = ExitStack()
    with ctx:
        def sb(name, shape, dt=f32, stack=ctx):
            return stack.enter_context(nc.sbuf_tensor(name, shape, dt))

        ident = sb("ident", [P, P])
        ones = sb("ones", [P, P])
        causal = sb("causal", [P, P], i8)
        causal_s = sb("causal_s", [NS, NS], i8)
        seq_rows = sb("seq_rows", [NS, NB])
        vecT = sb("vecT", [P, NVEC])
        csT = sb("csT", [P, KD, NC_])
        mods = [sb("mod0", [P, 24, NC_]), sb("mod1", [P, 24, NC_])]
        win_on = sb("win_on", [P, NG, 3])
        win_inv = sb("win_inv", [P, NG])
        cnt_inv = sb("cnt_inv", [P, NG, 16])
        eps = sb("eps", [P, 1])
        gs_tmp = sb("gs_tmp", [P, NS])
        xT = sb("xT", [P, KD, T])
        oT = sb("oT", [P, KG, T])
        stage = sb("stage", [P, 2, 1024])
        w_hi = sb("w_hi", [P, 2, 1024], f32r)
        w_lo = sb("w_lo", [P, 2, 1024], f32r)
        G = sb("G", [P, WE + 1])
        PQ = sb("PQ", [P, 2568])
        SZ = sb("SZ", [P, T])
        early = ExitStack()
        ada_stage = sb("ada_stage", [P, KD, P], stack=early)
        hist = sb("hist", [NB * BUF, 2, P], stack=early)
        tail_out = sb("tail_out", [NS + BUF, 2, P], stack=early)
        tail = sb("tail", [P, NS + BUF], stack=early)
        early.close()
        low_rank = ExitStack()
        w_gl = sb("w_gl", [P, KD, RANK], stack=low_rank)
        w_gl_hi = sb("w_gl_hi", [P, KD, RANK], f32r, stack=low_rank)
        w_gl_lo = sb("w_gl_lo", [P, KD, RANK], f32r, stack=low_rank)
        low_rank.close()
        S = sb("S", [P, GW])
        qd = sb("qd", [P, SUP])
        qs = sb("qs", [P, SUP])
        ks = sb("ks", [P, SUP])
        ksT = sb("ksT", [P, 2, P])
        att = sb("att", [P, 2, SUP])
        att_s = sb("att_s", [NS, NS])
        ksm = sb("ksm", [NS, 2, P])
        dec = sb("dec", [P, NSUP + NB])
        w_up = sb("w_up", [RANK, P])
        start = ExitStack()
        ada0 = sb("ada0", [P, 6, KD, 512], stack=start)
        start.close()
        end = ExitStack()
        y_rows = sb("y_rows", [P, 4, D], stack=end)
        end.close()
        h_hi = sb("h_hi", [P, KD, T], f32r)
        h_lo = sb("h_lo", [P, KD, T], f32r)
        heads = ExitStack()
        v = sb("v", [P, NSUP + 1, GW], stack=heads)
        qT = sb("qT", [P, T], stack=heads)
        kT = sb("kT", [P, T], stack=heads)
        L = sb("L", [P, T], stack=heads)
        Kp = sb("Kp", [P, 4, SUP], stack=heads)
        heads.close()
        a_hi = sb("a_hi", [P, KG, T], f32r)
        a_lo = sb("a_lo", [P, KG, T], f32r)

        s1 = PQ[:, 0:WE]
        s2 = PQ[:, 1300:1300 + WE]
        vT = [PQ[:, 0:T], PQ[:, 1300:1300 + T]]
        S0 = [PQ[:, 0:GW], PQ[:, GW:2 * GW], PQ[:, 2 * GW:3 * GW], PQ[:, 3 * GW:4 * GW]]
        sq4 = PQ[:, 0:4 * 364].rearrange("p (k n) -> p k n", k=4)
        acc = PQ[:, 1480:1480 + T]
        sqx = [PQ[:, i * 364:(i + 1) * 364] for i in range(4)]
        ht = [PQ[:, (4 + i) * 364:(5 + i) * 364] for i in range(3)]
        hs = G[:, 0:KD * NS].rearrange("p (k t) -> p k t", k=KD)
        xrow = [G[:, 0:D], PQ[:, 0:D], PQ[:, 1300:1300 + D], SZ[:, 0:D]]
        rstd = SZ
        vec_rows = oT[0:NVEC, 0, 0:P]
        c_rows = oT[0:NC_, 1, 0:D]
        glT = G[0:RANK, 0:T]

        psA = ctx.enter_context(nc.psum_tensor("psA", [P, 3, 512], f32))
        psB = ctx.enter_context(nc.psum_tensor("psB", [P, 3, 512], f32))
        ps = [psA, psB]
        X = [ctx.enter_context(nc.psum_tensor(f"X{i}", [P, 512], f32)) for i in range(2)]

        def sem(name):
            return ctx.enter_context(nc.semaphore(name))

        c_loaded, vec_loaded, consts_ready = sem("c_loaded"), sem("vec_loaded"), sem("consts_ready")
        x_loaded = [sem(f"x_loaded{i}") for i in range(4)]
        ada0_loaded = [sem(f"ada0_loaded{i}") for i in range(6)]
        cT_done, vT_done, cs_ready, vec_ready = sem("cT_done"), sem("vecT_done"), sem("cs_ready"), sem("vec_ready")
        xT_done, xT_ready = sem("xT_done"), sem("xT_ready")
        mod_done, mod_ready = sem("mod_done"), sem("mod_ready")
        sq_ready, ss_done, std_ready, rstd_ready = sem("sq_ready"), sem("ss_done"), sem("std_ready"), sem("rstd_ready")
        ht_ready, hhi_ready, h_ready, hs_ready, hshi_ready = (sem("ht_ready"), sem("hhi_ready"), sem("h_ready"),
                                                              sem("hs_ready"), sem("hshi_ready"))
        x_final = sem("x_final")
        copied = sem("copied")
        chain_v, chain_a, chain_p = sem("chain_v"), sem("chain_a"), sem("chain_p")
        y_ready, yT_done, y_evac = sem("y_ready"), sem("yT_done"), [sem("y_evac_a"), sem("y_evac_v")]
        y_stored = [sem(f"y_stored{i}") for i in range(4)]

        class Stream:

            def __init__(self, tag):
                self.w_loaded = [sem(f"{tag}_w_loaded{i}") for i in range(2)]
                self.hi_done = sem(f"{tag}_hi_done")
                self.lo_done = sem(f"{tag}_lo_done")
                self.unit_done = sem(f"{tag}_unit_done")
                self.evac = [sem(f"{tag}_evac{i}") for i in range(2)]
                self.act_ready = sem(f"{tag}_gated")

        L0, L1 = Stream("pool"), Stream("gla")
        ada_loaded, mini_done, mini_free = sem("ada_loaded"), sem("mini_done"), sem("mini_free")
        hist_loaded, hist_T, hist_evac = [sem("hist_loaded0"), sem("hist_loaded1")], sem("hist_T"), sem("hist_evac")
        pooled, diff_ready = sem("pooled"), sem("diff_ready")
        tail_stored = [sem("tail_stored0"), sem("tail_stored1")]
        wgl_loaded, wgl_hi, wgl_lo, gl_done, gl_ready = (sem("wgl_loaded"), sem("wgl_hi"), sem("wgl_lo"),
                                                          sem("gl_done"), sem("gl_ready"))
        wup_loaded, sp_ready, lg_ready = sem("wup_loaded"), sem("sp_ready"), sem("lg_ready")
        dec_ready = sem("dec_ready")
        kp_zero, kp_exp, kp_ready = sem("kp_zero"), sem("kp_exp"), sem("kp_ready")
        qd_arg, qd_exp, qd_ready = sem("qd_arg"), sem("qd_exp"), sem("qd_ready")
        qs_exp, qs_ready, ks_exp, ks_ready = sem("qs_exp"), sem("qs_ready"), sem("ks_exp"), sem("ks_ready")
        att_done, att_ready, o_done, o_evac = sem("att_done"), sem("att_ready"), sem("o_done"), sem("o_evac")
        kT_done, ksT_ready, upd_done, S_ready = sem("kT_done"), sem("ksT_ready"), sem("upd_done"), sem("S_ready")
        smp_arg, smp_exp, smp_ready = sem("smp_arg"), sem("smp_exp"), sem("smp_ready")
        smp_att, smp_attr, smp_kT, ksm_ready = sem("smp_att"), sem("smp_attr"), sem("smp_kT"), sem("ksm_ready")
        s0_loaded = [sem(f"s0_loaded{i}") for i in range(4)]
        s0_stored = [sem(f"s0_stored{i}") for i in range(4)]
        s0_ready, smp_inter, smp_upd = sem("s0_ready"), sem("smp_inter"), sem("smp_upd")
        S_stored = sem("S_stored")
        osq_ready, oacc_ready, ostd_ready = sem("osq_ready"), sem("oacc_ready"), sem("ostd_ready")

        def units(plan, g, n):
            return g * plan.units + n + 3

        def evacs(plan, g, u):
            return g * (plan.units // 2) + u // 2 + 2

        def token_parts():
            return [(0, 0, 0, 364), (1, 364, 0, 362), (2, 726, 0, N2P)]

        def wait_apart(eng, what, count):
            count = eng.to_reg(count)
            eng.wait_ge(vec_ready, 1)
            eng.wait_ge(what, count)

        def split_slot(lay, plan, eng, g, j):
            before = plan.after[j - 2] if j >= 2 else plan.after[j - 2] - plan.units
            eng.wait_ge(lay.unit_done, units(plan, g, before))
            eng.wait_ge(lay.w_loaded[j % 2], 16 * (plan.slots // 2) * g + 16 * (j // 2 + 1))
            nc.scalar.activation(w_hi[:, j % 2, :], stage[:, j % 2, :], ACT.Copy).then_inc(lay.hi_done, 1)

        def lo_slots(lay, plan, eng, g, j):
            eng.wait_ge(lay.hi_done, g * plan.slots + j + 1)
            nc.gpsimd.tensor_tensor(w_lo[:, j % 2, :], stage[:, j % 2, :], w_hi[:, j % 2, :].bitcast(f32),
                                    ALU.subtract).then_inc(lay.lo_done, 1)

        def slot_free(lay, plan, g, j, eng):
            wait_apart(eng, lay.lo_done, g * plan.slots + j + 1)

        def norm_squares(act, r, x_here):
            act.wait_ge(*x_here)
            i = 24 * r
            for t, (n0, w) in enumerate(NT):
                for k in range(KD):
                    if i - 24 * r >= 4:
                        act.wait_ge(ss_done, i - 3)
                    nc.scalar.activation(sqx[i % 4][:, 0:w], xT[:, k, n0:n0 + w], ACT.Square).then_inc(sq_ready, 1)
                    i += 1
            for t, (n0, w) in enumerate(NT):
                act.wait_ge(ss_done, 24 * r + 8 * t + 8)
                nc.scalar.activation(rstd[:, n0:n0 + w], ps[1][:, t, 0:w], ACT.Sqrt, bias=eps[:, 0:1],
                                     scale=1.0 / D).then_inc(std_ready, 1)

        def norm_sums(pe, r):
            i = 24 * r
            for t, (n0, w) in enumerate(NT):
                for k in range(KD):
                    pe.wait_ge(sq_ready, i + 1)
                    nc.tensor.matmul(ps[1][:, t, 0:w], ones[:], sqx[i % 4][:, 0:w], start=(k == 0),
                                     stop=(k == KD - 1)).then_inc(ss_done, 1)
                    i += 1

        def h_vector(dve, r, mod):
            for t, (n0, w) in enumerate(NT):
                dve.wait_ge(std_ready, 3 * r + t + 1)
                nc.vector.reciprocal(rstd[:, n0:n0 + w], rstd[:, n0:n0 + w]).then_inc(rstd_ready, 1)
            dve.wait_ge(rstd_ready, 3 * r + 3)
            i = 24 * r

            def low(i):
                t, k = (i - 24 * r) // KD, i % KD
                n0, w = token_parts()[t][1], token_parts()[t][3]
                dve.wait_ge(hhi_ready, i + 1)
                nc.vector.scalar_tensor_tensor(
                    out=h_lo[:, k, n0:n0 + w], in0=ht[i % 3][:, 0:w], scalar=mod[:, k, 0:1],
                    in1=h_hi[:, k, n0:n0 + w].bitcast(f32), op0=ALU.add, op1=ALU.subtract).then_inc(h_ready, 1)

            for t, n0, _, w in token_parts():
                if t == 2:
                    a_s = mod[:, 8:16, 1:NC_].unsqueeze(3).broadcast_to([P, KD, NB, TS])
                    sh_s = mod[:, 0:8, 1:NC_].unsqueeze(3).broadcast_to([P, KD, NB, TS])
                    r_s = rstd[:, TP:T].rearrange("p (b t) -> p b t", b=NB).unsqueeze(1).broadcast_to([P, KD, NB, TS])
                    x_s = xT[:, :, TP:T].rearrange("p k (b t) -> p k b t", b=NB)
                    h4 = hs.rearrange("p k (b t) -> p k b t", b=NB)
                    nc.vector.tensor_tensor(h4, x_s, r_s, ALU.mult).then_inc(hs_ready, 1)
                    dve.wait_ge(hs_ready, 3 * r + 1)
                    nc.vector.tensor_tensor(h4, h4, a_s, ALU.mult).then_inc(hs_ready, 1)
                    dve.wait_ge(hs_ready, 3 * r + 2)
                    nc.vector.tensor_tensor(h4, h4, sh_s, ALU.add).then_inc(hs_ready, 1)
                for k in range(KD):
                    if i - 24 * r >= 3:
                        dve.wait_ge(h_ready, 25 * r + (i - 24 * r) - 2)
                    nc.vector.scalar_tensor_tensor(
                        out=ht[i % 3][:, 0:w], in0=xT[:, k, n0:n0 + w], scalar=mod[:, 8 + k, 0:1],
                        in1=rstd[:, n0:n0 + w], op0=ALU.mult, op1=ALU.mult).then_inc(ht_ready, 1)
                    if i - 24 * r >= 1:
                        low(i - 1)
                    i += 1
            low(i - 1)
            dve.wait_ge(hshi_ready, r + 1)
            nc.vector.tensor_tensor(h_lo[:, :, TP:T], hs, h_hi[:, :, TP:T].bitcast(f32),
                                    ALU.subtract).then_inc(h_ready, 1)

        def h_scalar(act, r, mod):
            i = 24 * r
            for t, n0, _, w in token_parts():
                for k in range(KD):
                    act.wait_ge(ht_ready, i + 1)
                    nc.scalar.activation(h_hi[:, k, n0:n0 + w], ht[i % 3][:, 0:w], ACT.Identity,
                                         bias=mod[:, k, 0:1]).then_inc(hhi_ready, 1)
                    i += 1
            act.wait_ge(hs_ready, 3 * r + 3)
            nc.scalar.activation(h_hi[:, :, TP:T], hs, ACT.Copy).then_inc(hshi_ready, 1)

        def mod_finish(dve, r, mod):
            g_b = vecT[:, V_NG + 8 * r:V_NG + 8 * r + 8].unsqueeze(2).broadcast_to([P, KD, NC_])
            nc.vector.scalar_tensor_tensor(out=mod[:, 8:16, :], in0=mod[:, 8:16, :], scalar=1.0, in1=g_b,
                                           op0=ALU.add, op1=ALU.mult).then_inc(mod_ready, 1)

        def h_wait(pe, r):
            pe.wait_ge(h_ready, 25 * r + 25)

        def product(pe, p, u, kt, weight, act_hi, act_lo, before_k=None):
            for k in range(kt):
                if before_k:
                    before_k(k)
                for pas, (w, a) in enumerate(((w_hi, act_hi), (w_hi, act_lo), (w_lo, act_hi))):
                    for t, (n0, width) in enumerate(NT):
                        last = nc.tensor.matmul(ps[u][:, t, 0:width], weight(w[:, p, :], k), a[:, k, n0:n0 + width],
                                                start=(k == 0 and pas == 0), stop=(k == kt - 1 and pas == 2))
            return last

        def w8(w, k):
            return w[:, k * P:(k + 1) * P]

        def w4(half):
            return lambda w, k: w[:, k * 256 + half * P:k * 256 + half * P + P]

        def slot_ready(pe, lay, plan, g, name):
            pe.wait_ge(lay.lo_done, g * plan.slots + plan.slot[name] + 3)

        def set_ready(pe, lay, plan, g, u):
            pe.wait_ge(lay.evac[u % 2], g * (plan.units // 2) + u // 2 + 1)

        def project(pe, lay, plan, g, name):
            u = plan.unit[name]
            set_ready(pe, lay, plan, g, u)
            slot_ready(pe, lay, plan, g, name)
            product(pe, plan.slot[name] % 2, u % 2, KD, w8, h_hi, h_lo).then_inc(lay.unit_done, 1)

        def project_inner(pe, lay, plan, g, name, ready):
            for half in range(2):
                u = plan.unit[name] + half
                set_ready(pe, lay, plan, g, u)
                if half == 0:
                    slot_ready(pe, lay, plan, g, name)
                product(pe, plan.slot[name] % 2, u % 2, KG, w4(half), a_hi, a_lo,
                        before_k=lambda k: pe.wait_ge(ready, g * KG + k + 1)).then_inc(lay.unit_done, 1)

        def add_branch(dve, lay, plan, g, name, mod, chain):
            for half in range(2):
                m = 2 * int(name[1]) // 2 + half
                u = plan.unit[name] + half
                src = ps[u % 2]
                dve.wait_ge(lay.unit_done, units(plan, g, u + 1))
                nc.vector.tensor_tensor(gs_tmp[:].rearrange("p (b t) -> p b t", b=NB),
                                        src[:, 2, N2P:N2P + NS].rearrange("p (b t) -> p b t", b=NB),
                                        mod[:, 16 + m, 1:NC_].unsqueeze(2).broadcast_to([P, NB, TS]),
                                        ALU.mult).then_inc(chain_v, 1)
                chain[0] += 1
                for t, n0, _, w in token_parts():
                    last = nc.vector.scalar_tensor_tensor(
                        out=xT[:, m, n0:n0 + w], in0=src[:, t, 0:w], scalar=mod[:, 16 + m, 0:1],
                        in1=xT[:, m, n0:n0 + w], op0=ALU.mult, op1=ALU.add)
                last.then_inc(lay.evac[u % 2], 1)
                dve.wait_ge(chain_v, chain[0])
                nc.vector.tensor_tensor(xT[:, m, TP:T], xT[:, m, TP:T], gs_tmp[:], ALU.add).then_inc(chain_v, 1)
                chain[0] += 1
                dve.wait_ge(chain_v, chain[0])

        def gate_tile(dve, lay, plan, g, i, chain, first_dep=None):
            u = plan.unit[f"Z{i}"]
            dve.wait_ge(lay.evac[u % 2], evacs(plan, g, u))
            nc.vector.tensor_tensor(oT[:, i, :], oT[:, i, :], SZ[:], ALU.mult).then_inc(chain_v, 1)
            chain[0] += 1
            dve.wait_ge(chain_v, chain[0])
            nc.vector.tensor_copy(a_hi[:, i, :], oT[:, i, :]).then_inc(chain_v, 1)
            chain[0] += 1
            dve.wait_ge(chain_v, chain[0])
            nc.vector.tensor_tensor(a_lo[:, i, :], oT[:, i, :], a_hi[:, i, :].bitcast(f32),
                                    ALU.subtract).then_inc(lay.act_ready, 1)
            dve.wait_ge(lay.act_ready, g * KG + i + 1)

        def silu_out(act, lay, plan, g, i):
            u = plan.unit[f"Z{i}"]
            act.wait_ge(lay.unit_done, units(plan, g, u + 1))
            if i:
                act.wait_ge(lay.act_ready, g * KG + i)
            for t, (n0, w) in enumerate(NT):
                last = nc.scalar.activation(SZ[:, n0:n0 + w], ps[u % 2][:, t, 0:w], ACT.Silu)
            last.then_inc(lay.evac[u % 2], 1)

        w_in0 = pool_w_in[0].rearrange("(k p) n -> p k n", p=P)
        w_in1 = gla_w_in[0].rearrange("(k p) n -> p k n", p=P)
        w_out0 = pool_w_out[0].rearrange("(q p) n -> p q n", p=P)
        w_out1 = gla_w_out[0].rearrange("(q p) n -> p q n", p=P)
        w_grp = pool_w_grp[0].rearrange("g (k p) n -> p (g k) n", p=P)
        ada_v = [ada_w[i].rearrange("(k p) n -> p k n", p=P) for i in range(2)]
        hist_v = state_pool[0].rearrange("b r n -> (b r) n")
        o_sem = sem("out_stored")

        block = ctx.enter_context(nc.Block())

        @block.sync
        def _(sp):
            sp.dma_start(c_rows[0:1, :], c_prompt).then_inc(c_loaded, 16)
            sp.dma_start(c_rows[1:NC_, :], c_sample).then_inc(c_loaded, 16)
            for lo, src in ((V_ADAB, ada_b.rearrange("l (m p) -> (l m) p", p=P)),
                            (V_NG, norm_g.rearrange("l (m p) -> (l m) p", p=P)),
                            (V_PS, pool_scale[0].rearrange("(m p) -> m p", p=P)),
                            (V_BG, gla_b_gate[0].rearrange("(m p) -> m p", p=P)),
                            (V_GN, gla_norm_g[0].rearrange("(m p) -> m p", p=P)),
                            (V_FG, final_g.rearrange("(m p) -> m p", p=P))):
                sp.dma_start(vec_rows[lo:lo + src.shape[0], :], src).then_inc(vec_loaded, 16)
            for q in range(6):
                sp.dma_start(ada0[:, q, :, :], ada_v[0][:, :, q * 512:(q + 1) * 512]).then_inc(ada0_loaded[q], 16)
            sp.dma_start(new_pool_sample[0, :, 0:BUF - TS, :], state_pool[0, :, TS:BUF, :]).then_inc(copied, 16)

            with sp.Fori(0, NG) as g:
                def load(j):
                    slot_free(L0, PP, g, j, sp)
                    name = PP.names[j]
                    i = int(name[1])
                    dst = stage[:, j % 2, :]
                    if name[0] in "UZ":
                        src = w_in0[:, :, ds(g * GW + (DI if name[0] == "Z" else 0) + i * P, P)]
                        dst = dst.rearrange("p (k n) -> p k n", k=KD)
                    else:
                        src = (w_grp if name[0] == "G" else w_out0)[:, ds(g * KG, KG), i * P:(i + 2) * P]
                        dst = dst.rearrange("p (k n) -> p k n", k=KG)
                    sp.dma_start(dst, src).then_inc(L0.w_loaded[j % 2], 16)

                def load_ada(a, minis):
                    wait_apart(sp, mini_done, g * 10 + minis + 1)
                    sp.dma_start(ada_stage[:], ada_v[1][:, :, ds(g * 6 * P + a * P, P)]).then_inc(ada_loaded, 16)

                def load_hist(i):
                    wait_apart(sp, hist_T, g * KG + i + 1)
                    sp.dma_start(hist[:, i % 2, :], hist_v[:, ds(g * GW + i * P, P)]).then_inc(hist_loaded[i % 2], 16)

                load_ada(0, 0)
                load_hist(0)
                load_hist(1)
                for j in range(PP.slots):
                    load(j)
                    if j in (2, 3):
                        load_hist(j)
                    if j == 3:
                        load_ada(1, 1)
                    if 8 <= j <= 11:
                        load_ada(j - 6, j - 2)

            sp.wait_ge(sq_ready, 25)
            sp.dma_start(w_gl[:], w_in1[:, :, 2 * 512 + 2 * DI:2 * 512 + 2 * DI + RANK]).then_inc(wgl_loaded, 16)
            for i in range(4):
                sp.sem_inc(s0_stored[i], 16)
            sp.sem_inc(S_stored, 16)
            with sp.Fori(0, NG) as g:
                wait_apart(sp, lg_ready, g + 1)
                sp.dma_start(w_up[:], gla_w_gate_up[0][:, ds(g * P, P)]).then_inc(wup_loaded, 16)
                def states():
                    def load_state(b):
                        wait_apart(sp, s0_stored[b % 4], g * 32 + (b // 4) * 16 + 16)
                        sp.dma_start(S0[b % 4], state_gla[0, b, ds(g, 1), :, :].rearrange("a p n -> p (a n)"))\
                            .then_inc(s0_loaded[b % 4], 16)

                    sp.wait_ge(L1.unit_done, units(GP, g, GP.unit["VT3"] + 1))
                    for b in range(4):
                        load_state(b)
                    wait_apart(sp, S_ready, (g + 1) * NSUP)
                    sp.dma_start(new_gla_prompt[0, 0, ds(g, 1), :, :].rearrange("a p n -> p (a n)"), S[:])\
                        .then_inc(S_stored, 16)
                    for b in range(NB):
                        wait_apart(sp, s0_ready, g * NB + b + 1)
                        sp.dma_start(new_gla_sample[0, b, ds(g, 1), :, :].rearrange("a p n -> p (a n)"), S0[b % 4])\
                            .then_inc(s0_stored[b % 4], 16)
                        if 1 <= b <= 4:
                            load_state(b + 3)

                for j in range(GP.slots):
                    slot_free(L1, GP, g, j, sp)
                    name = GP.names[j]
                    dst = stage[:, j % 2, :]
                    if name[0] == "O":
                        i = int(name[1])
                        src = w_out1[:, ds(g * KG, KG), i * P:(i + 2) * P]
                        dst = dst.rearrange("p (k n) -> p k n", k=KG)
                    else:
                        col = {"Q": g * P, "K": g * P + 512}.get(name)
                        if col is None:
                            col = g * GW + 1024 + (DI if name[0] == "Z" else 0) + int(name[1]) * P
                        src = w_in1[:, :, ds(col, P)]
                        dst = dst.rearrange("p (k n) -> p k n", k=KD)
                    sp.dma_start(dst, src).then_inc(L1.w_loaded[j % 2], 16)
                    if j == GP.slot["Z3"]:
                        states()

            for i in range(4):
                sp.wait_ge(s0_stored[i], 16 * (1 + 2 * NG))
            sp.wait_ge(S_stored, 16 * (1 + NG))

            for s in range(NSUP + 1):
                n = P if s < NSUP else NS
                sp.wait_ge(y_evac[s % 2], s // 2 + 1)
                dst = y_prompt[0, s * P:(s + 1) * P, :] if s < NSUP else y_sample.rearrange("b t n -> (b t) n")
                sp.dma_start(dst, y_rows[0:n, s % 4, :]).then_inc(y_stored[s % 4], 16)
            for i in range(4):
                sp.wait_ge(y_stored[i], 16 * (3 if i == 0 else 2))
            sp.wait_ge(copied, 16)

        @block.gpsimd
        def _(pool):
            n = 0

            def link(ins):
                nonlocal n
                n += 1
                ins.then_inc(chain_p, 1)
                pool.wait_ge(chain_p, n)

            link(pool.memset(ident[:], 0.0))
            link(pool.affine_select(out=ident[:], in_=ident[:], compare_op=ALU.not_equal, fill=1.0, base=0,
                                    pattern=[[-1, P]], channel_multiplier=1))
            link(pool.memset(ones[:], 1.0))
            link(pool.memset(causal[:], 1))
            link(pool.affine_select(out=causal[:], in_=causal[:], compare_op=ALU.is_ge, fill=0, base=0,
                                    pattern=[[1, P]], channel_multiplier=-1))
            link(pool.memset(seq_rows[:], 1.0))
            link(pool.affine_select(out=seq_rows[:], in_=seq_rows[:], compare_op=ALU.is_ge, fill=0.0, base=0,
                                    pattern=[[-TS, NB]], channel_multiplier=1))
            link(pool.affine_select(out=seq_rows[:], in_=seq_rows[:], compare_op=ALU.is_ge, fill=0.0, base=TS - 1,
                                    pattern=[[TS, NB]], channel_multiplier=-1))
            cs3 = causal_s[:].rearrange("p (b t) -> p b t", b=NB)
            link(pool.memset(causal_s[:], 1))
            link(pool.affine_select(out=cs3, in_=cs3, compare_op=ALU.is_ge, fill=0, base=0,
                                    pattern=[[-TS, NB], [0, TS]], channel_multiplier=1))
            link(pool.affine_select(out=cs3, in_=cs3, compare_op=ALU.is_ge, fill=0, base=0,
                                    pattern=[[TS, NB], [1, TS]], channel_multiplier=-1))
            link(pool.memset(win_on[:], 0.0))
            for k in range(3):
                link(pool.memset(win_on[:, k + 1:NG, k:k + 1], 1.0))
            for g in range(NG):
                w = 2 << g
                link(pool.memset(win_inv[:, g:g + 1], 1.0 / w))
                link(pool.memset(cnt_inv[:, g, :], 1.0 / w))
                for t in range(w - 1):
                    link(pool.memset(cnt_inv[:, g, t:t + 1], 1.0 / (t + 1)))
            link(pool.memset(eps[:], EPS))
            pool.memset(gs_tmp[:], 0.0).then_inc(consts_ready, 1)

            pool.sem_inc(L0.lo_done, 2)
            with pool.Fori(0, NG) as g:
                for j in range(PP.slots):
                    lo_slots(L0, PP, pool, g, j)

            pool.wait_ge(wgl_hi, 1)
            pool.tensor_tensor(w_gl_lo[:], w_gl[:], w_gl_hi[:].bitcast(f32), ALU.subtract).then_inc(wgl_lo, 1)
            pool.sem_inc(L1.lo_done, 2)
            with pool.Fori(0, NG) as g:
                for j in range(GP.slot["Z2"] + 1):
                    lo_slots(L1, GP, pool, g, j)
                wait_apart(pool, L1.unit_done, units(GP, g, GP.unit["VT3"] + 1))
                pool.memset(Kp[:], 0.0).then_inc(kp_zero, 1)

                for s in range(NSUP):
                    pool.wait_ge(kp_exp, g * NSUP + s + 1)
                    for b in range(4):
                        last = pool.tensor_tensor(Kp[:, b, 0:CH * (b + 1)], Kp[:, b, 0:CH * (b + 1)],
                                                  kT[:, s * SUP:s * SUP + CH * (b + 1)], ALU.mult)
                    last.then_inc(kp_ready, 1)
                for j in range(GP.slot["Z3"], GP.slots):
                    lo_slots(L1, GP, pool, g, j)

        @block.scalar
        def _(act):
            def load_x(s):
                if s >= 4:
                    act.wait_ge(xT_done, s - 3)
                n = P if s < NSUP else NS
                src = x_prompt[0, s * P:(s + 1) * P, :] if s < NSUP else x_sample.rearrange("b t n -> (b t) n")
                act.dma_start(xrow[s % 4][0:n, :], src).then_inc(x_loaded[s % 4], 16)

            for s in range(4):
                load_x(s)
            act.wait_ge(cT_done, 1)
            nc.scalar.activation(csT[:].rearrange("p k c -> p (k c)"), X[0][:, 0:KD * NC_], ACT.Silu).then_inc(cs_ready, 1)
            act.wait_ge(vT_done, 1)
            nc.scalar.activation(vecT[:], X[1][:, 0:NVEC], ACT.Copy).then_inc(vec_ready, 1)
            for s in range(NSUP + 1):
                n = P if s < NSUP else NS
                if s >= 1 and s + 3 <= NSUP:
                    load_x(s + 3)
                act.wait_ge(xT_done, s + 1)
                nc.scalar.activation(xT[:, :, s * P:s * P + n],
                                     ps[s % 2][:, 0:2, :].rearrange("p a (k t) -> p (a k) t", k=4)[:, :, 0:n],
                                     ACT.Copy).then_inc(xT_ready, 1)
            norm_squares(act, 0, (xT_ready, NSUP + 1))
            act.wait_ge(mod_ready, 1)
            h_scalar(act, 0, mods[0])
            act.sem_inc(mini_free, 1)
            act.sem_inc(hist_evac, 1)
            act.sem_inc(tail_stored[0], 32)
            act.sem_inc(tail_stored[1], 32)

            with act.Fori(0, NG) as g:
                def u_out(i):
                    u = PP.unit[f"U{i}"]
                    act.wait_ge(L0.unit_done, units(PP, g, u + 1))
                    act.wait_ge(pooled, g * KG + i + 1)
                    act.wait_ge(hist_T, g * KG + i + 3)
                    seg = G[:, SE0:SE0 + NB * SEG].rearrange("p (b r) -> p b r", b=NB)
                    nc.scalar.activation(seg[:, :, 0:BUF], X[0][:, 0:NB * BUF].rearrange("p (b r) -> p b r", b=NB),
                                         ACT.Copy).then_inc(hist_evac, 1)
                    for t, n0, _, w in token_parts():
                        nc.scalar.activation(G[:, BUF + n0:BUF + n0 + w], ps[u % 2][:, t, 0:w], ACT.Copy)
                    smp = ps[u % 2][:, 2, N2P:N2P + NS]
                    nc.scalar.activation(seg[:, :, BUF:SEG], smp.rearrange("p (b t) -> p b t", b=NB), ACT.Copy)
                    act.wait_ge(mini_done, g * 10 + (1 + i) + 1)
                    nc.scalar.activation(tail[:, 0:NS], smp, ACT.Copy)
                    nc.scalar.activation(tail[:, NS:NS + BUF], ps[u % 2][:, 2, N2P - BUF:N2P], ACT.Copy)\
                        .then_inc(L0.evac[u % 2], 1)

                def ada_out(a, mini):
                    act.wait_ge(mini_done, g * 10 + mini + 2)
                    nc.scalar.activation(mods[1][:].rearrange("p m c -> p (m c)")[:, ds(g * 6 * NC_ + a * NC_, NC_)],
                                         X[1][:, 0:NC_], ACT.Identity,
                                         bias=vecT[:, ds(g * 6 + (V_ADAB + 24 + a), 1)]).then_inc(mini_free, 1)

                def tail_store(i):
                    act.wait_ge(mini_done, g * 10 + (1 + i) + 2)
                    act.wait_ge(tail_stored[i % 2], g * 64 + (i // 2) * 32 + 32)
                    nc.scalar.activation(tail_out[:, i % 2, :], X[1][0:NS + BUF, 0:P], ACT.Copy).then_inc(mini_free, 1)
                    act.wait_ge(mini_free, g * 10 + (1 + i) + 2)
                    act.dma_start(new_pool_sample[0, :, BUF - TS:BUF, ds(g * GW + i * P, P)],
                                  tail_out[0:NS, i % 2, :]).then_inc(tail_stored[i % 2], 16)
                    act.dma_start(new_pool_prompt[0, 0, :, ds(g * GW + i * P, P)],
                                  tail_out[NS:NS + BUF, i % 2, :]).then_inc(tail_stored[i % 2], 16)

                split_slot(L0, PP, act, g, 0)
                split_slot(L0, PP, act, g, 1)
                extra = {0: lambda: ada_out(0, 0), 1: lambda: tail_store(0), 2: lambda: tail_store(1),
                         3: lambda: tail_store(2), 4: lambda: tail_store(3), 5: lambda: ada_out(1, 5),
                         6: lambda: ada_out(2, 6), 7: lambda: ada_out(3, 7), 8: lambda: ada_out(4, 8),
                         9: lambda: ada_out(5, 9)}
                for j, name in enumerate(PP.names):
                    if name[0] == "U":
                        u_out(int(name[1]))
                    if name[0] == "Z":
                        silu_out(act, L0, PP, g, int(name[1]))
                    if j + 2 < PP.slots:
                        split_slot(L0, PP, act, g, j + 2)
                    if j in extra:
                        extra[j]()
            for i in range(2):
                act.wait_ge(tail_stored[i], 32 + 64 * NG)

            norm_squares(act, 1, (x_final, 1))
            act.wait_ge(mod_ready, 2)
            h_scalar(act, 1, mods[1])
            act.wait_ge(wgl_loaded, 16)
            nc.scalar.activation(w_gl_hi[:], w_gl[:], ACT.Copy).then_inc(wgl_hi, 1)
            for t, (n0, w) in enumerate(NT):
                act.wait_ge(gl_done, 1)
                last = nc.scalar.activation(glT[:, n0:n0 + w], ps[0][0:RANK, t, 0:w], ACT.Copy)
            last.then_inc(gl_ready, 1)

            with act.Fori(0, NG) as g:
                def copy_out(name, dst, scale=1.0, wait=None):
                    u = GP.unit[name]
                    act.wait_ge(L1.unit_done, units(GP, g, u + 1))
                    if wait:
                        wait()
                    for t, (n0, w) in enumerate(NT):
                        last = nc.scalar.activation(dst[:, n0:n0 + w], ps[u % 2][:, t, 0:w], ACT.Copy, scale=scale)
                    last.then_inc(L1.evac[u % 2], 1)

                split_slot(L1, GP, act, g, 0)
                split_slot(L1, GP, act, g, 1)
                copy_out("Q", qT[:], scale=float(P) ** -0.5)
                split_slot(L1, GP, act, g, 2)
                copy_out("K", kT[:])
                split_slot(L1, GP, act, g, 3)
                u = GP.unit["LG"]
                act.wait_ge(L1.unit_done, units(GP, g, u + 1))
                for t, (n0, w) in enumerate(NT):
                    last = nc.scalar.activation(L[:, n0:n0 + w], ps[u % 2][:, t, 0:w], ACT.Identity,
                                                bias=vecT[:, ds(g + V_BG, 1)])
                last.then_inc(L1.evac[u % 2], 1)
                act.wait_ge(L1.evac[u % 2], evacs(GP, g, u))
                nc.scalar.activation(SZ[:], L[:], ACT.Abs).then_inc(chain_a, 1)
                act.wait_ge(chain_a, 1)
                nc.scalar.activation(SZ[:], SZ[:], ACT.Exp, scale=-1.0).then_inc(chain_a, 1)
                act.wait_ge(chain_a, 2)
                nc.scalar.activation(SZ[:], SZ[:], ACT.Ln, bias=1.0).then_inc(sp_ready, 1)
                copy_out("V0", vT[0])
                split_slot(L1, GP, act, g, 4)
                copy_out("V1", vT[1])
                split_slot(L1, GP, act, g, 5)
                copy_out("V2", vT[0])
                split_slot(L1, GP, act, g, 6)
                copy_out("V3", vT[1])
                split_slot(L1, GP, act, g, 7)
                act.wait_ge(lg_ready, g + 2)
                silu_out(act, L1, GP, g, 0)
                split_slot(L1, GP, act, g, 8)

                nc.scalar.activation(dec[:, 0:NSUP], L[:, SUP - 1:TP:SUP], ACT.Exp)
                nc.scalar.activation(dec[:, NSUP:NSUP + NB], L[:, TP + TS - 1:T:TS], ACT.Exp).then_inc(dec_ready, 1)
                act.wait_ge(kp_zero, g + 1)

                def exps(s):
                    c0 = s * SUP
                    if s >= 1:
                        act.wait_ge(att_done, g * NSUP + s)
                    for b in range(4):
                        kw = {} if b == 0 else {"bias": L[:, c0 + CH * b - 1:c0 + CH * b]}
                        last = nc.scalar.activation(Kp[:, b, 0:CH * (b + 1)], L[:, c0:c0 + CH * (b + 1)], ACT.Exp,
                                                    scale=-1.0, **kw)
                    last.then_inc(kp_exp, 1)
                    act.wait_ge(qd_arg, g * NSUP + s + 1)
                    nc.scalar.activation(qd[:], qd[:], ACT.Exp).then_inc(qd_exp, 1)
                    if s >= 1:
                        act.wait_ge(kT_done, g * NSUP + s)
                    nc.scalar.activation(ks[:], L[:, c0:c0 + SUP], ACT.Exp, scale=-1.0,
                                         bias=L[:, c0 + SUP - 1:c0 + SUP]).then_inc(ks_exp, 1)

                def exp_qs(s):
                    if s >= 1:
                        act.wait_ge(o_done, g * (NSUP + 1) + s)
                    nc.scalar.activation(qs[:], L[:, s * SUP:(s + 1) * SUP], ACT.Exp).then_inc(qs_exp, 1)

                def ksT_out(s):
                    act.wait_ge(kT_done, g * NSUP + s + 1)
                    if s >= 2:
                        act.wait_ge(upd_done, g * NSUP + s - 1)
                    nc.scalar.activation(ksT[:, s % 2, :], ps[0][:, 2, 0:P], ACT.Copy).then_inc(ksT_ready, 1)

                def o_out(s):
                    act.wait_ge(o_done, g * (NSUP + 1) + s + 1)
                    nc.scalar.activation(oT[:, :, s * SUP:(s + 1) * SUP],
                                         ps[0][:, s % 2, :].rearrange("p (e t) -> p e t", e=KG),
                                         ACT.Copy).then_inc(o_evac, 1)

                exps(0)
                exp_qs(0)
                ksT_out(0)
                for s in range(NSUP):
                    if s + 1 < NSUP:
                        exps(s + 1)
                        ksT_out(s + 1)
                    o_out(s)
                    if s + 1 < NSUP:
                        exp_qs(s + 1)
                nc.scalar.activation(qd[:, 0:NS], L[:, TP:T], ACT.Exp)
                nc.scalar.activation(qs[:, 0:NS], L[:, TP:T], ACT.Exp, scale=-1.0)
                act.wait_ge(smp_arg, g + 1)
                nc.scalar.activation(ks[:, 0:NS], ks[:, 0:NS], ACT.Exp).then_inc(smp_exp, 1)
                act.wait_ge(o_done, (g + 1) * (NSUP + 1))
                nc.scalar.activation(oT[:, :, TP:T], ps[0][:, 0, 0:KG * NS].rearrange("p (e t) -> p e t", e=KG),
                                     ACT.Copy).then_inc(L1.evac[0], 1)
                for i in range(4):
                    act.wait_ge(s0_stored[i], g * 32 + 48)
                act.wait_ge(L1.evac[0], evacs(GP, g, GP.unit["ATT"]))
                for t, (n0, w) in enumerate(NT):
                    if t:
                        act.wait_ge(oacc_ready, g * 3 + t)
                    nc.scalar.activation(sq4[:, :, 0:w], oT[:, :, n0:n0 + w], ACT.Square).then_inc(osq_ready, 1)
                u = GP.unit["NRM"]
                act.wait_ge(L1.unit_done, units(GP, g, u + 1))
                for t, (n0, w) in enumerate(NT):
                    last = nc.scalar.activation(acc[:, n0:n0 + w], ps[u % 2][:, t, 0:w], ACT.Sqrt, bias=eps[:, 0:1],
                                                scale=1.0 / GW)
                last.then_inc(L1.evac[u % 2], 1)
                split_slot(L1, GP, act, g, 9)
                silu_out(act, L1, GP, g, 1)
                silu_out(act, L1, GP, g, 2)
                split_slot(L1, GP, act, g, 10)
                silu_out(act, L1, GP, g, 3)
                for j in range(11, 14):
                    split_slot(L1, GP, act, g, j)
                act.sem_clear(chain_a)

            norm_squares(act, 2, (x_final, 2))
            for s in range(0, NSUP + 1, 2):
                n = P if s < NSUP else NS
                act.wait_ge(yT_done, s + 1)
                if s >= 4:
                    act.wait_ge(y_stored[s % 4], 16 * (s // 4))
                nc.scalar.activation(y_rows[0:n, s % 4, :], ps[s % 2][0:n, 0:2, :].rearrange("p a n -> p (a n)"),
                                     ACT.Copy).then_inc(y_evac[0], 1)

        @block.vector
        def _(dve):
            chain = [0]

            def link(ins):
                chain[0] += 1
                ins.then_inc(chain_v, 1)
                dve.wait_ge(chain_v, chain[0])

            def chain_restart():
                dve.wait_ge(chain_v, chain[0])
                dve.sem_clear(chain_v)
                chain[0] = 0

            dve.wait_ge(consts_ready, 1)
            dve.wait_ge(vec_ready, 1)
            for part, (m0, m1) in enumerate(((0, 16), (16, 24))):
                dve.wait_ge(mod_done, part + 1)
                bias = vecT[:, V_ADAB + m0:V_ADAB + m1].unsqueeze(2).broadcast_to([P, m1 - m0, NC_])
                link(nc.vector.tensor_tensor(mods[0][:, m0:m1, :],
                                             X[part][:, 0:(m1 - m0) * NC_].rearrange("p (m c) -> p m c", c=NC_),
                                             bias, ALU.add))
            mod_finish(dve, 0, mods[0])
            dve.wait_ge(mod_ready, 1)
            h_vector(dve, 0, mods[0])
            dve.wait_ge(h_ready, 25)
            link(nc.vector.memset(G[:, 0:BUF], 0.0))
            chain_restart()
            dve.sem_inc(pooled, 1)

            with dve.Fori(0, NG) as g:
                chain[0] = 0

                def pool_tile(i):
                    u = PP.unit[f"U{i}"]
                    dve.wait_ge(L0.evac[u % 2], evacs(PP, g, u))
                    link(nc.vector.tensor_tensor(s1[:, 1:WE], G[:, 1:WE], G[:, 0:WE - 1], ALU.add))
                    src, dst, have = s1, s2, 1
                    for k in range(3):
                        sh = 2 << k
                        lo = have + sh
                        link(nc.vector.scalar_tensor_tensor(
                            out=dst[:, lo:WE], in0=src[:, lo - sh:WE - sh],
                            scalar=win_on[:].rearrange("p g k -> p (g k)")[:, ds(g * 3 + k, 1)],
                            in1=src[:, lo:WE], op0=ALU.mult, op1=ALU.add))
                        src, dst, have = dst, src, lo
                    diff = s1[:, 0:T]
                    inv = win_inv[:, ds(g, 1)]
                    nc.vector.scalar_tensor_tensor(out=diff[:, 0:TP], in0=src[:, BUF:BUF + TP], scalar=inv,
                                                   in1=G[:, BUF:BUF + TP], op0=ALU.mult, op1=ALU.subtract)
                    seg = src[:, SE0:SE0 + NB * SEG].rearrange("p (b r) -> p b r", b=NB)[:, :, BUF:SEG]
                    useg = G[:, SE0:SE0 + NB * SEG].rearrange("p (b r) -> p b r", b=NB)[:, :, BUF:SEG]
                    link(nc.vector.scalar_tensor_tensor(out=diff[:, TP:T].rearrange("p (b t) -> p b t", b=NB), in0=seg,
                                                        scalar=inv, in1=useg, op0=ALU.mult, op1=ALU.subtract))
                    link(nc.vector.tensor_tensor(diff[:, 0:16], src[:, BUF:BUF + 16],
                                                 cnt_inv[:].rearrange("p g t -> p (g t)")[:, ds(g * 16, 16)], ALU.mult))
                    nc.vector.tensor_tensor(diff[:, 0:16], diff[:, 0:16], G[:, BUF:BUF + 16],
                                            ALU.subtract).then_inc(pooled, 1)
                    dve.wait_ge(pooled, g * KG + i + 2)
                    link(nc.vector.tensor_copy(a_hi[:, i, :], diff))
                    nc.vector.tensor_tensor(a_lo[:, i, :], diff, a_hi[:, i, :].bitcast(f32),
                                            ALU.subtract).then_inc(diff_ready, 1)
                    dve.wait_ge(diff_ready, g * KG + i + 1)

                for i in range(KG):
                    pool_tile(i)
                for m in range(KG):
                    u = PP.unit["G01"] + m
                    dve.wait_ge(L0.unit_done, units(PP, g, u + 1))
                    for t, (n0, w) in enumerate(NT):
                        last = nc.vector.tensor_scalar(oT[:, m, n0:n0 + w], ps[u % 2][:, t, 0:w],
                                                       vecT[:, ds(g * KG + (V_PS + m), 1)], None, ALU.mult)
                    last.then_inc(L0.evac[u % 2], 1)
                for i in range(KG):
                    if i == 0:
                        dve.wait_ge(L0.evac[(PP.unit["G23"] + 1) % 2], evacs(PP, g, PP.unit["G23"] + 1))
                    gate_tile(dve, L0, PP, g, i, chain)
                for name in ("O01", "O23", "O45", "O67"):
                    add_branch(dve, L0, PP, g, name, mods[0], chain)
                chain_restart()

            dve.wait_ge(mini_free, 1 + 10 * NG)
            mod_finish(dve, 1, mods[1])
            dve.wait_ge(mod_ready, 2)
            link(nc.vector.memset(gs_tmp[:], 0.0))
            nc.vector.memset(gs_tmp[:], 0.0).then_inc(x_final, 1)
            h_vector(dve, 1, mods[1])
            dve.sem_inc(lg_ready, 1)
            link(nc.vector.memset(att_s[:], 0.0))
            link(nc.vector.memset(att[:], 0.0))
            chain_restart()

            with dve.Fori(0, NG) as g:
                chain[0] = 0
                dve.wait_ge(sp_ready, g + 1)
                link(nc.vector.scalar_tensor_tensor(out=L[:], in0=L[:], scalar=0.0, in1=SZ[:], op0=ALU.min,
                                                    op1=ALU.subtract))
                link(nc.vector.tensor_scalar(L[:], L[:], 1.0 / 16.0, None, ALU.mult))
                for s in range(NSUP):
                    c = slice(s * SUP, (s + 1) * SUP)
                    nc.vector.tensor_tensor_scan(L[:, c], ones[:, 0:SUP], L[:, c], 0.0, ALU.mult, ALU.add)
                for b in range(NB):
                    c = slice(TP + b * TS, TP + (b + 1) * TS)
                    last = nc.vector.tensor_tensor_scan(L[:, c], ones[:, 0:TS], L[:, c], 0.0, ALU.mult, ALU.add)
                last.then_inc(lg_ready, 1)
                for i in range(KG):
                    u = GP.unit[f"VT{i}"]
                    dve.wait_ge(L1.unit_done, units(GP, g, u + 1))
                    for half in range(2):
                        nc.vector.tensor_copy(v[:, 4 * half:4 * half + 4, i * P:(i + 1) * P],
                                              ps[u % 2][:, half, :].rearrange("p (s n) -> p s n", s=4))
                    nc.vector.tensor_copy(v[0:NS, NSUP, i * P:(i + 1) * P], ps[u % 2][0:NS, 2, 0:P])\
                        .then_inc(L1.evac[u % 2], 1)
                dve.wait_ge(lg_ready, g + 2)

                def qd_args(s):
                    c0 = s * SUP
                    if s >= 1:
                        dve.wait_ge(att_done, g * NSUP + s)
                    nc.vector.tensor_copy(qd[:, 0:CH], L[:, c0:c0 + CH])
                    nc.vector.tensor_tensor(qd[:, CH:SUP].rearrange("p (b t) -> p b t", b=3),
                                            L[:, c0 + CH:c0 + SUP].rearrange("p (b t) -> p b t", b=3),
                                            L[:, c0 + CH - 1:c0 + SUP - 1:CH].unsqueeze(2).broadcast_to([P, 3, CH]),
                                            ALU.subtract).then_inc(qd_arg, 1)

                def scale_qk(s):
                    c = slice(s * SUP, (s + 1) * SUP)
                    dve.wait_ge(qd_exp, g * NSUP + s + 1)
                    nc.vector.tensor_tensor(qd[:], qd[:], qT[:, c], ALU.mult).then_inc(qd_ready, 1)
                    dve.wait_ge(ks_exp, g * NSUP + s + 1)
                    nc.vector.tensor_tensor(ks[:], ks[:], kT[:, c], ALU.mult).then_inc(ks_ready, 1)

                def scale_qs(s):
                    dve.wait_ge(qs_exp, g * NSUP + s + 1)
                    nc.vector.tensor_tensor(qs[:], qs[:], qT[:, s * SUP:(s + 1) * SUP], ALU.mult).then_inc(qs_ready, 1)

                def att_out(s):
                    if s >= 2:
                        wait_apart(dve, o_done, g * (NSUP + 1) + s - 1)
                    wait_apart(dve, att_done, g * NSUP + s + 1)
                    nc.vector.copy_predicated(att[:, s % 2, :], causal[:], X[s % 2][:, 0:SUP]).then_inc(att_ready, 1)

                def state(s):
                    if s == 0:
                        dve.wait_ge(S_stored, g * 16 + 16)
                        dve.wait_ge(upd_done, g * NSUP + s + 1)
                        nc.vector.tensor_copy(S[:], ps[1][:, s % 2, :]).then_inc(S_ready, 1)
                    else:
                        dve.wait_ge(upd_done, g * NSUP + s + 1)
                        dve.wait_ge(S_ready, g * NSUP + s)
                        nc.vector.scalar_tensor_tensor(out=S[:], in0=S[:], scalar=dec[:, s:s + 1], in1=ps[1][:, s % 2, :],
                                                       op0=ALU.mult, op1=ALU.add).then_inc(S_ready, 1)

                dve.wait_ge(dec_ready, g + 1)
                qd_args(0)
                scale_qk(0)
                scale_qs(0)
                att_out(0)
                for s in range(NSUP):
                    if s + 1 < NSUP:
                        qd_args(s + 1)
                        scale_qk(s + 1)
                        att_out(s + 1)
                    state(s)
                    if s + 1 < NSUP:
                        scale_qs(s + 1)
                dve.wait_ge(kT_done, (g + 1) * NSUP)
                l_end = L[:, TP + TS - 1:T:TS].unsqueeze(2).broadcast_to([P, NB, TS])
                nc.vector.tensor_tensor(ks[:, 0:NS].rearrange("p (b t) -> p b t", b=NB), l_end,
                                        L[:, TP:T].rearrange("p (b t) -> p b t", b=NB), ALU.subtract).then_inc(smp_arg, 1)
                dve.wait_ge(smp_exp, g + 1)
                nc.vector.tensor_tensor(qd[:, 0:NS], qd[:, 0:NS], qT[:, TP:T], ALU.mult)
                nc.vector.tensor_tensor(qs[:, 0:NS], qs[:, 0:NS], kT[:, TP:T], ALU.mult)
                nc.vector.tensor_tensor(ks[:, 0:NS], ks[:, 0:NS], kT[:, TP:T], ALU.mult).then_inc(smp_ready, 1)
                wait_apart(dve, smp_att, g + 1)
                nc.vector.copy_predicated(att_s[:], causal_s[:], X[0][0:NS, 0:NS]).then_inc(smp_attr, 1)
                dve.wait_ge(smp_kT, g + 1)

                def ks_rows(b):
                    if b >= 2:
                        dve.wait_ge(smp_upd, g * NB + b - 1)
                    nc.vector.tensor_scalar(ksm[:, b % 2, :], ps[0][0:NS, 2, 0:P], seq_rows[:, b:b + 1], None,
                                            ALU.mult).then_inc(ksm_ready, 1)

                ks_rows(0)
                for b in range(NB):
                    if b + 1 < NB:
                        ks_rows(b + 1)
                    dve.wait_ge(smp_upd, g * NB + b + 1)
                    last = nc.vector.scalar_tensor_tensor(
                        out=S0[b % 4], in0=S0[b % 4], scalar=dec[:, NSUP + b:NSUP + b + 1], in1=ps[1][:, b % 2, :],
                        op0=ALU.mult, op1=ALU.add)
                    last.then_inc(s0_ready, 1)
                dve.wait_ge(s0_ready, (g + 1) * NB)
                dve.sem_inc(L1.evac[1], 1)
                for t, (n0, w) in enumerate(NT):
                    dve.wait_ge(osq_ready, g * 3 + t + 1)
                    link(nc.vector.tensor_tensor(sq4[:, 0:2, 0:w], sq4[:, 0:2, 0:w], sq4[:, 2:4, 0:w], ALU.add))
                    nc.vector.tensor_tensor(acc[:, n0:n0 + w], sq4[:, 0, 0:w], sq4[:, 1, 0:w],
                                            ALU.add).then_inc(oacc_ready, 1)
                u = GP.unit["NRM"]
                dve.wait_ge(L1.evac[u % 2], evacs(GP, g, u))
                link(nc.vector.reciprocal(acc, acc))
                for i in range(KG):
                    ins = nc.vector.scalar_tensor_tensor(out=oT[:, i, :], in0=oT[:, i, :],
                                                         scalar=vecT[:, ds(g * KG + (V_GN + i), 1)], in1=acc,
                                                         op0=ALU.mult, op1=ALU.mult)
                link(ins)
                for i in range(KG):
                    gate_tile(dve, L1, GP, g, i, chain)
                for name in ("O01", "O23", "O45", "O67"):
                    add_branch(dve, L1, GP, g, name, mods[1], chain)
                chain_restart()

            nc.vector.memset(gs_tmp[:], 0.0).then_inc(x_final, 1)
            for t, (n0, w) in enumerate(NT):
                dve.wait_ge(std_ready, 6 + t + 1)
                nc.vector.reciprocal(rstd[:, n0:n0 + w], rstd[:, n0:n0 + w]).then_inc(rstd_ready, 1)
                dve.wait_ge(rstd_ready, 6 + t + 1)
                for k in range(KD):
                    last = nc.vector.scalar_tensor_tensor(out=xT[:, k, n0:n0 + w], in0=xT[:, k, n0:n0 + w],
                                                          scalar=vecT[:, V_FG + k:V_FG + k + 1], in1=rstd[:, n0:n0 + w],
                                                          op0=ALU.mult, op1=ALU.mult)
                last.then_inc(y_ready, 1)
            for s in range(1, NSUP, 2):
                dve.wait_ge(yT_done, s + 1)
                if s >= 4:
                    dve.wait_ge(y_stored[s % 4], 16 * (s // 4))
                nc.vector.tensor_copy(y_rows[:, s % 4, :], ps[s % 2][:, 0:2, :].rearrange("p a n -> p (a n)"))\
                    .then_inc(y_evac[1], 1)

        @block.tensor
        def _(pe):
            pe.wait_ge(consts_ready, 1)
            pe.wait_ge(c_loaded, 32)
            for k in range(KD):
                last = nc.tensor.transpose(X[0][:, k * NC_:(k + 1) * NC_], c_rows[:, k * P:(k + 1) * P],
                                           ident[0:NC_, 0:NC_])
            last.then_inc(cT_done, 1)
            pe.wait_ge(vec_loaded, 16 * 6)
            nc.tensor.transpose(X[1][:, 0:NVEC], vec_rows, ident[0:NVEC, 0:NVEC]).then_inc(vT_done, 1)
            for s in range(NSUP + 1):
                n = P if s < NSUP else NS
                pe.wait_ge(x_loaded[s % 4], 16 * (s // 4 + 1))
                if s >= 2:
                    pe.wait_ge(xT_ready, s - 1)
                for k in range(KD):
                    last = nc.tensor.transpose(ps[s % 2][:, k // 4, (k % 4) * P:(k % 4) * P + n],
                                               xrow[s % 4][0:n, k * P:(k + 1) * P], ident[0:n, 0:n])
                last.then_inc(xT_done, 1)
            pe.wait_ge(cs_ready, 1)
            pe.wait_ge(vec_ready, 1)
            pe.wait_ge(xT_ready, NSUP + 1)
            norm_sums(pe, 0)
            for m in range(24):
                if m % 4 == 0:
                    pe.wait_ge(ada0_loaded[m // 4], 16)
                dst = X[0][:, m * NC_:(m + 1) * NC_] if m < 16 else X[1][:, (m - 16) * NC_:(m - 15) * NC_]
                for k in range(KD):
                    last = nc.tensor.matmul(dst, ada0[:, m // 4, k, (m % 4) * P:(m % 4 + 1) * P], csT[:, k, :],
                                            start=(k == 0), stop=(k == KD - 1))
                if m in (15, 23):
                    last.then_inc(mod_done, 1)
            h_wait(pe, 0)
            pe.sem_inc(L0.unit_done, 3)
            pe.sem_inc(mini_done, 1)
            pe.sem_inc(hist_T, 2)

            def start_sets(lay):
                pe.sem_inc(lay.evac[0], 1)
                pe.sem_inc(lay.evac[1], 1)

            start_sets(L0)
            with pe.Fori(0, NG) as g:
                def hist_mini(i):
                    pe.wait_ge(hist_evac, g * KG + i + 1)
                    pe.wait_ge(hist_loaded[i % 2], g * 32 + (i // 2) * 16 + 16)
                    nc.tensor.transpose(X[0][:, 0:NB * BUF], hist[:, i % 2, :], ident[0:NB * BUF, 0:NB * BUF])\
                        .then_inc(hist_T, 1)

                def ada_mini(a, mini):
                    pe.wait_ge(mini_free, g * 10 + mini + 1)
                    pe.wait_ge(ada_loaded, g * 96 + a * 16 + 16)
                    for k in range(KD):
                        last = nc.tensor.matmul(X[1][:, 0:NC_], ada_stage[:, k, :], csT[:, k, :], start=(k == 0),
                                                stop=(k == KD - 1))
                    last.then_inc(mini_done, 1)

                def tail_mini(i):
                    u = PP.unit[f"U{i}"]
                    pe.wait_ge(L0.evac[u % 2], evacs(PP, g, u))
                    pe.wait_ge(mini_free, g * 10 + (1 + i) + 1)
                    nc.tensor.transpose(X[1][0:NS + BUF, 0:P], tail[:], ident[:]).then_inc(mini_done, 1)

                for name in PP.names:
                    if name[0] == "U":
                        hist_mini(int(name[1]))
                    if name[0] in "UZ":
                        project(pe, L0, PP, g, name)
                    elif name[0] == "G":
                        project_inner(pe, L0, PP, g, name, diff_ready)
                    else:
                        project_inner(pe, L0, PP, g, name, L0.act_ready)
                    j = PP.slot[name]
                    if j == 0:
                        ada_mini(0, 0)
                    if 1 <= j <= 4:
                        tail_mini(j - 1)
                    if 5 <= j <= 9:
                        ada_mini(j - 4, j)

            norm_sums(pe, 1)
            h_wait(pe, 1)
            pe.sem_inc(L1.unit_done, 3)
            pe.wait_ge(wgl_lo, 1)
            for k in range(KD):
                for pas, (w, a) in enumerate(((w_gl_hi, h_hi), (w_gl_hi, h_lo), (w_gl_lo, h_hi))):
                    for t, (n0, width) in enumerate(NT):
                        last = nc.tensor.matmul(ps[0][0:RANK, t, 0:width], w[:, k, :], a[:, k, n0:n0 + width],
                                                start=(k == 0 and pas == 0), stop=(k == KD - 1 and pas == 2))
            last.then_inc(gl_done, 1)
            pe.wait_ge(gl_ready, 1)
            start_sets(L1)
            with pe.Fori(0, NG) as g:
                def v_transpose(i):
                    u = GP.unit[f"VT{i}"]
                    src = GP.unit[f"V{i}"]
                    set_ready(pe, L1, GP, g, u)
                    pe.wait_ge(L1.evac[src % 2], evacs(GP, g, src))
                    for s in range(NSUP + 1):
                        n = P if s < NSUP else NS
                        last = nc.tensor.transpose(ps[u % 2][0:n, s // 4, (s % 4) * P:(s % 4 + 1) * P],
                                                   vT[i % 2][:, s * P:s * P + n], ident[:])
                    last.then_inc(L1.unit_done, 1)

                def log_decay():
                    u = GP.unit["LG"]
                    set_ready(pe, L1, GP, g, u)
                    pe.wait_ge(wup_loaded, g * 16 + 16)
                    for t, (n0, width) in enumerate(NT):
                        last = nc.tensor.matmul(ps[u % 2][:, t, 0:width], w_up[:], glT[:, n0:n0 + width],
                                                start=True, stop=True)
                    last.then_inc(L1.unit_done, 1)

                def attend():
                    u = GP.unit["ATT"]
                    set_ready(pe, L1, GP, g, u)
                    set_ready(pe, L1, GP, g, u + 1)

                    def scores(s):
                        pe.wait_ge(kp_ready, g * NSUP + s + 1)
                        pe.wait_ge(qd_ready, g * NSUP + s + 1)
                        if s >= 2:
                            pe.wait_ge(att_ready, g * NSUP + s - 1)
                        for b in range(4):
                            last = nc.tensor.matmul(X[s % 2][:, b * CH:(b + 1) * CH], Kp[:, b, :],
                                                    qd[:, b * CH:(b + 1) * CH], start=True, stop=True)
                        last.then_inc(att_done, 1)

                    def key_rows(s):
                        pe.wait_ge(ks_ready, g * NSUP + s + 1)
                        if s >= 1:
                            pe.wait_ge(ksT_ready, g * NSUP + s)
                        nc.tensor.transpose(ps[0][:, 2, 0:P], ks[:], ident[:]).then_inc(kT_done, 1)

                    scores(0)
                    key_rows(0)
                    for s in range(NSUP):
                        if s + 1 < NSUP:
                            scores(s + 1)
                            key_rows(s + 1)
                        pe.wait_ge(att_ready, g * NSUP + s + 1)
                        if s >= 2:
                            pe.wait_ge(o_evac, g * NSUP + s - 1)
                        for e in range(KG):
                            last = nc.tensor.matmul(ps[0][:, s % 2, e * P:(e + 1) * P], v[:, s, e * P:(e + 1) * P],
                                                    att[:, s % 2, :], start=(e == 0), stop=(s == 0 and e == KG - 1),
                                                    skip_group_check=True)
                        if s:
                            pe.wait_ge(S_ready, g * NSUP + s)
                        pe.wait_ge(qs_ready, g * NSUP + s + 1)
                        if s:
                            for e in range(KG):
                                last = nc.tensor.matmul(ps[0][:, s % 2, e * P:(e + 1) * P], S[:, e * P:(e + 1) * P],
                                                        qs[:], start=False, stop=(e == KG - 1), skip_group_check=True)
                        last.then_inc(o_done, 1)
                        pe.wait_ge(ksT_ready, g * NSUP + s + 1)
                        nc.tensor.matmul(ps[1][:, s % 2, :], ksT[:, s % 2, :], v[:, s, :], start=True,
                                         stop=True).then_inc(upd_done, 1)
                    pe.wait_ge(smp_ready, g + 1)
                    pe.wait_ge(att_ready, (g + 1) * NSUP)
                    nc.tensor.matmul(X[0][0:NS, 0:NS], qs[:, 0:NS], qd[:, 0:NS], start=True, stop=True)\
                        .then_inc(smp_att, 1)
                    nc.tensor.transpose(ps[0][0:NS, 2, 0:P], ks[:, 0:NS], ident[:]).then_inc(smp_kT, 1)
                    pe.wait_ge(smp_attr, g + 1)
                    pe.wait_ge(o_evac, (g + 1) * NSUP)
                    pe.wait_ge(S_ready, (g + 1) * NSUP)
                    for e in range(KG):
                        nc.tensor.matmul(ps[0][:, 0, e * NS:(e + 1) * NS], v[0:NS, NSUP, e * P:(e + 1) * P], att_s[:],
                                         start=(e == 0), stop=False, skip_group_check=True)
                    for b in range(NB):
                        pe.wait_ge(s0_loaded[b % 4], g * 32 + (b // 4) * 16 + 16)
                        for e in range(KG):
                            c = e * NS + b * TS
                            last = nc.tensor.matmul(ps[0][:, 0, c:c + TS], S0[b % 4][:, e * P:(e + 1) * P],
                                                    qd[:, b * TS:(b + 1) * TS], start=False,
                                                    stop=(b == NB - 1 and e == KG - 1), skip_group_check=True)
                        if b == NB - 1:
                            last.then_inc(o_done, 1)
                        pe.wait_ge(ksm_ready, g * NB + b + 1)
                        if b >= 2:
                            pe.wait_ge(s0_ready, g * NB + b - 1)
                        nc.tensor.matmul(ps[1][:, b % 2, :], ksm[:, b % 2, :], v[0:NS, NSUP, :], start=True,
                                         stop=True).then_inc(smp_upd, 1)
                    pe.sem_inc(L1.unit_done, 2)

                def head_sums():
                    u = GP.unit["NRM"]
                    set_ready(pe, L1, GP, g, u)
                    pe.wait_ge(oacc_ready, g * 3 + 3)
                    for t, (n0, width) in enumerate(NT):
                        last = nc.tensor.matmul(ps[u % 2][:, t, 0:width], ones[:], acc[:, n0:n0 + width], start=True,
                                                stop=True)
                    last.then_inc(L1.unit_done, 1)

                for name, _, _ in GLA_PLAN:
                    if name == "LG":
                        log_decay()
                    elif name[0:2] == "VT":
                        v_transpose(int(name[2]))
                    elif name == "ATT":
                        attend()
                    elif name == "NRM":
                        head_sums()
                    elif name[0] == "O":
                        project_inner(pe, L1, GP, g, name, L1.act_ready)
                    else:
                        project(pe, L1, GP, g, name)

            norm_sums(pe, 2)
            for s in range(NSUP + 1):
                n = P if s < NSUP else NS
                hi = s * P + n
                pe.wait_ge(y_ready, 1 if hi <= NT[0][1] else 2 if hi <= NT[2][0] else 3)
                if s == 1 or s == 0:
                    pe.wait_ge(std_ready, 9)
                if s >= 2:
                    pe.wait_ge(y_evac[s % 2], s // 2)
                for k in range(KD):
                    last = nc.tensor.transpose(ps[s % 2][0:n, k // 4, (k % 4) * P:(k % 4 + 1) * P],
                                               xT[:, k, s * P:s * P + n], ident[:])
                last.then_inc(yT_done, 1)


_INS = ["x_prompt", "x_sample", "c_prompt", "c_sample", "state_pool", "state_gla", "ada_w", "ada_b", "norm_g",
        "pool_w_in", "pool_w_grp", "pool_scale", "pool_w_out", "gla_w_in", "gla_w_gate_up", "gla_b_gate",
        "gla_norm_g", "gla_w_out", "final_g"]
_OUTS = [("y_prompt", (1, TP, D)), ("y_sample", (NB, TS, D)), ("new_pool_prompt", (1, 1, BUF, DI)),
         ("new_gla_prompt", (1, 1, NG, P, GW)), ("new_pool_sample", (1, NB, BUF, DI)),
         ("new_gla_sample", (1, NB, NG, P, GW))]


def kernel(**inputs):
    import numpy as _np
    import concourse.bacc as _bacc
    from concourse import mybir as _mybir
    from concourse.bass_utils import run_bass_kernel_spmd as _run

    nc = _bacc.Bacc("TRN2", target_bir_lowering=False, num_devices=1)
    arrays, args = {}, []
    for name in _INS:
        a = _np.ascontiguousarray(inputs[name])
        arrays[f"in_{name}"] = a
        args.append(nc.dram_tensor(f"in_{name}", a.shape, _mybir.dt.from_np(a.dtype), kind="ExternalInput").ap())
    for name, shape in _OUTS:
        args.append(nc.dram_tensor(f"out_{name}", shape, _mybir.dt.float32, kind="ExternalOutput").ap())
    trunk(nc, *args)
    r = _run(nc, [arrays], core_ids=[0])
    return tuple(r.results[0][f"out_{name}"] for name, _ in _OUTS)
```

```python
import concourse.bass as bass
from concourse import mybir
from contextlib import ExitStack

P = 128
D = 1024
DI = 2048
KD = D // P
NG = 4
GW = DI // NG
KG = GW // P
TP = 1024
NB = 8
TS = 8
NS = NB * TS
T = TP + NS
BUF = 15
SEG = BUF + TS
WE = BUF + TP + NB * SEG
SE0 = BUF + TP
RANK = 16
CH = 32
SUP = 4 * CH
NSUP = TP // SUP
EPS = 1e-6
NC_ = 1 + NB
NT = [(0, 364), (364, 362), (726, 362)]
N2P = TP - NT[2][0]
V_ADAB, V_NG, V_PS, V_BG, V_GN, V_FG = 0, 48, 64, 80, 84, 100
NVEC = 108

POOL_PLAN = [("U0", 1, "0"), ("U1", 1, "1"), ("U2", 1, "0"), ("U3", 1, "1"), ("Z0", 1, "0"),
             ("G01", 1, "10"), ("G23", 1, "10"), ("Z1", 1, "1"), ("Z2", 1, "0"), ("Z3", 1, "1"),
             ("O01", 1, "01"), ("O23", 1, "01"), ("O45", 1, "01"), ("O67", 1, "01")]
GLA_PLAN = [("Q", 1, "0"), ("K", 1, "1"), ("LG", 0, "0"), ("V0", 1, "1"), ("V1", 1, "0"), ("VT0", 0, "1"),
            ("V2", 1, "0"), ("VT1", 0, "1"), ("V3", 1, "0"), ("VT2", 0, "1"), ("VT3", 0, "1"),
            ("Z0", 1, "0"), ("Z1", 1, "0"), ("Z2", 1, "0"), ("ATT", 0, "1"), ("Z3", 1, "0"), ("NRM", 0, "1"),
            ("O01", 1, "01"), ("O23", 1, "01"), ("O45", 1, "01"), ("O67", 1, "01")]
FILL_START, FILL_STEP = 6, 2


class Plan:

    def __init__(self, rows):
        self.unit, self.slot, self.names, self.after = {}, {}, [], []
        self.set, self.place, self.in_set = [], [], [0, 0]
        for name, slots, sets in rows:
            self.unit[name] = len(self.set)
            for c in sets:
                self.set.append(int(c))
                self.place.append(self.in_set[int(c)])
                self.in_set[int(c)] += 1
            if slots:
                self.slot[name] = len(self.names)
                self.names.append(name)
                self.after.append(len(self.set))
        self.units, self.slots = len(self.set), len(self.names)


def trunk(nc, x_prompt, x_sample, c_prompt, c_sample, state_pool, state_gla, ada_w, ada_b, norm_g,
          pool_w_in, pool_w_grp, pool_scale, pool_w_out, gla_w_in, gla_w_gate_up, gla_b_gate,
          gla_norm_g, gla_w_out, final_g, y_prompt, y_sample, new_pool_prompt, new_gla_prompt,
          new_pool_sample, new_gla_sample):
    f32, f32r, i8 = mybir.dt.float32, mybir.dt.float32r, mybir.dt.int8
    ACT, ALU = mybir.ActivationFunctionType, mybir.AluOpType
    ds = bass.ds
    PP, GP = Plan(POOL_PLAN), Plan(GLA_PLAN)
    ctx = ExitStack()
    with ctx:
        def sb(name, shape, dt=f32, stack=ctx):
            return stack.enter_context(nc.sbuf_tensor(name, shape, dt))

        ident = sb("ident", [P, P])
        ones = sb("ones", [P, P])
        causal = sb("causal", [P, P], i8)
        causal_s = sb("causal_s", [NS, NS], i8)
        seq_rows = sb("seq_rows", [NS, NB])
        vecT = sb("vecT", [P, NVEC])
        csT = sb("csT", [P, KD, NC_])
        mods = [sb("mod0", [P, 24, NC_]), sb("mod1", [P, 24, NC_])]
        win_on = sb("win_on", [P, NG, 3])
        win_inv = sb("win_inv", [P, NG])
        cnt_inv = sb("cnt_inv", [P, NG, 16])
        eps = sb("eps", [P, 1])
        gs_tmp = sb("gs_tmp", [P, NS])
        xT = sb("xT", [P, KD, T])
        oT = sb("oT", [P, KG, T])
        stage = sb("stage", [P, 2, 1024])
        w_hi = sb("w_hi", [P, 2, 1024], f32r)
        w_lo = sb("w_lo", [P, 2, 1024], f32r)
        G = sb("G", [P, WE + 1])
        PQ = sb("PQ", [P, 2568])
        SZ = sb("SZ", [P, T])
        early = ExitStack()
        ada_stage = sb("ada_stage", [P, KD, P], stack=early)
        hist = sb("hist", [NB * BUF, 2, P], stack=early)
        tail_out = sb("tail_out", [NS + BUF, 2, P], stack=early)
        tail = sb("tail", [P, NS + BUF], stack=early)
        early.close()
        low_rank = ExitStack()
        w_gl = sb("w_gl", [P, KD, RANK], stack=low_rank)
        w_gl_hi = sb("w_gl_hi", [P, KD, RANK], f32r, stack=low_rank)
        w_gl_lo = sb("w_gl_lo", [P, KD, RANK], f32r, stack=low_rank)
        low_rank.close()
        S = sb("S", [P, GW])
        qd = sb("qd", [P, SUP])
        qs = sb("qs", [P, SUP])
        ks = sb("ks", [P, SUP])
        ksT = sb("ksT", [P, 2, P])
        att = sb("att", [P, 2, SUP])
        att_s = sb("att_s", [NS, NS])
        ksm = sb("ksm", [NS, 2, P])
        dec = sb("dec", [P, NSUP + NB])
        rms_cols = sb("rms_cols", [P, NSUP + 1])
        w_up = sb("w_up", [P, P])
        start = ExitStack()
        ada0 = sb("ada0", [P, 4, KD, 512], stack=start)
        start.close()
        end = ExitStack()
        y_rows = sb("y_rows", [P, 4, D], stack=end)
        end.close()
        h_hi = sb("h_hi", [P, KD, T], f32r)
        h_lo = sb("h_lo", [P, KD, T], f32r)
        heads = ExitStack()
        qT = sb("qT", [P, T], stack=heads)
        kT = sb("kT", [P, T], stack=heads)
        L = sb("L", [P, T], stack=heads)
        Kp = sb("Kp", [P, 4, SUP], stack=heads)
        qd_s = sb("qd_s", [P, NS], stack=heads)
        ki_s = sb("ki_s", [P, NS], stack=heads)
        ks_s = sb("ks_s", [P, NS], stack=heads)
        ksT_s = sb("ksT_s", [NS, P], stack=heads)
        v = sb("v", [P, NSUP + 1, GW], stack=heads)
        heads.close()
        start = ExitStack()
        ada0_gate = sb("ada0_gate", [P, 2, KD, 512], stack=start)
        start.close()
        a_hi = sb("a_hi", [P, KG, T], f32r)
        a_lo = sb("a_lo", [P, KG, T], f32r)

        s1 = PQ[:, 0:WE]
        s2 = PQ[:, 1300:1300 + WE]
        vT = [PQ[:, 0:T], PQ[:, T:2 * T]]
        szT = [PQ[:, 0:T], PQ[:, T:2 * T], SZ[:], PQ[:, 0:T]]
        scaled = [SZ[:], PQ[:, T:2 * T]]
        sqo = [G[:, i * GW:(i + 1) * GW] for i in range(2)]
        rms_diag = G[:, 0:T]
        rms_row = G[:, 0:T]
        sqx = [PQ[:, i * 364:(i + 1) * 364] for i in range(4)]
        ht = [PQ[:, (4 + i) * 364:(5 + i) * 364] for i in range(3)]
        hs = G[:, 0:KD * NS].rearrange("p (k t) -> p k t", k=KD)
        xrow = [G[:, 0:D], PQ[:, 0:D], PQ[:, 1300:1300 + D], SZ[:, 0:D], stage[:, 0, :]] + \
               [oT[:, i, 0:D] for i in range(KG)]
        rstd = SZ
        vec_rows = ada_stage[0:NVEC, 0, :]
        c_rows = stage[0:NC_, 1, :]
        glT = PQ[:, 2 * T:2 * T + NT[0][1]]

        psA = ctx.enter_context(nc.psum_tensor("psA", [P, 3, 512], f32))
        psB = ctx.enter_context(nc.psum_tensor("psB", [P, 3, 512], f32))
        ps = [psA, psB]
        X = [ctx.enter_context(nc.psum_tensor(f"X{i}", [P, 512], f32)) for i in range(2)]

        def sem(name):
            return ctx.enter_context(nc.semaphore(name))

        c_loaded, vec_loaded, consts_ready = sem("c_loaded"), sem("vec_loaded"), sem("consts_ready")
        x_loaded = [sem(f"x_loaded{i}") for i in range(NSUP + 1)]
        ada0_loaded = [sem(f"ada0_loaded{i}") for i in range(6)]
        cT_done, vT_done, cs_ready, vec_ready = sem("cT_done"), sem("vecT_done"), sem("cs_ready"), sem("vec_ready")
        xT_done, xT_ready = sem("xT_done"), sem("xT_ready")
        mod_done, mod_ready, gate_ready = sem("mod_done"), sem("mod_ready"), sem("gate_ready")
        sq_ready, ss_done, std_ready, rstd_ready = sem("sq_ready"), sem("ss_done"), sem("std_ready"), sem("rstd_ready")
        ht_ready, hhi_ready, h_ready, hs_ready, hshi_ready = (sem("ht_ready"), sem("hhi_ready"), sem("h_ready"),
                                                              sem("hs_ready"), sem("hshi_ready"))
        x_final = sem("x_final")
        copied = sem("copied")
        chain_v, chain_a, chain_p = sem("chain_v"), sem("chain_a"), sem("chain_p")
        y_ready, yT_done, y_evac = sem("y_ready"), sem("yT_done"), [sem("y_evac_a"), sem("y_evac_v")]
        y_stored = [sem(f"y_stored{i}") for i in range(4)]

        class Stream:

            def __init__(self, tag):
                self.w_loaded = [sem(f"{tag}_w_loaded{i}") for i in range(2)]
                self.hi_done = sem(f"{tag}_hi_done")
                self.lo_done = sem(f"{tag}_lo_done")
                self.unit_done = sem(f"{tag}_unit_done")
                self.evac = [sem(f"{tag}_evac{i}") for i in range(2)]
                self.act_ready = sem(f"{tag}_gated")

        L0, L1 = Stream("pool"), Stream("gla")
        ada_loaded, mini_done, mini_free = sem("ada_loaded"), sem("mini_done"), sem("mini_free")
        hist_loaded, hist_T, hist_evac = [sem("hist_loaded0"), sem("hist_loaded1")], sem("hist_T"), sem("hist_evac")
        pooled, diff_ready = sem("pooled"), sem("diff_ready")
        tail_stored = [sem("tail_stored0"), sem("tail_stored1")]
        wgl_loaded, wgl_hi, wgl_lo, gl_done, gl_ready = (sem("wgl_loaded"), sem("wgl_hi"), sem("wgl_lo"),
                                                          sem("gl_done"), sem("gl_ready"))
        wup_loaded, sp_ready, lg_ready = sem("wup_loaded"), sem("sp_ready"), sem("lg_ready")
        dec_ready = sem("dec_ready")
        kp_zero, kp_exp, kp_ready = sem("kp_zero"), sem("kp_exp"), sem("kp_ready")
        qd_arg, qd_exp, qd_ready = sem("qd_arg"), sem("qd_exp"), sem("qd_ready")
        qs_exp, qs_ready, ks_exp, ks_ready = sem("qs_exp"), sem("qs_ready"), sem("ks_exp"), sem("ks_ready")
        att_done, att_ready, o_done, o_evac = sem("att_done"), sem("att_ready"), sem("o_done"), sem("o_evac")
        kT_done, ksT_ready, upd_done, S_ready = sem("kT_done"), sem("ksT_ready"), sem("upd_done"), sem("S_ready")
        smp_arg, smp_exp, smp_ready = sem("smp_arg"), sem("smp_exp"), sem("smp_ready")
        smp_att, smp_attr, smp_kT, ksm_ready = sem("smp_att"), sem("smp_attr"), sem("smp_kT"), sem("ksm_ready")
        s0_loaded = [sem(f"s0_loaded{i}") for i in range(4)]
        s0_stored = [sem(f"s0_stored{i}") for i in range(4)]
        s0_ready, smp_inter, smp_upd = sem("s0_ready"), sem("smp_inter"), sem("smp_upd")
        S_stored = sem("S_stored")
        smp_o_done, smp_o_evac, smp_ksT = sem("smp_o_done"), sem("smp_o_evac"), sem("smp_ksT")
        osq_ready, osum_ready, oms_done, orms_ready, odiag_ready = (
            sem("osq_ready"), sem("osum_ready"), sem("oms_done"), sem("orms_ready"), sem("odiag_ready"))
        gated, gated_hi = sem("gated"), sem("gated_hi")

        def units(plan, g, n):
            return g * plan.units + n + 3

        def evacs(plan, g, u):
            return g * plan.in_set[plan.set[u]] + plan.place[u] + 2

        def token_parts():
            return [(0, 0, 0, 364), (1, 364, 0, 362), (2, 726, 0, N2P)]

        def wait_apart(eng, what, count):
            count = eng.to_reg(count)
            eng.wait_ge(vec_ready, 1)
            eng.wait_ge(what, count)

        def split_slot(lay, plan, eng, g, j):
            before = plan.after[j - 2] if j >= 2 else plan.after[j - 2] - plan.units
            eng.wait_ge(lay.unit_done, units(plan, g, before))
            eng.wait_ge(lay.w_loaded[j % 2], 16 * (plan.slots // 2) * g + 16 * (j // 2 + 1))
            nc.scalar.activation(w_hi[:, j % 2, :], stage[:, j % 2, :], ACT.Copy).then_inc(lay.hi_done, 1)

        def lo_slots(lay, plan, eng, g, j):
            eng.wait_ge(lay.hi_done, g * plan.slots + j + 1)
            nc.gpsimd.tensor_tensor(w_lo[:, j % 2, :], stage[:, j % 2, :], w_hi[:, j % 2, :].bitcast(f32),
                                    ALU.subtract).then_inc(lay.lo_done, 1)

        def slot_free(lay, plan, g, j, eng):
            wait_apart(eng, lay.lo_done, g * plan.slots + j + 1)

        def norm_squares(act, r, x_here):
            act.wait_ge(*x_here)
            i = 24 * r
            for t, (n0, w) in enumerate(NT):
                for k in range(KD):
                    if i - 24 * r >= 4:
                        act.wait_ge(ss_done, i - 3)
                    nc.scalar.activation(sqx[i % 4][:, 0:w], xT[:, k, n0:n0 + w], ACT.Square).then_inc(sq_ready, 1)
                    i += 1
            for t, (n0, w) in enumerate(NT):
                act.wait_ge(ss_done, 24 * r + 8 * t + 8)
                nc.scalar.activation(rstd[:, n0:n0 + w], ps[1][:, t, 0:w], ACT.Sqrt, bias=eps[:, 0:1],
                                     scale=1.0 / D).then_inc(std_ready, 1)

        def norm_sums(pe, r):
            i = 24 * r
            for t, (n0, w) in enumerate(NT):
                for k in range(KD):
                    pe.wait_ge(sq_ready, i + 1)
                    nc.tensor.matmul(ps[1][:, t, 0:w], ones[:], sqx[i % 4][:, 0:w], start=(k == 0),
                                     stop=(k == KD - 1)).then_inc(ss_done, 1)
                    i += 1

        def rms_inverse(dve, r):
            for t, (n0, w) in enumerate(NT):
                dve.wait_ge(std_ready, 3 * r + t + 1)
                nc.vector.reciprocal(rstd[:, n0:n0 + w], rstd[:, n0:n0 + w]).then_inc(rstd_ready, 1)
            dve.wait_ge(rstd_ready, 3 * r + 3)

        def h_vector(dve, r, mod):
            i = 24 * r

            def low(i):
                t, k = (i - 24 * r) // KD, i % KD
                n0, w = token_parts()[t][1], token_parts()[t][3]
                dve.wait_ge(hhi_ready, i + 1)
                nc.vector.scalar_tensor_tensor(
                    out=h_lo[:, k, n0:n0 + w], in0=ht[i % 3][:, 0:w], scalar=mod[:, k, 0:1],
                    in1=h_hi[:, k, n0:n0 + w].bitcast(f32), op0=ALU.add, op1=ALU.subtract).then_inc(h_ready, 1)

            for t, n0, _, w in token_parts():
                if t == 2:
                    a_s = mod[:, 8:16, 1:NC_].unsqueeze(3).broadcast_to([P, KD, NB, TS])
                    sh_s = mod[:, 0:8, 1:NC_].unsqueeze(3).broadcast_to([P, KD, NB, TS])
                    r_s = rstd[:, TP:T].rearrange("p (b t) -> p b t", b=NB).unsqueeze(1).broadcast_to([P, KD, NB, TS])
                    x_s = xT[:, :, TP:T].rearrange("p k (b t) -> p k b t", b=NB)
                    h4 = hs.rearrange("p k (b t) -> p k b t", b=NB)
                    nc.vector.tensor_tensor(h4, x_s, r_s, ALU.mult).then_inc(hs_ready, 1)
                    dve.wait_ge(hs_ready, 3 * r + 1)
                    nc.vector.tensor_tensor(h4, h4, a_s, ALU.mult).then_inc(hs_ready, 1)
                    dve.wait_ge(hs_ready, 3 * r + 2)
                    nc.vector.tensor_tensor(h4, h4, sh_s, ALU.add).then_inc(hs_ready, 1)
                for k in range(KD):
                    if i - 24 * r >= 3:
                        dve.wait_ge(h_ready, 25 * r + (i - 24 * r) - 2)
                    nc.vector.scalar_tensor_tensor(
                        out=ht[i % 3][:, 0:w], in0=xT[:, k, n0:n0 + w], scalar=mod[:, 8 + k, 0:1],
                        in1=rstd[:, n0:n0 + w], op0=ALU.mult, op1=ALU.mult).then_inc(ht_ready, 1)
                    if i - 24 * r >= 1:
                        low(i - 1)
                    i += 1
            low(i - 1)
            dve.wait_ge(hshi_ready, r + 1)
            nc.vector.tensor_tensor(h_lo[:, :, TP:T], hs, h_hi[:, :, TP:T].bitcast(f32),
                                    ALU.subtract).then_inc(h_ready, 1)

        def h_scalar(act, r, mod):
            i = 24 * r
            for t, n0, _, w in token_parts():
                for k in range(KD):
                    act.wait_ge(ht_ready, i + 1)
                    nc.scalar.activation(h_hi[:, k, n0:n0 + w], ht[i % 3][:, 0:w], ACT.Identity,
                                         bias=mod[:, k, 0:1]).then_inc(hhi_ready, 1)
                    i += 1
            act.wait_ge(hs_ready, 3 * r + 3)
            nc.scalar.activation(h_hi[:, :, TP:T], hs, ACT.Copy).then_inc(hshi_ready, 1)

        def mod_finish(dve, r, mod):
            g_b = vecT[:, V_NG + 8 * r:V_NG + 8 * r + 8].unsqueeze(2).broadcast_to([P, KD, NC_])
            nc.vector.scalar_tensor_tensor(out=mod[:, 8:16, :], in0=mod[:, 8:16, :], scalar=1.0, in1=g_b,
                                           op0=ALU.add, op1=ALU.mult).then_inc(mod_ready, 1)

        def h_wait(pe, r):
            pe.wait_ge(h_ready, 25 * r + 25)

        def product_step(p, u, k, kt, weight, act_hi, act_lo):
            for pas, (w, a) in enumerate(((w_hi, act_hi), (w_hi, act_lo), (w_lo, act_hi))):
                for t, (n0, width) in enumerate(NT):
                    last = nc.tensor.matmul(ps[u][:, t, 0:width], weight(w[:, p, :], k), a[:, k, n0:n0 + width],
                                            start=(k == 0 and pas == 0), stop=(k == kt - 1 and pas == 2))
            return last

        def product(pe, p, u, kt, weight, act_hi, act_lo, before_k=None):
            for k in range(kt):
                if before_k:
                    before_k(k)
                last = product_step(p, u, k, kt, weight, act_hi, act_lo)
            return last

        def w8(w, k):
            return w[:, k * P:(k + 1) * P]

        def w4(half):
            return lambda w, k: w[:, k * 256 + half * P:k * 256 + half * P + P]

        def slot_ready(pe, lay, plan, g, name):
            pe.wait_ge(lay.lo_done, g * plan.slots + plan.slot[name] + 3)

        def set_ready(pe, lay, plan, g, u):
            pe.wait_ge(lay.evac[plan.set[u]], g * plan.in_set[plan.set[u]] + plan.place[u] + 1)

        def project(pe, lay, plan, g, name):
            u = plan.unit[name]
            set_ready(pe, lay, plan, g, u)
            slot_ready(pe, lay, plan, g, name)
            product(pe, plan.slot[name] % 2, plan.set[u], KD, w8, h_hi, h_lo).then_inc(lay.unit_done, 1)

        def project_inner(pe, lay, plan, g, name, ready):
            for half in range(2):
                u = plan.unit[name] + half
                set_ready(pe, lay, plan, g, u)
                if half == 0:
                    slot_ready(pe, lay, plan, g, name)
                product(pe, plan.slot[name] % 2, plan.set[u], KG, w4(half), a_hi, a_lo,
                        before_k=lambda k: pe.wait_ge(ready, g * KG + k + 1)).then_inc(lay.unit_done, 1)

        def add_branch(dve, lay, plan, g, name, mod, chain):
            for half in range(2):
                m = 2 * int(name[1]) // 2 + half
                u = plan.unit[name] + half
                src = ps[plan.set[u]]
                dve.wait_ge(lay.unit_done, units(plan, g, u + 1))
                nc.vector.tensor_tensor(gs_tmp[:].rearrange("p (b t) -> p b t", b=NB),
                                        src[:, 2, N2P:N2P + NS].rearrange("p (b t) -> p b t", b=NB),
                                        mod[:, 16 + m, 1:NC_].unsqueeze(2).broadcast_to([P, NB, TS]),
                                        ALU.mult).then_inc(chain_v, 1)
                chain[0] += 1
                for t, n0, _, w in token_parts():
                    last = nc.vector.scalar_tensor_tensor(
                        out=xT[:, m, n0:n0 + w], in0=src[:, t, 0:w], scalar=mod[:, 16 + m, 0:1],
                        in1=xT[:, m, n0:n0 + w], op0=ALU.mult, op1=ALU.add)
                last.then_inc(lay.evac[plan.set[u]], 1)
                dve.wait_ge(chain_v, chain[0])
                nc.vector.tensor_tensor(xT[:, m, TP:T], xT[:, m, TP:T], gs_tmp[:], ALU.add).then_inc(chain_v, 1)
                chain[0] += 1
                dve.wait_ge(chain_v, chain[0])

        def gate_tile(dve, lay, plan, g, i, chain, first_dep=None):
            u = plan.unit[f"Z{i}"]
            dve.wait_ge(lay.evac[plan.set[u]], evacs(plan, g, u))
            nc.vector.tensor_tensor(oT[:, i, :], oT[:, i, :], SZ[:], ALU.mult).then_inc(chain_v, 1)
            chain[0] += 1
            dve.wait_ge(chain_v, chain[0])
            nc.vector.tensor_copy(a_hi[:, i, :], oT[:, i, :]).then_inc(chain_v, 1)
            chain[0] += 1
            dve.wait_ge(chain_v, chain[0])
            nc.vector.tensor_tensor(a_lo[:, i, :], oT[:, i, :], a_hi[:, i, :].bitcast(f32),
                                    ALU.subtract).then_inc(lay.act_ready, 1)
            dve.wait_ge(lay.act_ready, g * KG + i + 1)

        def add_head(dve, g, name, chain):
            for half in range(2):
                m = int(name[1]) + half
                u = GP.unit[name] + half
                src, row = ps[GP.set[u]], scaled[half]
                dve.wait_ge(L1.unit_done, units(GP, g, u + 1))
                nc.vector.tensor_tensor(row[:, TP:T].rearrange("p (b t) -> p b t", b=NB),
                                        src[:, 2, N2P:N2P + NS].rearrange("p (b t) -> p b t", b=NB),
                                        mods[1][:, 16 + m, 1:NC_].unsqueeze(2).broadcast_to([P, NB, TS]),
                                        ALU.mult).then_inc(chain_v, 1)
                chain[0] += 1
                for t, n0, _, w in token_parts():
                    last = nc.vector.scalar_tensor_tensor(
                        out=row[:, n0:n0 + w], in0=src[:, t, 0:w], scalar=mods[1][:, 16 + m, 0:1],
                        in1=rms_row[:, n0:n0 + w], op0=ALU.mult, op1=ALU.mult)
                dve.wait_ge(chain_v, chain[0])
                nc.vector.tensor_tensor(row[:, TP:T], row[:, TP:T], rms_row[:, TP:T], ALU.mult).then_inc(chain_v, 1)
                chain[0] += 1
                dve.wait_ge(chain_v, chain[0])
                nc.vector.tensor_tensor(xT[:, m, :], xT[:, m, :], row, ALU.add).then_inc(L1.evac[GP.set[u]], 1)
                dve.wait_ge(L1.evac[GP.set[u]], evacs(GP, g, u))

        def silu_out(act, lay, plan, g, i):
            u = plan.unit[f"Z{i}"]
            act.wait_ge(lay.unit_done, units(plan, g, u + 1))
            if i:
                act.wait_ge(lay.act_ready, g * KG + i)
            for t, (n0, w) in enumerate(NT):
                last = nc.scalar.activation(SZ[:, n0:n0 + w], ps[plan.set[u]][:, t, 0:w], ACT.Silu)
            last.then_inc(lay.evac[plan.set[u]], 1)

        w_in0 = pool_w_in[0].rearrange("(k p) n -> p k n", p=P)
        w_in1 = gla_w_in[0].rearrange("(k p) n -> p k n", p=P)
        w_out0 = pool_w_out[0].rearrange("(q p) n -> p q n", p=P)
        w_out1 = gla_w_out[0].rearrange("(q p) n -> p q n", p=P)
        w_grp = pool_w_grp[0].rearrange("g (k p) n -> p (g k) n", p=P)
        ada_v = [ada_w[i].rearrange("(k p) n -> p k n", p=P) for i in range(2)]
        hist_v = state_pool[0].rearrange("b r n -> (b r) n")
        o_sem = sem("out_stored")

        block = ctx.enter_context(nc.Block())

        @block.sync
        def _(sp):
            sp.dma_start(c_rows[0:1, :], c_prompt).then_inc(c_loaded, 16)
            sp.dma_start(c_rows[1:NC_, :], c_sample).then_inc(c_loaded, 16)
            for lo, src in ((V_ADAB, ada_b.rearrange("l (m p) -> (l m) p", p=P)),
                            (V_NG, norm_g.rearrange("l (m p) -> (l m) p", p=P)),
                            (V_PS, pool_scale[0].rearrange("(m p) -> m p", p=P)),
                            (V_BG, gla_b_gate[0].rearrange("(m p) -> m p", p=P)),
                            (V_GN, gla_norm_g[0].rearrange("(m p) -> m p", p=P)),
                            (V_FG, final_g.rearrange("(m p) -> m p", p=P))):
                sp.dma_start(vec_rows[lo:lo + src.shape[0], :], src).then_inc(vec_loaded, 16)
            for s in range(NSUP + 1):
                n = P if s < NSUP else NS
                src = x_prompt[0, s * P:(s + 1) * P, :] if s < NSUP else x_sample.rearrange("b t n -> (b t) n")
                sp.dma_start(xrow[s][0:n, :], src).then_inc(x_loaded[s], 16)
            for q in range(6):
                dst = ada0[:, q, :, :] if q < 4 else ada0_gate[:, q - 4, :, :]
                sp.dma_start(dst, ada_v[0][:, :, q * 512:(q + 1) * 512]).then_inc(ada0_loaded[q], 16)
            sp.dma_start(new_pool_sample[0, :, 0:BUF - TS, :], state_pool[0, :, TS:BUF, :]).then_inc(copied, 16)

            with sp.Fori(0, NG) as g:
                def load(j):
                    slot_free(L0, PP, g, j, sp)
                    name = PP.names[j]
                    i = int(name[1])
                    dst = stage[:, j % 2, :]
                    if name[0] in "UZ":
                        src = w_in0[:, :, ds(g * GW + (DI if name[0] == "Z" else 0) + i * P, P)]
                        dst = dst.rearrange("p (k n) -> p k n", k=KD)
                    else:
                        src = (w_grp if name[0] == "G" else w_out0)[:, ds(g * KG, KG), i * P:(i + 2) * P]
                        dst = dst.rearrange("p (k n) -> p k n", k=KG)
                    sp.dma_start(dst, src).then_inc(L0.w_loaded[j % 2], 16)

                def load_ada(a, minis):
                    wait_apart(sp, mini_done, g * 10 + minis + 1)
                    sp.dma_start(ada_stage[:], ada_v[1][:, :, ds(g * 6 * P + a * P, P)]).then_inc(ada_loaded, 16)

                def load_hist(i):
                    wait_apart(sp, hist_T, g * KG + i + 1)
                    sp.dma_start(hist[:, i % 2, :], hist_v[:, ds(g * GW + i * P, P)]).then_inc(hist_loaded[i % 2], 16)

                load_ada(0, 0)
                load_hist(0)
                load_hist(1)
                for j in range(PP.slots):
                    load(j)
                    if j in (2, 3):
                        load_hist(j)
                    if j == 3:
                        load_ada(1, 1)
                    if 8 <= j <= 11:
                        load_ada(j - 6, j - 2)

            sp.wait_ge(sq_ready, 25)
            sp.dma_start(w_gl[:], w_in1[:, :, 2 * 512 + 2 * DI:2 * 512 + 2 * DI + RANK]).then_inc(wgl_loaded, 16)
            for i in range(4):
                sp.sem_inc(s0_stored[i], 16)
            sp.sem_inc(S_stored, 16)
            with sp.Fori(0, NG) as g:
                wait_apart(sp, lg_ready, g + 1)
                for t in range(3):
                    sp.dma_start(w_up[32 * t:32 * t + RANK, :], gla_w_gate_up[0][:, ds(g * P, P)])\
                        .then_inc(wup_loaded, 16)

                def load_state(b):
                    wait_apart(sp, upd_done, g * NSUP + b + 1)
                    sp.dma_start(v[:, b, :], state_gla[0, b, ds(g, 1), :, :].rearrange("a p n -> p (a n)"))\
                        .then_inc(s0_loaded[b % 4], 16)

                def store_state(b):
                    wait_apart(sp, s0_ready, g * NB + b + 1)
                    wait_apart(sp, s0_stored[b % 4], g * 32 + (b // 4) * 16 + 16)
                    sp.dma_start(new_gla_sample[0, b, ds(g, 1), :, :].rearrange("a p n -> p (a n)"), v[:, b, :])\
                        .then_inc(s0_stored[b % 4], 16)

                def load(j):
                    slot_free(L1, GP, g, j, sp)
                    name = GP.names[j]
                    dst = stage[:, j % 2, :]
                    if name[0] == "O":
                        i = int(name[1])
                        src = w_out1[:, ds(g * KG, KG), i * P:(i + 2) * P]
                        dst = dst.rearrange("p (k n) -> p k n", k=KG)
                    else:
                        col = {"Q": g * P, "K": g * P + 512}.get(name)
                        if col is None:
                            col = g * GW + 1024 + (DI if name[0] == "Z" else 0) + int(name[1]) * P
                        src = w_in1[:, :, ds(col, P)]
                        dst = dst.rearrange("p (k n) -> p k n", k=KD)
                    sp.dma_start(dst, src).then_inc(L1.w_loaded[j % 2], 16)

                for j in range(GP.slot["Z3"] + 1):
                    load(j)
                for s in range(NSUP + 2):
                    if s < NSUP:
                        load_state(s)
                    if s == 2:
                        load(GP.slot["O01"])
                    if s == 6:
                        load(GP.slot["O23"])
                    if s == NSUP:
                        wait_apart(sp, S_ready, (g + 1) * NSUP)
                        sp.dma_start(new_gla_prompt[0, 0, ds(g, 1), :, :].rearrange("a p n -> p (a n)"), S[:])\
                            .then_inc(S_stored, 16)
                    if s >= 2:
                        store_state(s - 2)
                for j in range(GP.slot["O45"], GP.slots):
                    load(j)

            for i in range(4):
                sp.wait_ge(s0_stored[i], 16 * (1 + 2 * NG))
            sp.wait_ge(S_stored, 16 * (1 + NG))

            for s in range(NSUP + 1):
                n = P if s < NSUP else NS
                sp.wait_ge(y_evac[s % 2], s // 2 + 1)
                dst = y_prompt[0, s * P:(s + 1) * P, :] if s < NSUP else y_sample.rearrange("b t n -> (b t) n")
                sp.dma_start(dst, y_rows[0:n, s % 4, :]).then_inc(y_stored[s % 4], 16)
            for i in range(4):
                sp.wait_ge(y_stored[i], 16 * (3 if i == 0 else 2))
            sp.wait_ge(copied, 16)

        @block.gpsimd
        def _(pool):
            n = 0

            def link(ins):
                nonlocal n
                n += 1
                ins.then_inc(chain_p, 1)
                pool.wait_ge(chain_p, n)

            link(pool.memset(ident[:], 0.0))
            link(pool.affine_select(out=ident[:], in_=ident[:], compare_op=ALU.not_equal, fill=1.0, base=0,
                                    pattern=[[-1, P]], channel_multiplier=1))
            link(pool.memset(ones[:], 1.0))
            link(pool.memset(causal[:], 1))
            link(pool.affine_select(out=causal[:], in_=causal[:], compare_op=ALU.is_ge, fill=0, base=0,
                                    pattern=[[1, P]], channel_multiplier=-1))
            link(pool.memset(seq_rows[:], 1.0))
            link(pool.affine_select(out=seq_rows[:], in_=seq_rows[:], compare_op=ALU.is_ge, fill=0.0, base=0,
                                    pattern=[[-TS, NB]], channel_multiplier=1))
            link(pool.affine_select(out=seq_rows[:], in_=seq_rows[:], compare_op=ALU.is_ge, fill=0.0, base=TS - 1,
                                    pattern=[[TS, NB]], channel_multiplier=-1))
            cs3 = causal_s[:].rearrange("p (b t) -> p b t", b=NB)
            link(pool.memset(causal_s[:], 1))
            link(pool.affine_select(out=cs3, in_=cs3, compare_op=ALU.is_ge, fill=0, base=0,
                                    pattern=[[-TS, NB], [0, TS]], channel_multiplier=1))
            link(pool.affine_select(out=cs3, in_=cs3, compare_op=ALU.is_ge, fill=0, base=0,
                                    pattern=[[TS, NB], [1, TS]], channel_multiplier=-1))
            link(pool.memset(win_on[:], 0.0))
            for k in range(3):
                link(pool.memset(win_on[:, k + 1:NG, k:k + 1], 1.0))
            for g in range(NG):
                w = 2 << g
                link(pool.memset(win_inv[:, g:g + 1], 1.0 / w))
                link(pool.memset(cnt_inv[:, g, :], 1.0 / w))
                for t in range(w - 1):
                    link(pool.memset(cnt_inv[:, g, t:t + 1], 1.0 / (t + 1)))
            link(pool.memset(eps[:], EPS))
            pool.memset(gs_tmp[:], 0.0).then_inc(consts_ready, 1)

            pool.wait_ge(xT_done, NSUP + 1)
            pool.sem_inc(L0.lo_done, 2)
            with pool.Fori(0, NG) as g:
                for j in range(PP.slots):
                    lo_slots(L0, PP, pool, g, j)

            pool.wait_ge(wgl_hi, 1)
            pool.tensor_tensor(w_gl_lo[:], w_gl[:], w_gl_hi[:].bitcast(f32), ALU.subtract).then_inc(wgl_lo, 1)
            pool.sem_inc(L1.lo_done, 2)
            pool.sem_clear(chain_p)
            with pool.Fori(0, NG) as g:
                for j in range(GP.slot["Z1"] + 1):
                    lo_slots(L1, GP, pool, g, j)
                wait_apart(pool, L1.unit_done, units(GP, g, GP.unit["V0"] + 1))
                pool.memset(Kp[:], 0.0).then_inc(kp_zero, 1)

                def scale_kp(s):
                    pool.wait_ge(kp_exp, g * NSUP + s + 1)
                    for b in range(4):
                        last = pool.tensor_tensor(Kp[:, b, 0:CH * (b + 1)], Kp[:, b, 0:CH * (b + 1)],
                                                  kT[:, s * SUP:s * SUP + CH * (b + 1)], ALU.mult)
                    last.then_inc(kp_ready, 1)

                def square_sum(s):
                    n = P if s < NSUP else NS
                    q = sqo[s % 2]
                    pool.wait_ge(osq_ready, g * (NSUP + 1) + s + 1)
                    pool.tensor_tensor(q[:, 0:2 * n], q[:, 0:2 * n], q[:, 2 * n:4 * n], ALU.add).then_inc(chain_p, 1)
                    pool.wait_ge(chain_p, s + 1)
                    pool.tensor_tensor(q[:, 0:n], q[:, 0:n], q[:, n:2 * n], ALU.add).then_inc(osum_ready, 1)

                scale_kp(0)
                for s in range(NSUP + 1):
                    if s + 1 < NSUP:
                        scale_kp(s + 1)
                    if s == 0:
                        lo_slots(L1, GP, pool, g, GP.slot["Z2"])
                    if s == 4:
                        lo_slots(L1, GP, pool, g, GP.slot["Z3"])
                    if s == NSUP:
                        lo_slots(L1, GP, pool, g, GP.slot["O01"])
                    square_sum(s)
                for j in range(GP.slot["O23"], GP.slots):
                    lo_slots(L1, GP, pool, g, j)
                pool.sem_clear(chain_p)

        @block.scalar
        def _(act):
            act.wait_ge(cT_done, 1)
            nc.scalar.activation(csT[:].rearrange("p k c -> p (k c)"), X[0][:, 0:KD * NC_], ACT.Silu).then_inc(cs_ready, 1)
            act.wait_ge(vT_done, 1)
            nc.scalar.activation(vecT[:], X[1][:, 0:NVEC], ACT.Copy).then_inc(vec_ready, 1)
            for s in range(NSUP + 1):
                n = P if s < NSUP else NS
                act.wait_ge(xT_done, s + 1)
                nc.scalar.activation(xT[:, :, s * P:s * P + n],
                                     ps[s % 2][:, 0:2, :].rearrange("p a (k t) -> p (a k) t", k=4)[:, :, 0:n],
                                     ACT.Copy).then_inc(xT_ready, 1)
            norm_squares(act, 0, (xT_ready, NSUP + 1))
            act.wait_ge(mod_ready, 1)
            h_scalar(act, 0, mods[0])
            act.sem_inc(mini_free, 1)
            act.sem_inc(hist_evac, 1)
            act.sem_inc(tail_stored[0], 32)
            act.sem_inc(tail_stored[1], 32)

            with act.Fori(0, NG) as g:
                def u_out(i):
                    u = PP.unit[f"U{i}"]
                    act.wait_ge(L0.unit_done, units(PP, g, u + 1))
                    act.wait_ge(pooled, g * KG + i + 1)
                    act.wait_ge(hist_T, g * KG + i + 3)
                    seg = G[:, SE0:SE0 + NB * SEG].rearrange("p (b r) -> p b r", b=NB)
                    nc.scalar.activation(seg[:, :, 0:BUF], X[0][:, 0:NB * BUF].rearrange("p (b r) -> p b r", b=NB),
                                         ACT.Copy).then_inc(hist_evac, 1)
                    for t, n0, _, w in token_parts():
                        nc.scalar.activation(G[:, BUF + n0:BUF + n0 + w], ps[PP.set[u]][:, t, 0:w], ACT.Copy)
                    smp = ps[PP.set[u]][:, 2, N2P:N2P + NS]
                    nc.scalar.activation(seg[:, :, BUF:SEG], smp.rearrange("p (b t) -> p b t", b=NB), ACT.Copy)
                    act.wait_ge(mini_done, g * 10 + (1 + i) + 1)
                    nc.scalar.activation(tail[:, 0:NS], smp, ACT.Copy)
                    nc.scalar.activation(tail[:, NS:NS + BUF], ps[PP.set[u]][:, 2, N2P - BUF:N2P], ACT.Copy)\
                        .then_inc(L0.evac[PP.set[u]], 1)

                def ada_out(a, mini):
                    act.wait_ge(mini_done, g * 10 + mini + 2)
                    nc.scalar.activation(mods[1][:].rearrange("p m c -> p (m c)")[:, ds(g * 6 * NC_ + a * NC_, NC_)],
                                         X[1][:, 0:NC_], ACT.Identity,
                                         bias=vecT[:, ds(g * 6 + (V_ADAB + 24 + a), 1)]).then_inc(mini_free, 1)

                def tail_store(i):
                    act.wait_ge(mini_done, g * 10 + (1 + i) + 2)
                    act.wait_ge(tail_stored[i % 2], g * 64 + (i // 2) * 32 + 32)
                    nc.scalar.activation(tail_out[:, i % 2, :], X[1][0:NS + BUF, 0:P], ACT.Copy).then_inc(mini_free, 1)
                    act.wait_ge(mini_free, g * 10 + (1 + i) + 2)
                    act.dma_start(new_pool_sample[0, :, BUF - TS:BUF, ds(g * GW + i * P, P)],
                                  tail_out[0:NS, i % 2, :]).then_inc(tail_stored[i % 2], 16)
                    act.dma_start(new_pool_prompt[0, 0, :, ds(g * GW + i * P, P)],
                                  tail_out[NS:NS + BUF, i % 2, :]).then_inc(tail_stored[i % 2], 16)

                split_slot(L0, PP, act, g, 0)
                split_slot(L0, PP, act, g, 1)
                extra = {0: lambda: ada_out(0, 0), 1: lambda: tail_store(0), 2: lambda: tail_store(1),
                         3: lambda: tail_store(2), 4: lambda: tail_store(3), 5: lambda: ada_out(1, 5),
                         6: lambda: ada_out(2, 6), 7: lambda: ada_out(3, 7), 8: lambda: ada_out(4, 8),
                         9: lambda: ada_out(5, 9)}
                for j, name in enumerate(PP.names):
                    if name[0] == "U":
                        u_out(int(name[1]))
                    if name[0] == "Z":
                        silu_out(act, L0, PP, g, int(name[1]))
                    if j + 2 < PP.slots:
                        split_slot(L0, PP, act, g, j + 2)
                    if j in extra:
                        extra[j]()
            for i in range(2):
                act.wait_ge(tail_stored[i], 32 + 64 * NG)

            norm_squares(act, 1, (x_final, 1))
            act.wait_ge(mod_ready, 2)
            h_scalar(act, 1, mods[1])
            act.wait_ge(wgl_loaded, 16)
            nc.scalar.activation(w_gl_hi[:], w_gl[:], ACT.Copy).then_inc(wgl_hi, 1)
            for t, (n0, w) in enumerate(NT):
                act.wait_ge(gl_done, 1)
                last = nc.scalar.activation(glT[32 * t:32 * t + RANK, 0:w], ps[0][0:RANK, t, 0:w], ACT.Copy)
            last.then_inc(gl_ready, 1)

            with act.Fori(0, NG) as g:
                def copy_out(name, dst, scale=1.0, wait=None):
                    u = GP.unit[name]
                    act.wait_ge(L1.unit_done, units(GP, g, u + 1))
                    if wait:
                        wait()
                    for t, (n0, w) in enumerate(NT):
                        last = nc.scalar.activation(dst[:, n0:n0 + w], ps[GP.set[u]][:, t, 0:w], ACT.Copy, scale=scale)
                    last.then_inc(L1.evac[GP.set[u]], 1)

                split_slot(L1, GP, act, g, 0)
                split_slot(L1, GP, act, g, 1)
                copy_out("Q", qT[:], scale=float(P) ** -0.5)
                split_slot(L1, GP, act, g, 2)
                copy_out("K", kT[:])
                split_slot(L1, GP, act, g, 3)
                u = GP.unit["LG"]
                act.wait_ge(L1.unit_done, units(GP, g, u + 1))
                for t, (n0, w) in enumerate(NT):
                    last = nc.scalar.activation(L[:, n0:n0 + w], ps[GP.set[u]][:, t, 0:w], ACT.Identity,
                                                bias=vecT[:, ds(g + V_BG, 1)])
                last.then_inc(L1.evac[GP.set[u]], 1)
                act.wait_ge(L1.evac[GP.set[u]], evacs(GP, g, u))
                nc.scalar.activation(SZ[:], L[:], ACT.Abs).then_inc(chain_a, 1)
                act.wait_ge(chain_a, 1)
                nc.scalar.activation(SZ[:], SZ[:], ACT.Exp, scale=-1.0).then_inc(chain_a, 1)
                act.wait_ge(chain_a, 2)
                nc.scalar.activation(SZ[:], SZ[:], ACT.Ln, bias=1.0).then_inc(sp_ready, 1)
                copy_out("V0", vT[0])
                split_slot(L1, GP, act, g, 4)
                copy_out("V1", vT[1])
                split_slot(L1, GP, act, g, 5)
                copy_out("V2", vT[0])
                split_slot(L1, GP, act, g, 6)
                copy_out("V3", vT[1])
                split_slot(L1, GP, act, g, 7)
                act.wait_ge(lg_ready, g + 2)
                nc.scalar.activation(dec[:, 0:NSUP], L[:, SUP - 1:TP:SUP], ACT.Exp)
                nc.scalar.activation(dec[:, NSUP:NSUP + NB], L[:, TP + TS - 1:T:TS], ACT.Exp).then_inc(dec_ready, 1)
                nc.scalar.activation(qd_s[:], L[:, TP:T], ACT.Exp)
                nc.scalar.activation(ki_s[:], L[:, TP:T], ACT.Exp, scale=-1.0)
                act.wait_ge(smp_arg, g + 1)
                nc.scalar.activation(ks_s[:], ks_s[:], ACT.Exp).then_inc(smp_exp, 1)
                act.wait_ge(kp_zero, g + 1)

                def exps(s):
                    c0 = s * SUP
                    if s >= 1:
                        act.wait_ge(att_done, g * NSUP + s)
                    for b in range(4):
                        kw = {} if b == 0 else {"bias": L[:, c0 + CH * b - 1:c0 + CH * b]}
                        last = nc.scalar.activation(Kp[:, b, 0:CH * (b + 1)], L[:, c0:c0 + CH * (b + 1)], ACT.Exp,
                                                    scale=-1.0, **kw)
                    last.then_inc(kp_exp, 1)
                    act.wait_ge(qd_arg, g * NSUP + s + 1)
                    nc.scalar.activation(qd[:], qd[:], ACT.Exp).then_inc(qd_exp, 1)
                    if s >= 1:
                        act.wait_ge(kT_done, g * NSUP + s)
                    nc.scalar.activation(ks[:], L[:, c0:c0 + SUP], ACT.Exp, scale=-1.0,
                                         bias=L[:, c0 + SUP - 1:c0 + SUP]).then_inc(ks_exp, 1)

                def exp_qs(s):
                    if s >= 1:
                        act.wait_ge(o_done, g * NSUP + s)
                    nc.scalar.activation(qs[:], L[:, s * SUP:(s + 1) * SUP], ACT.Exp).then_inc(qs_exp, 1)

                def ksT_out(s):
                    act.wait_ge(kT_done, g * NSUP + s + 1)
                    if s >= 2:
                        act.wait_ge(upd_done, g * NSUP + s - 1)
                    nc.scalar.activation(ksT[:, s % 2, :], ps[1][:, 1, 0:P], ACT.Copy).then_inc(ksT_ready, 1)

                def o_out(s):
                    if s < NSUP:
                        act.wait_ge(o_done, g * NSUP + s + 1)
                        src, c = ps[1][:, 0, :], slice(s * SUP, (s + 1) * SUP)
                    else:
                        act.wait_ge(smp_o_done, g + 1)
                        src, c = X[1][:, 256:512], slice(TP, T)
                    if s >= 2:
                        act.wait_ge(oms_done, g * (NSUP + 1) + s - 1)
                    nc.scalar.activation(sqo[s % 2][:, 0:src.shape[1]], src, ACT.Square).then_inc(osq_ready, 1)
                    nc.scalar.activation(oT[:, :, c], src.rearrange("p (e t) -> p e t", e=KG), ACT.Copy)\
                        .then_inc(o_evac if s < NSUP else smp_o_evac, 1)

                def gate_in(i):
                    u = GP.unit[f"Z{i}"]
                    act.wait_ge(L1.unit_done, units(GP, g, u + 1))
                    if i == 3:
                        act.wait_ge(gated, g * KG + 1)
                    for t, (n0, w) in enumerate(NT):
                        last = nc.scalar.activation(szT[i][:, n0:n0 + w], ps[GP.set[u]][:, t, 0:w], ACT.Silu)
                    last.then_inc(L1.evac[GP.set[u]], 1)

                def high(i):
                    act.wait_ge(gated, g * KG + i + 1)
                    nc.scalar.activation(a_hi[:, i, :], oT[:, i, :], ACT.Copy).then_inc(gated_hi, 1)

                exps(0)
                exp_qs(0)
                act.wait_ge(smp_kT, g + 1)
                nc.scalar.activation(ksT_s[:], ps[1][0:NS, 1, 0:P], ACT.Copy).then_inc(smp_ksT, 1)
                ksT_out(0)
                for s in range(NSUP):
                    if s + 1 < NSUP:
                        exps(s + 1)
                        ksT_out(s + 1)
                    o_out(s)
                    if s + 1 < NSUP:
                        exp_qs(s + 1)
                    if s in (0, 4):
                        gate_in(s // 4)
                        split_slot(L1, GP, act, g, GP.slot["Z2"] + s // 4)
                gate_in(2)
                split_slot(L1, GP, act, g, GP.slot["O01"])
                o_out(NSUP)
                act.wait_ge(oms_done, (g + 1) * (NSUP + 1))
                nc.scalar.activation(rms_cols[:, 0:NSUP], X[1][:, 0:NSUP], ACT.Sqrt, bias=eps[:, 0:1],
                                     scale=1.0 / GW)
                nc.scalar.activation(rms_cols[0:NS, NSUP:NSUP + 1], X[1][0:NS, NSUP:NSUP + 1], ACT.Sqrt,
                                     bias=eps[0:NS, 0:1], scale=1.0 / GW).then_inc(orms_ready, 1)
                high(0)
                high(1)
                high(2)
                gate_in(3)
                split_slot(L1, GP, act, g, GP.slot["O23"])
                high(3)
                u = GP.unit["NRM"]
                act.wait_ge(L1.unit_done, units(GP, g, u + 1))
                for t, (n0, w) in enumerate(NT):
                    last = nc.scalar.activation(rms_row[:, n0:n0 + w], ps[GP.set[u]][:, t, 0:w], ACT.Copy)
                last.then_inc(L1.evac[GP.set[u]], 1)
                for j in range(GP.slot["O45"], GP.slots):
                    split_slot(L1, GP, act, g, j)
                act.sem_clear(chain_a)

            norm_squares(act, 2, (x_final, 2))
            for s in range(0, NSUP + 1, 2):
                n = P if s < NSUP else NS
                act.wait_ge(yT_done, s + 1)
                if s >= 4:
                    act.wait_ge(y_stored[s % 4], 16 * (s // 4))
                nc.scalar.activation(y_rows[0:n, s % 4, :], ps[s % 2][0:n, 0:2, :].rearrange("p a n -> p (a n)"),
                                     ACT.Copy).then_inc(y_evac[0], 1)

        @block.vector
        def _(dve):
            chain = [0]

            def link(ins):
                chain[0] += 1
                ins.then_inc(chain_v, 1)
                dve.wait_ge(chain_v, chain[0])

            def chain_restart():
                dve.wait_ge(chain_v, chain[0])
                dve.sem_clear(chain_v)
                chain[0] = 0

            dve.wait_ge(consts_ready, 1)
            dve.wait_ge(vec_ready, 1)
            def mod_part(part, m0, m1):
                dve.wait_ge(mod_done, part + 1)
                bias = vecT[:, V_ADAB + m0:V_ADAB + m1].unsqueeze(2).broadcast_to([P, m1 - m0, NC_])
                return nc.vector.tensor_tensor(mods[0][:, m0:m1, :],
                                               X[part][:, 0:(m1 - m0) * NC_].rearrange("p (m c) -> p m c", c=NC_),
                                               bias, ALU.add)

            rms_inverse(dve, 0)
            link(mod_part(0, 0, 16))
            mod_finish(dve, 0, mods[0])
            dve.wait_ge(mod_ready, 1)
            h_vector(dve, 0, mods[0])
            mod_part(1, 16, 24).then_inc(gate_ready, 1)
            dve.wait_ge(gate_ready, 1)
            dve.wait_ge(h_ready, 25)
            link(nc.vector.memset(G[:, 0:BUF], 0.0))
            chain_restart()
            dve.sem_inc(pooled, 1)

            with dve.Fori(0, NG) as g:
                chain[0] = 0

                def pool_tile(i):
                    u = PP.unit[f"U{i}"]
                    dve.wait_ge(L0.evac[PP.set[u]], evacs(PP, g, u))
                    link(nc.vector.tensor_tensor(s1[:, 1:WE], G[:, 1:WE], G[:, 0:WE - 1], ALU.add))
                    src, dst, have = s1, s2, 1
                    for k in range(3):
                        sh = 2 << k
                        lo = have + sh
                        link(nc.vector.scalar_tensor_tensor(
                            out=dst[:, lo:WE], in0=src[:, lo - sh:WE - sh],
                            scalar=win_on[:].rearrange("p g k -> p (g k)")[:, ds(g * 3 + k, 1)],
                            in1=src[:, lo:WE], op0=ALU.mult, op1=ALU.add))
                        src, dst, have = dst, src, lo
                    diff = s1[:, 0:T]
                    inv = win_inv[:, ds(g, 1)]
                    nc.vector.scalar_tensor_tensor(out=diff[:, 0:TP], in0=src[:, BUF:BUF + TP], scalar=inv,
                                                   in1=G[:, BUF:BUF + TP], op0=ALU.mult, op1=ALU.subtract)
                    seg = src[:, SE0:SE0 + NB * SEG].rearrange("p (b r) -> p b r", b=NB)[:, :, BUF:SEG]
                    useg = G[:, SE0:SE0 + NB * SEG].rearrange("p (b r) -> p b r", b=NB)[:, :, BUF:SEG]
                    link(nc.vector.scalar_tensor_tensor(out=diff[:, TP:T].rearrange("p (b t) -> p b t", b=NB), in0=seg,
                                                        scalar=inv, in1=useg, op0=ALU.mult, op1=ALU.subtract))
                    link(nc.vector.tensor_tensor(diff[:, 0:16], src[:, BUF:BUF + 16],
                                                 cnt_inv[:].rearrange("p g t -> p (g t)")[:, ds(g * 16, 16)], ALU.mult))
                    nc.vector.tensor_tensor(diff[:, 0:16], diff[:, 0:16], G[:, BUF:BUF + 16],
                                            ALU.subtract).then_inc(pooled, 1)
                    dve.wait_ge(pooled, g * KG + i + 2)
                    link(nc.vector.tensor_copy(a_hi[:, i, :], diff))
                    nc.vector.tensor_tensor(a_lo[:, i, :], diff, a_hi[:, i, :].bitcast(f32),
                                            ALU.subtract).then_inc(diff_ready, 1)
                    dve.wait_ge(diff_ready, g * KG + i + 1)

                for i in range(KG):
                    pool_tile(i)
                for m in range(KG):
                    u = PP.unit["G01"] + m
                    dve.wait_ge(L0.unit_done, units(PP, g, u + 1))
                    for t, (n0, w) in enumerate(NT):
                        last = nc.vector.tensor_scalar(oT[:, m, n0:n0 + w], ps[PP.set[u]][:, t, 0:w],
                                                       vecT[:, ds(g * KG + (V_PS + m), 1)], None, ALU.mult)
                    last.then_inc(L0.evac[PP.set[u]], 1)
                for i in range(KG):
                    if i == 0:
                        dve.wait_ge(L0.evac[PP.set[PP.unit["G23"] + 1]], evacs(PP, g, PP.unit["G23"] + 1))
                    gate_tile(dve, L0, PP, g, i, chain)
                for name in ("O01", "O23", "O45", "O67"):
                    add_branch(dve, L0, PP, g, name, mods[0], chain)
                chain_restart()

            dve.wait_ge(mini_free, 1 + 10 * NG)
            mod_finish(dve, 1, mods[1])
            dve.wait_ge(mod_ready, 2)
            link(nc.vector.memset(gs_tmp[:], 0.0))
            nc.vector.memset(gs_tmp[:], 0.0).then_inc(x_final, 1)
            rms_inverse(dve, 1)
            h_vector(dve, 1, mods[1])
            dve.sem_inc(lg_ready, 1)
            link(nc.vector.memset(G[NS:P, TP:T], 0.0))
            link(nc.vector.memset(att_s[:], 0.0))
            link(nc.vector.memset(att[:], 0.0))
            chain_restart()

            with dve.Fori(0, NG) as g:
                chain[0] = 0
                dve.wait_ge(sp_ready, g + 1)
                link(nc.vector.scalar_tensor_tensor(out=L[:], in0=L[:], scalar=0.0, in1=SZ[:], op0=ALU.min,
                                                    op1=ALU.subtract))
                link(nc.vector.tensor_scalar(L[:], L[:], 1.0 / 16.0, None, ALU.mult))
                for s in range(NSUP):
                    c = slice(s * SUP, (s + 1) * SUP)
                    nc.vector.tensor_tensor_scan(L[:, c], ones[:, 0:SUP], L[:, c], 0.0, ALU.mult, ALU.add)
                for b in range(NB):
                    c = slice(TP + b * TS, TP + (b + 1) * TS)
                    last = nc.vector.tensor_tensor_scan(L[:, c], ones[:, 0:TS], L[:, c], 0.0, ALU.mult, ALU.add)
                last.then_inc(lg_ready, 1)
                def v_rows(i):
                    u = GP.unit[f"VT{i}"]
                    dve.wait_ge(L1.unit_done, units(GP, g, u + 1))
                    for half in range(2):
                        nc.vector.tensor_copy(v[:, 4 * half:4 * half + 4, i * P:(i + 1) * P],
                                              ps[1][:, half, :].rearrange("p (s n) -> p s n", s=4))
                    nc.vector.tensor_copy(v[0:NS, NSUP, i * P:(i + 1) * P], ps[1][0:NS, 2, 0:P])\
                        .then_inc(L1.evac[1], 1)

                def qd_args(s):
                    c0 = s * SUP
                    if s >= 1:
                        dve.wait_ge(att_done, g * NSUP + s)
                    nc.vector.tensor_copy(qd[:, 0:CH], L[:, c0:c0 + CH])
                    nc.vector.tensor_tensor(qd[:, CH:SUP].rearrange("p (b t) -> p b t", b=3),
                                            L[:, c0 + CH:c0 + SUP].rearrange("p (b t) -> p b t", b=3),
                                            L[:, c0 + CH - 1:c0 + SUP - 1:CH].unsqueeze(2).broadcast_to([P, 3, CH]),
                                            ALU.subtract).then_inc(qd_arg, 1)

                def scale_qk(s):
                    c = slice(s * SUP, (s + 1) * SUP)
                    dve.wait_ge(qd_exp, g * NSUP + s + 1)
                    nc.vector.tensor_tensor(qd[:], qd[:], qT[:, c], ALU.mult).then_inc(qd_ready, 1)
                    dve.wait_ge(ks_exp, g * NSUP + s + 1)
                    nc.vector.tensor_tensor(ks[:], ks[:], kT[:, c], ALU.mult).then_inc(ks_ready, 1)

                def scale_qs(s):
                    dve.wait_ge(qs_exp, g * NSUP + s + 1)
                    nc.vector.tensor_tensor(qs[:], qs[:], qT[:, s * SUP:(s + 1) * SUP], ALU.mult).then_inc(qs_ready, 1)

                def att_out(s):
                    if s >= 2:
                        wait_apart(dve, o_done, g * NSUP + s - 1)
                    wait_apart(dve, att_done, g * NSUP + s + 1)
                    nc.vector.copy_predicated(att[:, s % 2, :], causal[:], X[0][:, 0:P])\
                        .then_inc(att_ready, 1)

                def state(s):
                    if s == 0:
                        dve.wait_ge(S_stored, g * 16 + 16)
                        dve.wait_ge(upd_done, g * NSUP + s + 1)
                        nc.vector.tensor_copy(S[:], ps[1][:, 2, :]).then_inc(S_ready, 1)
                    else:
                        dve.wait_ge(upd_done, g * NSUP + s + 1)
                        dve.wait_ge(S_ready, g * NSUP + s)
                        nc.vector.scalar_tensor_tensor(out=S[:], in0=S[:], scalar=dec[:, s:s + 1], in1=ps[1][:, 2, :],
                                                       op0=ALU.mult, op1=ALU.add).then_inc(S_ready, 1)

                def ks_rows(b):
                    if b >= 2:
                        dve.wait_ge(smp_upd, g * NB + b - 1)
                    nc.vector.tensor_scalar(ksm[:, b % 2, :], ksT_s[:], seq_rows[:, b:b + 1], None,
                                            ALU.mult).then_inc(ksm_ready, 1)

                def sample_state(b):
                    dve.wait_ge(smp_upd, g * NB + b + 1)
                    nc.vector.scalar_tensor_tensor(
                        out=v[:, b, :], in0=v[:, b, :], scalar=dec[:, NSUP + b:NSUP + b + 1], in1=ps[1][:, 2, :],
                        op0=ALU.mult, op1=ALU.add).then_inc(s0_ready, 1)

                def gate_product(i):
                    u = GP.unit[f"Z{i}"]
                    dve.wait_ge(L1.evac[0], evacs(GP, g, u))
                    nc.vector.scalar_tensor_tensor(out=oT[:, i, :], in0=oT[:, i, :],
                                                   scalar=vecT[:, ds(g * KG + (V_GN + i), 1)], in1=szT[i],
                                                   op0=ALU.mult, op1=ALU.mult).then_inc(gated, 1)

                def low(i):
                    for b in range(4):
                        if i == 0:
                            dve.wait_ge(s0_stored[b], g * 32 + 32)
                    if i >= 1:
                        for b in {1: (4,), 2: (5, 6), 3: (7,)}[i]:
                            dve.wait_ge(s0_stored[b % 4], g * 32 + 48)
                    dve.wait_ge(gated_hi, g * KG + i + 1)
                    nc.vector.tensor_tensor(a_lo[:, i, :], oT[:, i, :], a_hi[:, i, :].bitcast(f32),
                                            ALU.subtract).then_inc(L1.act_ready, 1)

                for i in range(3):
                    v_rows(i)
                dve.wait_ge(lg_ready, g + 2)
                l_end = L[:, TP + TS - 1:T:TS].unsqueeze(2).broadcast_to([P, NB, TS])
                nc.vector.tensor_tensor(ks_s[:].rearrange("p (b t) -> p b t", b=NB), l_end,
                                        L[:, TP:T].rearrange("p (b t) -> p b t", b=NB), ALU.subtract).then_inc(smp_arg, 1)
                qd_args(0)
                v_rows(3)
                dve.wait_ge(smp_exp, g + 1)
                nc.vector.tensor_tensor(qd_s[:], qd_s[:], qT[:, TP:T], ALU.mult)
                nc.vector.tensor_tensor(ki_s[:], ki_s[:], kT[:, TP:T], ALU.mult)
                nc.vector.tensor_tensor(ks_s[:], ks_s[:], kT[:, TP:T], ALU.mult).then_inc(smp_ready, 1)
                dve.wait_ge(dec_ready, g + 1)
                scale_qk(0)
                scale_qs(0)
                wait_apart(dve, smp_att, g + 1)
                nc.vector.copy_predicated(att_s[:], causal_s[:], X[0][0:NS, 0:NS]).then_inc(smp_attr, 1)
                att_out(0)
                dve.wait_ge(smp_ksT, g + 1)
                for s in range(NSUP + 2):
                    if s >= 2:
                        ks_rows(s - 2)
                    if s + 1 < NSUP:
                        qd_args(s + 1)
                        scale_qk(s + 1)
                        att_out(s + 1)
                    if s < NSUP:
                        state(s)
                    if s + 1 < NSUP:
                        scale_qs(s + 1)
                    if s >= 2:
                        sample_state(s - 2)
                dve.wait_ge(s0_ready, (g + 1) * NB)
                dve.wait_ge(o_evac, (g + 1) * NSUP)
                dve.sem_inc(L1.evac[1], 1)
                dve.wait_ge(smp_o_evac, g + 1)
                gate_product(0)
                gate_product(1)
                dve.wait_ge(orms_ready, g + 1)
                nc.vector.reciprocal(rms_cols[:, 0:NSUP], rms_cols[:, 0:NSUP])
                link(nc.vector.reciprocal(rms_cols[0:NS, NSUP:NSUP + 1], rms_cols[0:NS, NSUP:NSUP + 1]))
                nc.vector.tensor_tensor(rms_diag[:, 0:TP].rearrange("p (s t) -> p s t", s=NSUP),
                                        ident[:].unsqueeze(1).broadcast_to([P, NSUP, P]),
                                        rms_cols[:, 0:NSUP].unsqueeze(2).broadcast_to([P, NSUP, P]), ALU.mult)
                nc.vector.tensor_scalar(rms_diag[0:NS, TP:T], ident[0:NS, 0:NS], rms_cols[0:NS, NSUP:NSUP + 1], None,
                                        ALU.mult).then_inc(odiag_ready, 1)
                low(0)
                gate_product(2)
                low(1)
                low(2)
                gate_product(3)
                low(3)
                u = GP.unit["NRM"]
                dve.wait_ge(L1.evac[GP.set[u]], evacs(GP, g, u))
                for name in ("O01", "O23", "O45", "O67"):
                    add_head(dve, g, name, chain)
                link(nc.vector.memset(G[NS:P, TP:T], 0.0))
                chain_restart()

            nc.vector.memset(gs_tmp[:], 0.0).then_inc(x_final, 1)
            for t, (n0, w) in enumerate(NT):
                dve.wait_ge(std_ready, 6 + t + 1)
                nc.vector.reciprocal(rstd[:, n0:n0 + w], rstd[:, n0:n0 + w]).then_inc(rstd_ready, 1)
                dve.wait_ge(rstd_ready, 6 + t + 1)
                for k in range(KD):
                    last = nc.vector.scalar_tensor_tensor(out=xT[:, k, n0:n0 + w], in0=xT[:, k, n0:n0 + w],
                                                          scalar=vecT[:, V_FG + k:V_FG + k + 1], in1=rstd[:, n0:n0 + w],
                                                          op0=ALU.mult, op1=ALU.mult)
                last.then_inc(y_ready, 1)
            for s in range(1, NSUP, 2):
                dve.wait_ge(yT_done, s + 1)
                if s >= 4:
                    dve.wait_ge(y_stored[s % 4], 16 * (s // 4))
                nc.vector.tensor_copy(y_rows[:, s % 4, :], ps[s % 2][:, 0:2, :].rearrange("p a n -> p (a n)"))\
                    .then_inc(y_evac[1], 1)

        @block.tensor
        def _(pe):
            pe.wait_ge(consts_ready, 1)
            pe.wait_ge(c_loaded, 32)
            for k in range(KD):
                last = nc.tensor.transpose(X[0][:, k * NC_:(k + 1) * NC_], c_rows[:, k * P:(k + 1) * P],
                                           ident[0:NC_, 0:NC_])
            last.then_inc(cT_done, 1)
            pe.wait_ge(vec_loaded, 16 * 6)
            nc.tensor.transpose(X[1][:, 0:NVEC], vec_rows, ident[0:NVEC, 0:NVEC]).then_inc(vT_done, 1)
            for s in range(NSUP + 1):
                n = P if s < NSUP else NS
                pe.wait_ge(x_loaded[s], 16)
                if s >= 2:
                    pe.wait_ge(xT_ready, s - 1)
                for k in range(KD):
                    last = nc.tensor.transpose(ps[s % 2][:, k // 4, (k % 4) * P:(k % 4) * P + n],
                                               xrow[s][0:n, k * P:(k + 1) * P], ident[0:n, 0:n])
                last.then_inc(xT_done, 1)
            pe.wait_ge(cs_ready, 1)
            pe.wait_ge(vec_ready, 1)
            pe.wait_ge(xT_ready, NSUP + 1)
            norm_sums(pe, 0)
            for m in range(24):
                if m % 4 == 0:
                    pe.wait_ge(ada0_loaded[m // 4], 16)
                dst = X[0][:, m * NC_:(m + 1) * NC_] if m < 16 else X[1][:, (m - 16) * NC_:(m - 15) * NC_]
                for k in range(KD):
                    src = ada0[:, m // 4] if m < 16 else ada0_gate[:, m // 4 - 4]
                    last = nc.tensor.matmul(dst, src[:, k, (m % 4) * P:(m % 4 + 1) * P], csT[:, k, :],
                                            start=(k == 0), stop=(k == KD - 1))
                if m in (15, 23):
                    last.then_inc(mod_done, 1)
            h_wait(pe, 0)
            pe.wait_ge(gate_ready, 1)
            pe.sem_inc(L0.unit_done, 3)
            pe.sem_inc(mini_done, 1)
            pe.sem_inc(hist_T, 2)

            def start_sets(lay):
                pe.sem_inc(lay.evac[0], 1)
                pe.sem_inc(lay.evac[1], 1)

            start_sets(L0)
            with pe.Fori(0, NG) as g:
                def hist_mini(i):
                    pe.wait_ge(hist_evac, g * KG + i + 1)
                    pe.wait_ge(hist_loaded[i % 2], g * 32 + (i // 2) * 16 + 16)
                    nc.tensor.transpose(X[0][:, 0:NB * BUF], hist[:, i % 2, :], ident[0:NB * BUF, 0:NB * BUF])\
                        .then_inc(hist_T, 1)

                def ada_mini(a, mini):
                    pe.wait_ge(mini_free, g * 10 + mini + 1)
                    pe.wait_ge(ada_loaded, g * 96 + a * 16 + 16)
                    for k in range(KD):
                        last = nc.tensor.matmul(X[1][:, 0:NC_], ada_stage[:, k, :], csT[:, k, :], start=(k == 0),
                                                stop=(k == KD - 1))
                    last.then_inc(mini_done, 1)

                def tail_mini(i):
                    u = PP.unit[f"U{i}"]
                    pe.wait_ge(L0.evac[PP.set[u]], evacs(PP, g, u))
                    pe.wait_ge(mini_free, g * 10 + (1 + i) + 1)
                    nc.tensor.transpose(X[1][0:NS + BUF, 0:P], tail[:], ident[:]).then_inc(mini_done, 1)

                for name in PP.names:
                    if name[0] == "U":
                        hist_mini(int(name[1]))
                    if name[0] in "UZ":
                        project(pe, L0, PP, g, name)
                    elif name[0] == "G":
                        project_inner(pe, L0, PP, g, name, diff_ready)
                    else:
                        project_inner(pe, L0, PP, g, name, L0.act_ready)
                    j = PP.slot[name]
                    if j == 0:
                        ada_mini(0, 0)
                    if 1 <= j <= 4:
                        tail_mini(j - 1)
                    if 5 <= j <= 9:
                        ada_mini(j - 4, j)

            norm_sums(pe, 1)
            h_wait(pe, 1)
            pe.sem_inc(L1.unit_done, 3)
            pe.wait_ge(wgl_lo, 1)
            for k in range(KD):
                for pas, (w, a) in enumerate(((w_gl_hi, h_hi), (w_gl_hi, h_lo), (w_gl_lo, h_hi))):
                    for t, (n0, width) in enumerate(NT):
                        last = nc.tensor.matmul(ps[0][0:RANK, t, 0:width], w[:, k, :], a[:, k, n0:n0 + width],
                                                start=(k == 0 and pas == 0), stop=(k == KD - 1 and pas == 2))
            last.then_inc(gl_done, 1)
            pe.wait_ge(gl_ready, 1)
            start_sets(L1)
            with pe.Fori(0, NG) as g:
                def v_transpose(i):
                    u = GP.unit[f"VT{i}"]
                    src = GP.unit[f"V{i}"]
                    set_ready(pe, L1, GP, g, u)
                    pe.wait_ge(L1.evac[GP.set[src]], evacs(GP, g, src))
                    for s in range(NSUP + 1):
                        n = P if s < NSUP else NS
                        last = nc.tensor.transpose(ps[GP.set[u]][0:n, s // 4, (s % 4) * P:(s % 4 + 1) * P],
                                                   vT[i % 2][:, s * P:s * P + n], ident[:])
                    last.then_inc(L1.unit_done, 1)

                def log_decay():
                    u = GP.unit["LG"]
                    set_ready(pe, L1, GP, g, u)
                    pe.wait_ge(wup_loaded, g * 48 + 48)
                    for t, (n0, width) in enumerate(NT):
                        last = nc.tensor.matmul(ps[GP.set[u]][:, t, 0:width], w_up[32 * t:32 * t + RANK, :],
                                                glT[32 * t:32 * t + RANK, 0:width],
                                                start=True, stop=True)
                    last.then_inc(L1.unit_done, 1)

                filled = [0]

                def fill(n):
                    for f in range(filled[0], filled[0] + n):
                        name, k = f"Z{f // KD}", f % KD
                        u = GP.unit[name]
                        if k == 0:
                            set_ready(pe, L1, GP, g, u)
                            slot_ready(pe, L1, GP, g, name)
                        last = product_step(GP.slot[name] % 2, GP.set[u], k, KD, w8, h_hi, h_lo)
                        if k == KD - 1:
                            last.then_inc(L1.unit_done, 1)
                    filled[0] += n

                def scores(s):
                    pe.wait_ge(kp_ready, g * NSUP + s + 1)
                    pe.wait_ge(qd_ready, g * NSUP + s + 1)
                    if s >= 1:
                        pe.wait_ge(att_ready, g * NSUP + s)
                    else:
                        pe.wait_ge(smp_attr, g + 1)
                    for b in range(4):
                        last = nc.tensor.matmul(X[0][:, b * CH:(b + 1) * CH], Kp[:, b, :], qd[:, b * CH:(b + 1) * CH],
                                                start=True, stop=True)
                    last.then_inc(att_done, 1)

                def key_rows(s):
                    pe.wait_ge(ks_ready, g * NSUP + s + 1)
                    if s >= 1:
                        pe.wait_ge(ksT_ready, g * NSUP + s)
                    else:
                        pe.wait_ge(smp_ksT, g + 1)
                    nc.tensor.transpose(ps[1][:, 1, 0:P], ks[:], ident[:]).then_inc(kT_done, 1)

                def output(s):
                    pe.wait_ge(att_ready, g * NSUP + s + 1)
                    if s >= 1:
                        pe.wait_ge(o_evac, g * NSUP + s)
                    for e in range(KG):
                        last = nc.tensor.matmul(ps[1][:, 0, e * P:(e + 1) * P], v[:, s, e * P:(e + 1) * P],
                                                att[:, s % 2, :], start=(e == 0), stop=(s == 0 and e == KG - 1),
                                                skip_group_check=True)
                    if s:
                        pe.wait_ge(S_ready, g * NSUP + s)
                    pe.wait_ge(qs_ready, g * NSUP + s + 1)
                    if s:
                        for e in range(KG):
                            last = nc.tensor.matmul(ps[1][:, 0, e * P:(e + 1) * P], S[:, e * P:(e + 1) * P],
                                                    qs[:], start=False, stop=(e == KG - 1), skip_group_check=True)
                    last.then_inc(o_done, 1)

                def update(s):
                    pe.wait_ge(ksT_ready, g * NSUP + s + 1)
                    if s >= 3:
                        pe.wait_ge(s0_ready, g * NB + s - 2)
                    nc.tensor.matmul(ps[1][:, 2, :], ksT[:, s % 2, :], v[:, s, :], start=True,
                                     stop=True).then_inc(upd_done, 1)

                def sample_scores():
                    set_ready(pe, L1, GP, g, GP.unit["ATT"])
                    pe.wait_ge(smp_ready, g + 1)
                    nc.tensor.matmul(X[0][0:NS, 0:NS], ki_s[:], qd_s[:], start=True, stop=True).then_inc(smp_att, 1)
                    nc.tensor.transpose(ps[1][0:NS, 1, 0:P], ks_s[:], ident[:]).then_inc(smp_kT, 1)

                def sample_intra():
                    pe.wait_ge(smp_attr, g + 1)
                    for e in range(KG):
                        nc.tensor.matmul(X[1][:, 256 + e * NS:256 + (e + 1) * NS], v[0:NS, NSUP, e * P:(e + 1) * P],
                                         att_s[:], start=(e == 0), stop=False, skip_group_check=True)

                def sample(b):
                    pe.wait_ge(s0_loaded[b % 4], g * 32 + (b // 4) * 16 + 16)
                    for e in range(KG):
                        c = 256 + e * NS + b * TS
                        last = nc.tensor.matmul(X[1][:, c:c + TS], v[:, b, e * P:(e + 1) * P],
                                                qd_s[:, b * TS:(b + 1) * TS], start=False,
                                                stop=(b == NB - 1 and e == KG - 1), skip_group_check=True)
                    if b == NB - 1:
                        last.then_inc(smp_o_done, 1)
                    pe.wait_ge(ksm_ready, g * NB + b + 1)
                    if b + 2 < NSUP:
                        pe.wait_ge(S_ready, g * NSUP + b + 3)
                    else:
                        pe.wait_ge(s0_ready, g * NB + b)
                    nc.tensor.matmul(ps[1][:, 2, :], ksm[:, b % 2, :], v[0:NS, NSUP, :], start=True,
                                     stop=True).then_inc(smp_upd, 1)

                def mean_square(s):
                    n = P if s < NSUP else NS
                    pe.wait_ge(osum_ready, g * (NSUP + 1) + s + 1)
                    nc.tensor.matmul(X[1][0:n, s:s + 1], sqo[s % 2][:, 0:n], ones[:, 0:1], start=False,
                                     stop=True, skip_group_check=True).then_inc(oms_done, 1)

                for name in ("Q", "K"):
                    project(pe, L1, GP, g, name)
                log_decay()
                project(pe, L1, GP, g, "V0")
                project(pe, L1, GP, g, "V1")
                v_transpose(0)
                project(pe, L1, GP, g, "V2")
                v_transpose(1)
                project(pe, L1, GP, g, "V3")
                v_transpose(2)
                fill(FILL_START - 3)
                v_transpose(3)
                fill(1)
                sample_scores()
                fill(1)
                scores(0)
                key_rows(0)
                sample_intra()
                fill(1)
                for s in range(NSUP + 2):
                    if s <= NSUP:
                        fill(1)
                    if s + 1 < NSUP:
                        scores(s + 1)
                        key_rows(s + 1)
                    if s <= NSUP:
                        fill(FILL_STEP - 1)
                    if s < NSUP:
                        output(s)
                        update(s)
                    if 1 <= s <= NSUP:
                        mean_square(s - 1)
                    if s >= 2:
                        sample(s - 2)
                pe.sem_inc(L1.unit_done, 1)
                u = GP.unit["Z3"]
                set_ready(pe, L1, GP, g, u)
                slot_ready(pe, L1, GP, g, "Z3")
                for k in range(KD):
                    last = product_step(GP.slot["Z3"] % 2, GP.set[u], k, KD, w8, h_hi, h_lo)
                    if k == 1:
                        pe.wait_ge(smp_o_evac, g + 1)
                        mean_square(NSUP)
                last.then_inc(L1.unit_done, 1)
                u = GP.unit["NRM"]
                set_ready(pe, L1, GP, g, u)
                pe.wait_ge(odiag_ready, g + 1)
                for t, (n0, width) in enumerate(NT):
                    last = nc.tensor.matmul(ps[GP.set[u]][:, t, 0:width], ones[:], rms_diag[:, n0:n0 + width],
                                            start=True, stop=True)
                last.then_inc(L1.unit_done, 1)
                for name in ("O01", "O23", "O45", "O67"):
                    project_inner(pe, L1, GP, g, name, L1.act_ready)

            norm_sums(pe, 2)
            for s in range(NSUP + 1):
                n = P if s < NSUP else NS
                hi = s * P + n
                pe.wait_ge(y_ready, 1 if hi <= NT[0][1] else 2 if hi <= NT[2][0] else 3)
                if s == 1 or s == 0:
                    pe.wait_ge(std_ready, 9)
                if s >= 2:
                    pe.wait_ge(y_evac[s % 2], s // 2)
                for k in range(KD):
                    last = nc.tensor.transpose(ps[s % 2][0:n, k // 4, (k % 4) * P:(k % 4 + 1) * P],
                                               xT[:, k, s * P:s * P + n], ident[:])
                last.then_inc(yT_done, 1)


_INS = ["x_prompt", "x_sample", "c_prompt", "c_sample", "state_pool", "state_gla", "ada_w", "ada_b", "norm_g",
        "pool_w_in", "pool_w_grp", "pool_scale", "pool_w_out", "gla_w_in", "gla_w_gate_up", "gla_b_gate",
        "gla_norm_g", "gla_w_out", "final_g"]
_OUTS = [("y_prompt", (1, TP, D)), ("y_sample", (NB, TS, D)), ("new_pool_prompt", (1, 1, BUF, DI)),
         ("new_gla_prompt", (1, 1, NG, P, GW)), ("new_pool_sample", (1, NB, BUF, DI)),
         ("new_gla_sample", (1, NB, NG, P, GW))]


def kernel(**inputs):
    import numpy as _np
    import concourse.bacc as _bacc
    from concourse import mybir as _mybir
    from concourse.bass_utils import run_bass_kernel_spmd as _run

    nc = _bacc.Bacc("TRN2", target_bir_lowering=False, num_devices=1)
    arrays, args = {}, []
    for name in _INS:
        a = _np.ascontiguousarray(inputs[name])
        arrays[f"in_{name}"] = a
        args.append(nc.dram_tensor(f"in_{name}", a.shape, _mybir.dt.from_np(a.dtype), kind="ExternalInput").ap())
    for name, shape in _OUTS:
        args.append(nc.dram_tensor(f"out_{name}", shape, _mybir.dt.float32, kind="ExternalOutput").ap())
    trunk(nc, *args)
    r = _run(nc, [arrays], core_ids=[0])
    return tuple(r.results[0][f"out_{name}"] for name, _ in _OUTS)
```

```python
import concourse.bass as bass
from concourse import mybir
from contextlib import ExitStack

P = 128
D = 1024
DI = 2048
KD = D // P
NG = 4
GW = DI // NG
KG = GW // P
TP = 1024
NB = 8
TS = 8
NS = NB * TS
T = TP + NS
BUF = 15
SEG = BUF + TS
WE = BUF + TP + NB * SEG
SE0 = BUF + TP
RANK = 16
CH = 32
SUP = 4 * CH
NSUP = TP // SUP
EPS = 1e-6
NC_ = 1 + NB
NT = [(0, 364), (364, 362), (726, 362)]
N2P = TP - NT[2][0]
V_ADAB, V_NG, V_PS, V_BG, V_GN, V_FG = 0, 48, 64, 80, 84, 100
NVEC = 108

POOL_PLAN = [("U0", 1, "0"), ("U1", 1, "1"), ("U2", 1, "0"), ("U3", 1, "1"), ("Z0", 1, "0"),
             ("G01", 1, "10"), ("G23", 1, "10"), ("Z1", 1, "1"), ("Z2", 1, "0"), ("Z3", 1, "1"),
             ("O01", 1, "01"), ("O23", 1, "01"), ("O45", 1, "01"), ("O67", 1, "01")]
GLA_PLAN = [("Q", 1, "0"), ("K", 1, "1"), ("LG", 0, "0"), ("V0", 1, "1"), ("V1", 1, "0"), ("VT0", 0, "1"),
            ("V2", 1, "0"), ("VT1", 0, "1"), ("V3", 1, "0"), ("VT2", 0, "1"), ("VT3", 0, "1"),
            ("Z0", 1, "0"), ("Z1", 1, "0"), ("Z2", 1, "0"), ("ATT", 0, "1"), ("Z3", 1, "0"), ("NRM", 0, "1"),
            ("O01", 1, "01"), ("O23", 1, "01"), ("O45", 1, "01"), ("O67", 1, "01")]
FILL_START, FILL_STEP = 7, 2
MINIS = 11


class Plan:

    def __init__(self, rows):
        self.unit, self.slot, self.names, self.after = {}, {}, [], []
        self.set, self.place, self.in_set = [], [], [0, 0]
        for name, slots, sets in rows:
            self.unit[name] = len(self.set)
            for c in sets:
                self.set.append(int(c))
                self.place.append(self.in_set[int(c)])
                self.in_set[int(c)] += 1
            if slots:
                self.slot[name] = len(self.names)
                self.names.append(name)
                self.after.append(len(self.set))
        self.units, self.slots = len(self.set), len(self.names)


def trunk(nc, x_prompt, x_sample, c_prompt, c_sample, state_pool, state_gla, ada_w, ada_b, norm_g,
          pool_w_in, pool_w_grp, pool_scale, pool_w_out, gla_w_in, gla_w_gate_up, gla_b_gate,
          gla_norm_g, gla_w_out, final_g, y_prompt, y_sample, new_pool_prompt, new_gla_prompt,
          new_pool_sample, new_gla_sample):
    f32, f32r, i8 = mybir.dt.float32, mybir.dt.float32r, mybir.dt.int8
    ACT, ALU = mybir.ActivationFunctionType, mybir.AluOpType
    ds = bass.ds
    PP, GP = Plan(POOL_PLAN), Plan(GLA_PLAN)
    ctx = ExitStack()
    with ctx:
        def sb(name, shape, dt=f32, stack=ctx):
            return stack.enter_context(nc.sbuf_tensor(name, shape, dt))

        ident = sb("ident", [P, P])
        ones = sb("ones", [P, P])
        causal = sb("causal", [P, P], i8)
        causal_s = sb("causal_s", [NS, NS], i8)
        seq_rows = sb("seq_rows", [NS, NB])
        vecT = sb("vecT", [P, NVEC])
        csT = sb("csT", [P, KD, NC_])
        mods = [sb("mod0", [P, 24, NC_]), sb("mod1", [P, 24, NC_])]
        win_on = sb("win_on", [P, NG, 3])
        win_inv = sb("win_inv", [P, NG])
        cnt_inv = sb("cnt_inv", [P, NG, 16])
        eps = sb("eps", [P, 1])
        gs_tmp = sb("gs_tmp", [P, NS])
        xT = sb("xT", [P, KD, T])
        oT = sb("oT", [P, KG, T])
        stage = sb("stage", [P, 2, 1024])
        w_hi = sb("w_hi", [P, 2, 1024], f32r)
        w_lo = sb("w_lo", [P, 2, 1024], f32r)
        G = sb("G", [P, WE + 1])
        PQ = sb("PQ", [P, 2568])
        SZ = sb("SZ", [P, T])
        early = ExitStack()
        ada_stage = sb("ada_stage", [P, KD, P], stack=early)
        hist = sb("hist", [NB * BUF, 2, P], stack=early)
        tail_out = sb("tail_out", [NS + BUF, 2, P], stack=early)
        tail = sb("tail", [P, NS + BUF], stack=early)
        mod_row = sb("mod_row", [NC_, P], stack=early)
        early.close()
        low_rank = ExitStack()
        w_gl = sb("w_gl", [P, KD, RANK], stack=low_rank)
        w_gl_hi = sb("w_gl_hi", [P, KD, RANK], f32r, stack=low_rank)
        w_gl_lo = sb("w_gl_lo", [P, KD, RANK], f32r, stack=low_rank)
        low_rank.close()
        S = sb("S", [P, GW])
        qd = sb("qd", [P, SUP])
        qs = sb("qs", [P, SUP])
        ks = sb("ks", [P, SUP])
        ksT = sb("ksT", [P, 2, P])
        att = sb("att", [P, 2, SUP])
        att_s = sb("att_s", [NS, NS])
        ksm = sb("ksm", [NS, 2, P])
        dec = sb("dec", [P, NSUP + NB])
        rms_cols = sb("rms_cols", [P, NSUP + 1])
        w_up = sb("w_up", [P, P])
        start = ExitStack()
        ada0_parts = sb("ada0", [P, 4, KG * T], stack=start)
        ada0 = [ada0_parts[:, i, 0:KD * 512].rearrange("p (k n) -> p k n", k=KD) for i in (0, 2, 1, 3)]
        start.close()
        end = ExitStack()
        y_rows = sb("y_rows", [P, NSUP + 1, D], stack=end)
        g_rows = sb("g_rows", [P, D], stack=end)
        squares = sb("squares", [P, D], stack=end)
        y_sum = sb("y_sum", [P, NSUP + 1], stack=end)
        y_rms = sb("y_rms", [P, NSUP + 1], stack=end)
        end.close()
        h_hi = sb("h_hi", [P, KD, T], f32r)
        h_lo = sb("h_lo", [P, KD, T], f32r)
        heads = ExitStack()
        qT = sb("qT", [P, T], stack=heads)
        kT = sb("kT", [P, T], stack=heads)
        L = sb("L", [P, T], stack=heads)
        Kp = sb("Kp", [P, 4, SUP], stack=heads)
        qd_s = sb("qd_s", [P, NS], stack=heads)
        ki_s = sb("ki_s", [P, NS], stack=heads)
        ks_s = sb("ks_s", [P, NS], stack=heads)
        ksT_s = sb("ksT_s", [NS, P], stack=heads)
        v = sb("v", [P, NSUP + 1, GW], stack=heads)
        heads.close()
        start = ExitStack()
        ada0_gate = sb("ada0_gate", [P, 2, KD, 512], stack=start)
        start.close()
        between = ExitStack()
        sq_all = sb("sq_all", [P, KD, T], stack=between)
        between.close()
        a_hi = sb("a_hi", [P, KG, T], f32r)
        a_lo = sb("a_lo", [P, KG, T], f32r)

        s1 = PQ[:, 0:WE]
        s2 = PQ[:, 1300:1300 + WE]
        vT = [PQ[:, 0:T], PQ[:, T:2 * T]]
        szT = [PQ[:, 0:T], PQ[:, T:2 * T], SZ[:], PQ[:, 0:T]]
        scaled = [SZ[:], PQ[:, T:2 * T]]
        sqo = [G[:, i * GW:(i + 1) * GW] for i in range(2)]
        rms_diag = G[:, 0:T]
        rms_row = G[:, 0:T]
        sqx = [PQ[:, i * 364:(i + 1) * 364] for i in range(4)]
        ht = [PQ[:, (4 + i) * 364:(5 + i) * 364] for i in range(2)]
        hto = [PQ[:, 6 * 364:7 * 364], G[:, KD * NS:KD * NS + 364]]
        hs = G[:, 0:KD * NS].rearrange("p (k t) -> p k t", k=KD)
        xrow = [G[:, 0:D], PQ[:, 0:D], PQ[:, 1300:1300 + D], SZ[:, 0:D], stage[:, 0, :]] + \
               [oT[:, i, 0:D] for i in range(KG)]
        rstd = SZ
        vec_rows = ada_stage[0:NVEC, 0, :]
        c_rows = stage[0:NC_, 1, :]
        mod_rows = oT[0:NC_].rearrange("p k t -> p (k t)")[:, 0:3 * D]
        glT = PQ[:, 2 * T:2 * T + NT[0][1]]

        psA = ctx.enter_context(nc.psum_tensor("psA", [P, 3, 512], f32))
        psB = ctx.enter_context(nc.psum_tensor("psB", [P, 3, 512], f32))
        ps = [psA, psB]
        psX = ctx.enter_context(nc.psum_tensor("psX", [P, 2, 512], f32))
        X = [psX[:, i, :] for i in range(2)]
        ps_y = [psA[:, 0:2, :], psB[:, 0:2, :], psX[:, :, :]]

        def sem(name):
            return ctx.enter_context(nc.semaphore(name))

        c_loaded, vec_loaded, consts_ready = sem("c_loaded"), sem("vec_loaded"), sem("consts_ready")
        x_loaded = [sem(f"x_loaded{i}") for i in range(NSUP + 1)]
        ada0_loaded = [sem(f"ada0_loaded{i}") for i in range(6)]
        cT_done, vT_done, cs_ready, vec_ready = sem("cT_done"), sem("vecT_done"), sem("cs_ready"), sem("vec_ready")
        xT_done, xT_ready = sem("xT_done"), sem("xT_ready")
        mod_done, mod_ready, gate_ready = sem("mod_done"), sem("mod_ready"), sem("gate_ready")
        mod_rows_done, mod_rows_out = sem("mod_rows_done"), sem("mod_rows_out")
        sq_last_ready = sem("sq_last_ready")
        sq_ready, ss_done, std_ready, rstd_ready = sem("sq_ready"), sem("ss_done"), sem("std_ready"), sem("rstd_ready")
        ht_ready, hhi_ready, h_ready, hs_ready, hshi_ready = (sem("ht_ready"), sem("hhi_ready"), sem("h_ready"),
                                                              sem("hs_ready"), sem("hshi_ready"))
        hfull_ready, h_odd_ready = sem("hfull_ready"), sem("h_odd_ready")
        x_final = sem("x_final")
        copied = sem("copied")
        chain_v, chain_a, chain_p = sem("chain_v"), sem("chain_a"), sem("chain_p")
        yT_done, y_root, y_inverse, y_evac = sem("yT_done"), sem("y_root"), sem("y_inverse"), sem("y_evac")
        y_sums, g_rows_loaded, y_stored = sem("y_sums"), sem("g_rows_loaded"), sem("y_stored")

        class Stream:

            def __init__(self, tag):
                self.w_loaded = [sem(f"{tag}_w_loaded{i}") for i in range(2)]
                self.hi_done = sem(f"{tag}_hi_done")
                self.lo_done = sem(f"{tag}_lo_done")
                self.unit_done = sem(f"{tag}_unit_done")
                self.evac = [sem(f"{tag}_evac{i}") for i in range(2)]
                self.act_ready = sem(f"{tag}_gated")

        L0, L1 = Stream("pool"), Stream("gla")
        ada_loaded, mini_done, mini_free = sem("ada_loaded"), sem("mini_done"), sem("mini_free")
        hist_loaded, hist_T, hist_evac = [sem("hist_loaded0"), sem("hist_loaded1")], sem("hist_T"), sem("hist_evac")
        pooled, diff_ready = sem("pooled"), sem("diff_ready")
        tail_stored = [sem("tail_stored0"), sem("tail_stored1")]
        wgl_loaded, wgl_hi, wgl_lo, gl_done, gl_ready = (sem("wgl_loaded"), sem("wgl_hi"), sem("wgl_lo"),
                                                          sem("gl_done"), sem("gl_ready"))
        wup_loaded, sp_ready, lg_ready = sem("wup_loaded"), sem("sp_ready"), sem("lg_ready")
        dec_ready = sem("dec_ready")
        kp_zero, kp_exp, kp_ready = sem("kp_zero"), sem("kp_exp"), sem("kp_ready")
        qd_arg, qd_exp, qd_ready = sem("qd_arg"), sem("qd_exp"), sem("qd_ready")
        qs_exp, qs_ready, ks_exp, ks_ready = sem("qs_exp"), sem("qs_ready"), sem("ks_exp"), sem("ks_ready")
        att_done, att_ready, o_done, o_evac = sem("att_done"), sem("att_ready"), sem("o_done"), sem("o_evac")
        kT_done, ksT_ready, upd_done, S_ready = sem("kT_done"), sem("ksT_ready"), sem("upd_done"), sem("S_ready")
        smp_arg, smp_exp, smp_ready = sem("smp_arg"), sem("smp_exp"), sem("smp_ready")
        smp_att, smp_attr, smp_kT, ksm_ready = sem("smp_att"), sem("smp_attr"), sem("smp_kT"), sem("ksm_ready")
        s0_loaded = [sem(f"s0_loaded{i}") for i in range(4)]
        s0_stored = [sem(f"s0_stored{i}") for i in range(4)]
        s0_ready, smp_upd = sem("s0_ready"), sem("smp_upd")
        S_stored = sem("S_stored")
        smp_o_done, smp_o_evac, smp_ksT = sem("smp_o_done"), sem("smp_o_evac"), sem("smp_ksT")
        osq_ready, osum_ready, oms_done, orms_ready, odiag_ready = (
            sem("osq_ready"), sem("osum_ready"), sem("oms_done"), sem("orms_ready"), sem("odiag_ready"))
        gated, gated_hi = sem("gated"), sem("gated_hi")

        def units(plan, g, n):
            return g * plan.units + n + 3

        def evacs(plan, g, u):
            return g * plan.in_set[plan.set[u]] + plan.place[u] + 2

        def token_parts():
            return [(0, 0, 0, 364), (1, 364, 0, 362), (2, 726, 0, N2P)]

        def wait_apart(eng, what, count):
            count = eng.to_reg(count)
            eng.wait_ge(vec_ready, 1)
            eng.wait_ge(what, count)

        def split_slot(lay, plan, eng, g, j):
            before = plan.after[j - 2] if j >= 2 else plan.after[j - 2] - plan.units
            eng.wait_ge(lay.unit_done, units(plan, g, before))
            eng.wait_ge(lay.w_loaded[j % 2], 16 * (plan.slots // 2) * g + 16 * (j // 2 + 1))
            nc.scalar.activation(w_hi[:, j % 2, :], stage[:, j % 2, :], ACT.Copy).then_inc(lay.hi_done, 1)

        def lo_slots(lay, plan, eng, g, j):
            eng.wait_ge(lay.hi_done, g * plan.slots + j + 1)
            nc.gpsimd.tensor_tensor(w_lo[:, j % 2, :], stage[:, j % 2, :], w_hi[:, j % 2, :].bitcast(f32),
                                    ALU.subtract).then_inc(lay.lo_done, 1)

        def slot_free(lay, plan, g, j, eng):
            wait_apart(eng, lay.lo_done, g * plan.slots + j + 1)

        def root(act, r, t):
            n0, w = NT[t]
            act.wait_ge(ss_done, 24 * r + 8 * t + 8)
            nc.scalar.activation(rstd[:, n0:n0 + w], ps[1][:, t, 0:w], ACT.Sqrt, bias=eps[:, 0:1],
                                 scale=1.0 / D).then_inc(std_ready, 1)

        def squares_first(act):
            act.wait_ge(xT_ready, NSUP + 1)
            i = 0
            for t, (n0, w) in enumerate(NT):
                for k in range(KD):
                    if i >= 4:
                        act.wait_ge(ss_done, i - 3)
                    nc.scalar.activation(sqx[i % 4][:, 0:w], xT[:, k, n0:n0 + w], ACT.Square).then_inc(sq_ready, 1)
                    i += 1
                    if t and k == 3:
                        root(act, 0, t - 1)
            root(act, 0, 2)

        def squares_between(act):
            act.wait_ge(x_final, 1)
            for t, (n0, w) in enumerate(NT[0:2]):
                for k in range(KD):
                    nc.scalar.activation(sq_all[:, k, n0:n0 + w], xT[:, k, n0:n0 + w], ACT.Square).then_inc(sq_ready, 1)

        def norm_sums(pe, r):
            i = 0
            for t, (n0, w) in enumerate(NT):
                for k in range(KD):
                    if r and t == 2:
                        pe.wait_ge(sq_last_ready, k + 1)
                    else:
                        pe.wait_ge(sq_ready, 24 * r + i + 1)
                    src = sq_all[:, k, n0:n0 + w] if r else sqx[i % 4][:, 0:w]
                    nc.tensor.matmul(ps[1][:, t, 0:w], ones[:], src, start=(k == 0),
                                     stop=(k == KD - 1)).then_inc(ss_done, 1)
                    i += 1

        def rms_inverse(dve, r, t):
            n0, w = NT[t]
            dve.wait_ge(std_ready, 3 * r + t + 1)
            nc.vector.reciprocal(rstd[:, n0:n0 + w], rstd[:, n0:n0 + w]).then_inc(rstd_ready, 1)
            dve.wait_ge(rstd_ready, 3 * r + t + 1)

        h_order = ([(t, k) for half in range(2) for t in range(3) for k in range(4 * half, 4 * half + 4)],
                   [(t, k) for t in range(3) for k in range(KD)])

        def h_vector(dve, r, mod, before):
            def low(i):
                t, k = h_order[r][i]
                n0, w = token_parts()[t][1], token_parts()[t][3]
                dve.wait_ge(hhi_ready, 24 * r + i + 1)
                nc.vector.scalar_tensor_tensor(
                    out=h_lo[:, k, n0:n0 + w], in0=ht[(i // 2) % 2][:, 0:w], scalar=mod[:, k, 0:1],
                    in1=h_hi[:, k, n0:n0 + w].bitcast(f32), op0=ALU.add, op1=ALU.subtract).then_inc(h_ready, 1)

            def scaled_x(i):
                t, k = h_order[r][i]
                n0, w = token_parts()[t][1], token_parts()[t][3]
                if i >= 4:
                    dve.wait_ge(*((h_odd_ready, 12 * r + i // 2 - 1) if k % 2 else (h_ready, 13 * r + i // 2 - 1)))
                nc.vector.scalar_tensor_tensor(
                    out=(hto if k % 2 else ht)[(i // 2) % 2][:, 0:w], in0=xT[:, k, n0:n0 + w],
                    scalar=mod[:, 8 + k, 0:1], in1=rstd[:, n0:n0 + w], op0=ALU.mult, op1=ALU.mult).then_inc(ht_ready, 1)

            for i in range(0, 24, 2):
                if i in before:
                    before[i]()
                if i == 16:
                    a_s = mod[:, 8:16, 1:NC_].unsqueeze(3).broadcast_to([P, KD, NB, TS])
                    sh_s = mod[:, 0:8, 1:NC_].unsqueeze(3).broadcast_to([P, KD, NB, TS])
                    r_s = rstd[:, TP:T].rearrange("p (b t) -> p b t", b=NB).unsqueeze(1).broadcast_to([P, KD, NB, TS])
                    x_s = xT[:, :, TP:T].rearrange("p k (b t) -> p k b t", b=NB)
                    h4 = hs.rearrange("p k (b t) -> p k b t", b=NB)
                    nc.vector.tensor_tensor(h4, x_s, r_s, ALU.mult).then_inc(hs_ready, 1)
                    dve.wait_ge(hs_ready, 3 * r + 1)
                    nc.vector.tensor_tensor(h4, h4, a_s, ALU.mult).then_inc(hs_ready, 1)
                    dve.wait_ge(hs_ready, 3 * r + 2)
                    nc.vector.tensor_tensor(h4, h4, sh_s, ALU.add).then_inc(hs_ready, 1)
                scaled_x(i)
                scaled_x(i + 1)
                if i:
                    low(i - 2)
            low(22)
            dve.wait_ge(hshi_ready, r + 1)
            nc.vector.tensor_tensor(h_lo[:, :, TP:T], hs, h_hi[:, :, TP:T].bitcast(f32),
                                    ALU.subtract).then_inc(h_ready, 1)

        def h_pool(pool, r):
            for i in range(1, 24, 2):
                t, k = h_order[r][i]
                n0, w = token_parts()[t][1], token_parts()[t][3]
                pool.wait_ge(hfull_ready, 12 * r + i // 2 + 1)
                nc.gpsimd.tensor_tensor(h_lo[:, k, n0:n0 + w], hto[(i // 2) % 2][:, 0:w],
                                        h_hi[:, k, n0:n0 + w].bitcast(f32), ALU.subtract).then_inc(h_odd_ready, 1)

        def h_scalar(act, r, mod, before):
            for i, (t, k) in enumerate(h_order[r]):
                n0, w = token_parts()[t][1], token_parts()[t][3]
                if i in before:
                    before[i]()
                act.wait_ge(ht_ready, 24 * r + i + 1)
                src = (hto if k % 2 else ht)[(i // 2) % 2][:, 0:w]
                nc.scalar.activation(h_hi[:, k, n0:n0 + w], src, ACT.Identity,
                                     bias=mod[:, k, 0:1]).then_inc(hhi_ready, 1)
                if k % 2:
                    act.wait_ge(hhi_ready, 24 * r + i + 1)
                    nc.scalar.activation(src, src, ACT.Identity, bias=mod[:, k, 0:1]).then_inc(hfull_ready, 1)
            act.wait_ge(hs_ready, 3 * r + 3)
            nc.scalar.activation(h_hi[:, :, TP:T], hs, ACT.Copy).then_inc(hshi_ready, 1)

        def mod_finish(dve, r, mod, k0, k1):
            g_b = vecT[:, V_NG + 8 * r + k0:V_NG + 8 * r + k1].unsqueeze(2).broadcast_to([P, k1 - k0, NC_])
            nc.vector.scalar_tensor_tensor(out=mod[:, 8 + k0:8 + k1, :], in0=mod[:, 8 + k0:8 + k1, :], scalar=1.0,
                                           in1=g_b, op0=ALU.add, op1=ALU.mult).then_inc(mod_ready, 1)

        def h_wait(pe, r):
            pe.wait_ge(h_ready, 13 * (r + 1))
            pe.wait_ge(h_odd_ready, 12 * (r + 1))

        def product_step(p, u, k, kt, weight, act_hi, act_lo):
            for pas, (w, a) in enumerate(((w_hi, act_hi), (w_hi, act_lo), (w_lo, act_hi))):
                for t, (n0, width) in enumerate(NT):
                    last = nc.tensor.matmul(ps[u][:, t, 0:width], weight(w[:, p, :], k), a[:, k, n0:n0 + width],
                                            start=(k == 0 and pas == 0), stop=(k == kt - 1 and pas == 2))
            return last

        def product(pe, p, u, kt, weight, act_hi, act_lo, before_k=None):
            for k in range(kt):
                if before_k:
                    before_k(k)
                last = product_step(p, u, k, kt, weight, act_hi, act_lo)
            return last

        def w8(w, k):
            return w[:, k * P:(k + 1) * P]

        def w4(half):
            return lambda w, k: w[:, k * 256 + half * P:k * 256 + half * P + P]

        def slot_ready(pe, lay, plan, g, name):
            pe.wait_ge(lay.lo_done, g * plan.slots + plan.slot[name] + 3)

        def set_ready(pe, lay, plan, g, u):
            pe.wait_ge(lay.evac[plan.set[u]], g * plan.in_set[plan.set[u]] + plan.place[u] + 1)

        def project(pe, lay, plan, g, name):
            u = plan.unit[name]
            set_ready(pe, lay, plan, g, u)
            slot_ready(pe, lay, plan, g, name)
            product(pe, plan.slot[name] % 2, plan.set[u], KD, w8, h_hi, h_lo).then_inc(lay.unit_done, 1)

        def project_inner(pe, lay, plan, g, name, ready):
            for half in range(2):
                u = plan.unit[name] + half
                set_ready(pe, lay, plan, g, u)
                if half == 0:
                    slot_ready(pe, lay, plan, g, name)
                product(pe, plan.slot[name] % 2, plan.set[u], KG, w4(half), a_hi, a_lo,
                        before_k=lambda k: pe.wait_ge(ready, g * KG + k + 1)).then_inc(lay.unit_done, 1)

        def add_branch(dve, lay, plan, g, name, mod, chain):
            for half in range(2):
                m = int(name[1]) + half
                u = plan.unit[name] + half
                src = ps[plan.set[u]]
                dve.wait_ge(lay.unit_done, units(plan, g, u + 1))
                nc.vector.tensor_tensor(gs_tmp[:].rearrange("p (b t) -> p b t", b=NB),
                                        src[:, 2, N2P:N2P + NS].rearrange("p (b t) -> p b t", b=NB),
                                        mod[:, 16 + m, 1:NC_].unsqueeze(2).broadcast_to([P, NB, TS]),
                                        ALU.mult).then_inc(chain_v, 1)
                chain[0] += 1
                for t, n0, _, w in token_parts():
                    last = nc.vector.scalar_tensor_tensor(
                        out=xT[:, m, n0:n0 + w], in0=src[:, t, 0:w], scalar=mod[:, 16 + m, 0:1],
                        in1=xT[:, m, n0:n0 + w], op0=ALU.mult, op1=ALU.add)
                last.then_inc(lay.evac[plan.set[u]], 1)
                dve.wait_ge(chain_v, chain[0])
                nc.vector.tensor_tensor(xT[:, m, TP:T], xT[:, m, TP:T], gs_tmp[:], ALU.add).then_inc(chain_v, 1)
                chain[0] += 1
                dve.wait_ge(chain_v, chain[0])

        def gate_tile(dve, lay, plan, g, i, chain):
            u = plan.unit[f"Z{i}"]
            dve.wait_ge(lay.evac[plan.set[u]], evacs(plan, g, u))
            nc.vector.tensor_tensor(oT[:, i, :], oT[:, i, :], SZ[:], ALU.mult).then_inc(chain_v, 1)
            chain[0] += 1
            dve.wait_ge(chain_v, chain[0])
            nc.vector.tensor_copy(a_hi[:, i, :], oT[:, i, :]).then_inc(chain_v, 1)
            chain[0] += 1
            dve.wait_ge(chain_v, chain[0])
            nc.vector.tensor_tensor(a_lo[:, i, :], oT[:, i, :], a_hi[:, i, :].bitcast(f32),
                                    ALU.subtract).then_inc(lay.act_ready, 1)
            dve.wait_ge(lay.act_ready, g * KG + i + 1)

        def add_head(dve, g, name, chain):
            for half in range(2):
                m = int(name[1]) + half
                u = GP.unit[name] + half
                src, row = ps[GP.set[u]], scaled[half]
                dve.wait_ge(L1.unit_done, units(GP, g, u + 1))
                nc.vector.tensor_tensor(row[:, TP:T].rearrange("p (b t) -> p b t", b=NB),
                                        src[:, 2, N2P:N2P + NS].rearrange("p (b t) -> p b t", b=NB),
                                        mods[1][:, 16 + m, 1:NC_].unsqueeze(2).broadcast_to([P, NB, TS]),
                                        ALU.mult).then_inc(chain_v, 1)
                chain[0] += 1
                for t, n0, _, w in token_parts():
                    last = nc.vector.scalar_tensor_tensor(
                        out=row[:, n0:n0 + w], in0=src[:, t, 0:w], scalar=mods[1][:, 16 + m, 0:1],
                        in1=rms_row[:, n0:n0 + w], op0=ALU.mult, op1=ALU.mult)
                dve.wait_ge(chain_v, chain[0])
                nc.vector.tensor_tensor(row[:, TP:T], row[:, TP:T], rms_row[:, TP:T], ALU.mult).then_inc(chain_v, 1)
                chain[0] += 1
                dve.wait_ge(chain_v, chain[0])
                nc.vector.tensor_tensor(xT[:, m, :], xT[:, m, :], row, ALU.add).then_inc(L1.evac[GP.set[u]], 1)
                dve.wait_ge(L1.evac[GP.set[u]], evacs(GP, g, u))

        def silu_out(act, lay, plan, g, i):
            u = plan.unit[f"Z{i}"]
            act.wait_ge(lay.unit_done, units(plan, g, u + 1))
            if i:
                act.wait_ge(lay.act_ready, g * KG + i)
            for t, (n0, w) in enumerate(NT):
                last = nc.scalar.activation(SZ[:, n0:n0 + w], ps[plan.set[u]][:, t, 0:w], ACT.Silu)
            last.then_inc(lay.evac[plan.set[u]], 1)

        w_in0 = pool_w_in[0].rearrange("(k p) n -> p k n", p=P)
        w_in1 = gla_w_in[0].rearrange("(k p) n -> p k n", p=P)
        w_out0 = pool_w_out[0].rearrange("(q p) n -> p q n", p=P)
        w_out1 = gla_w_out[0].rearrange("(q p) n -> p q n", p=P)
        w_grp = pool_w_grp[0].rearrange("g (k p) n -> p (g k) n", p=P)
        ada_v = [ada_w[i].rearrange("(k p) n -> p k n", p=P) for i in range(2)]
        hist_v = state_pool[0].rearrange("b r n -> (b r) n")

        block = ctx.enter_context(nc.Block())

        @block.sync
        def _(sp):
            sp.dma_start(c_rows[0:1, :], c_prompt).then_inc(c_loaded, 16)
            sp.dma_start(c_rows[1:NC_, :], c_sample).then_inc(c_loaded, 16)
            for lo, src in ((V_ADAB, ada_b.rearrange("l (m p) -> (l m) p", p=P)),
                            (V_NG, norm_g.rearrange("l (m p) -> (l m) p", p=P)),
                            (V_PS, pool_scale[0].rearrange("(m p) -> m p", p=P)),
                            (V_BG, gla_b_gate[0].rearrange("(m p) -> m p", p=P)),
                            (V_GN, gla_norm_g[0].rearrange("(m p) -> m p", p=P)),
                            (V_FG, final_g.rearrange("(m p) -> m p", p=P))):
                sp.dma_start(vec_rows[lo:lo + src.shape[0], :], src).then_inc(vec_loaded, 16)
            for s in range(NSUP + 1):
                n = P if s < NSUP else NS
                src = x_prompt[0, s * P:(s + 1) * P, :] if s < NSUP else x_sample.rearrange("b t n -> (b t) n")
                sp.dma_start(xrow[s][0:n, :], src).then_inc(x_loaded[s], 16)
            for i, q in enumerate((0, 2, 1, 3, 4, 5)):
                dst = ada0[i] if i < 4 else ada0_gate[:, i - 4, :, :]
                sp.dma_start(dst, ada_v[0][:, :, q * 512:(q + 1) * 512]).then_inc(ada0_loaded[i], 16)
            sp.dma_start(new_pool_sample[0, :, 0:BUF - TS, :], state_pool[0, :, TS:BUF, :]).then_inc(copied, 16)

            with sp.Fori(0, NG) as g:
                def load(j):
                    slot_free(L0, PP, g, j, sp)
                    name = PP.names[j]
                    i = int(name[1])
                    dst = stage[:, j % 2, :]
                    if name[0] in "UZ":
                        src = w_in0[:, :, ds(g * GW + (DI if name[0] == "Z" else 0) + i * P, P)]
                        dst = dst.rearrange("p (k n) -> p k n", k=KD)
                    else:
                        src = (w_grp if name[0] == "G" else w_out0)[:, ds(g * KG, KG), i * P:(i + 2) * P]
                        dst = dst.rearrange("p (k n) -> p k n", k=KG)
                    sp.dma_start(dst, src).then_inc(L0.w_loaded[j % 2], 16)

                def load_ada(a, minis):
                    wait_apart(sp, mini_done, g * MINIS + minis + 1)
                    sp.dma_start(ada_stage[:], ada_v[1][:, :, ds(g * 6 * P + a * P, P)]).then_inc(ada_loaded, 16)

                def load_hist(i):
                    wait_apart(sp, hist_T, g * KG + i + 1)
                    sp.dma_start(hist[:, i % 2, :], hist_v[:, ds(g * GW + i * P, P)]).then_inc(hist_loaded[i % 2], 16)

                load_ada(0, 0)
                load_hist(0)
                load_hist(1)
                for j in range(PP.slots):
                    load(j)
                    if j in (2, 3):
                        load_hist(j)
                    if j == 3:
                        load_ada(1, 1)
                    if 8 <= j <= 11:
                        load_ada(j - 6, j - 2)

            sp.wait_ge(sq_ready, 25)
            sp.dma_start(w_gl[:], w_in1[:, :, 2 * 512 + 2 * DI:2 * 512 + 2 * DI + RANK]).then_inc(wgl_loaded, 16)
            for i in range(4):
                sp.sem_inc(s0_stored[i], 16)
            sp.sem_inc(S_stored, 16)
            with sp.Fori(0, NG) as g:
                wait_apart(sp, lg_ready, g + 1)
                for t in range(3):
                    sp.dma_start(w_up[32 * t:32 * t + RANK, :], gla_w_gate_up[0][:, ds(g * P, P)])\
                        .then_inc(wup_loaded, 16)

                def load_state(b):
                    wait_apart(sp, upd_done, g * NSUP + b + 1)
                    sp.dma_start(v[:, b, :], state_gla[0, b, ds(g, 1), :, :].rearrange("a p n -> p (a n)"))\
                        .then_inc(s0_loaded[b % 4], 16)

                def store_state(b):
                    wait_apart(sp, s0_ready, g * NB + b + 1)
                    wait_apart(sp, s0_stored[b % 4], g * 32 + (b // 4) * 16 + 16)
                    sp.dma_start(new_gla_sample[0, b, ds(g, 1), :, :].rearrange("a p n -> p (a n)"), v[:, b, :])\
                        .then_inc(s0_stored[b % 4], 16)

                def load(j):
                    slot_free(L1, GP, g, j, sp)
                    name = GP.names[j]
                    dst = stage[:, j % 2, :]
                    if name[0] == "O":
                        i = int(name[1])
                        src = w_out1[:, ds(g * KG, KG), i * P:(i + 2) * P]
                        dst = dst.rearrange("p (k n) -> p k n", k=KG)
                    else:
                        col = {"Q": g * P, "K": g * P + 512}.get(name)
                        if col is None:
                            col = g * GW + 1024 + (DI if name[0] == "Z" else 0) + int(name[1]) * P
                        src = w_in1[:, :, ds(col, P)]
                        dst = dst.rearrange("p (k n) -> p k n", k=KD)
                    sp.dma_start(dst, src).then_inc(L1.w_loaded[j % 2], 16)

                for j in range(GP.slot["Z3"] + 1):
                    load(j)
                for s in range(NSUP + 2):
                    if s < NSUP:
                        load_state(s)
                    if s == 3:
                        load(GP.slot["O01"])
                    if s == 7:
                        load(GP.slot["O23"])
                    if s == NSUP:
                        wait_apart(sp, S_ready, (g + 1) * NSUP)
                        sp.dma_start(new_gla_prompt[0, 0, ds(g, 1), :, :].rearrange("a p n -> p (a n)"), S[:])\
                            .then_inc(S_stored, 16)
                    if s >= 2:
                        store_state(s - 2)
                for j in range(GP.slot["O45"], GP.slots):
                    load(j)

            sp.wait_ge(L1.act_ready, KG * NG)
            sp.dma_start(g_rows[:], final_g.unsqueeze(0).broadcast_to([P, D])).then_inc(g_rows_loaded, 16)
            for i in range(4):
                sp.wait_ge(s0_stored[i], 16 * (1 + 2 * NG))
            sp.wait_ge(S_stored, 16 * (1 + NG))

            for s in range(NSUP + 1):
                n = P if s < NSUP else NS
                sp.wait_ge(y_evac, s + 1)
                dst = y_prompt[0, s * P:(s + 1) * P, :] if s < NSUP else y_sample.rearrange("b t n -> (b t) n")
                sp.dma_start(dst, y_rows[0:n, s, :]).then_inc(y_stored, 16)
            sp.wait_ge(y_stored, 16 * (NSUP + 1))
            sp.wait_ge(copied, 16)

        @block.gpsimd
        def _(pool):
            n = 0

            def link(ins):
                nonlocal n
                n += 1
                ins.then_inc(chain_p, 1)
                pool.wait_ge(chain_p, n)

            link(pool.memset(ident[:], 0.0))
            link(pool.affine_select(out=ident[:], in_=ident[:], compare_op=ALU.not_equal, fill=1.0, base=0,
                                    pattern=[[-1, P]], channel_multiplier=1))
            link(pool.memset(ones[:], 1.0))
            link(pool.memset(causal[:], 1))
            link(pool.affine_select(out=causal[:], in_=causal[:], compare_op=ALU.is_ge, fill=0, base=0,
                                    pattern=[[1, P]], channel_multiplier=-1))
            link(pool.memset(seq_rows[:], 1.0))
            link(pool.affine_select(out=seq_rows[:], in_=seq_rows[:], compare_op=ALU.is_ge, fill=0.0, base=0,
                                    pattern=[[-TS, NB]], channel_multiplier=1))
            link(pool.affine_select(out=seq_rows[:], in_=seq_rows[:], compare_op=ALU.is_ge, fill=0.0, base=TS - 1,
                                    pattern=[[TS, NB]], channel_multiplier=-1))
            cs3 = causal_s[:].rearrange("p (b t) -> p b t", b=NB)
            link(pool.memset(causal_s[:], 1))
            link(pool.affine_select(out=cs3, in_=cs3, compare_op=ALU.is_ge, fill=0, base=0,
                                    pattern=[[-TS, NB], [0, TS]], channel_multiplier=1))
            link(pool.affine_select(out=cs3, in_=cs3, compare_op=ALU.is_ge, fill=0, base=0,
                                    pattern=[[TS, NB], [1, TS]], channel_multiplier=-1))
            link(pool.memset(win_on[:], 0.0))
            for k in range(3):
                link(pool.memset(win_on[:, k + 1:NG, k:k + 1], 1.0))
            for g in range(NG):
                w = 2 << g
                link(pool.memset(win_inv[:, g:g + 1], 1.0 / w))
                link(pool.memset(cnt_inv[:, g, :], 1.0 / w))
                for t in range(w - 1):
                    link(pool.memset(cnt_inv[:, g, t:t + 1], 1.0 / (t + 1)))
            link(pool.memset(eps[:], EPS))
            pool.memset(gs_tmp[:], 0.0).then_inc(consts_ready, 1)

            pool.wait_ge(xT_done, NSUP + 1)
            pool.sem_inc(L0.lo_done, 2)
            h_pool(pool, 0)
            with pool.Fori(0, NG) as g:
                for j in range(PP.slots):
                    lo_slots(L0, PP, pool, g, j)

            n0, w = NT[2]
            pool.wait_ge(x_final, 1)
            for k in range(KD):
                pool.tensor_tensor(sq_all[:, k, n0:n0 + w], xT[:, k, n0:n0 + w], xT[:, k, n0:n0 + w],
                                   ALU.mult).then_inc(sq_last_ready, 1)
            pool.wait_ge(wgl_hi, 1)
            pool.tensor_tensor(w_gl_lo[:], w_gl[:], w_gl_hi[:].bitcast(f32), ALU.subtract).then_inc(wgl_lo, 1)
            pool.sem_inc(L1.lo_done, 2)
            h_pool(pool, 1)
            pool.sem_clear(chain_p)
            with pool.Fori(0, NG) as g:
                for j in range(GP.slot["Z1"] + 1):
                    lo_slots(L1, GP, pool, g, j)
                wait_apart(pool, L1.unit_done, units(GP, g, GP.unit["V0"] + 1))
                pool.memset(Kp[:], 0.0).then_inc(kp_zero, 1)

                def scale_kp(s):
                    pool.wait_ge(kp_exp, g * NSUP + s + 1)
                    for b in range(4):
                        last = pool.tensor_tensor(Kp[:, b, 0:CH * (b + 1)], Kp[:, b, 0:CH * (b + 1)],
                                                  kT[:, s * SUP:s * SUP + CH * (b + 1)], ALU.mult)
                    last.then_inc(kp_ready, 1)

                def square_sum(s):
                    n = P if s < NSUP else NS
                    q = sqo[s % 2]
                    pool.wait_ge(osq_ready, g * (NSUP + 1) + s + 1)
                    pool.tensor_tensor(q[:, 0:2 * n], q[:, 0:2 * n], q[:, 2 * n:4 * n], ALU.add).then_inc(chain_p, 1)
                    pool.wait_ge(chain_p, s + 1)
                    pool.tensor_tensor(q[:, 0:n], q[:, 0:n], q[:, n:2 * n], ALU.add).then_inc(osum_ready, 1)

                scale_kp(0)
                scale_kp(1)
                for s in range(NSUP + 1):
                    if s + 2 < NSUP:
                        scale_kp(s + 2)
                    if s == 1:
                        lo_slots(L1, GP, pool, g, GP.slot["Z2"])
                    if s == 5:
                        lo_slots(L1, GP, pool, g, GP.slot["Z3"])
                    if s == NSUP:
                        lo_slots(L1, GP, pool, g, GP.slot["O01"])
                    square_sum(s)
                for j in range(GP.slot["O23"], GP.slots):
                    lo_slots(L1, GP, pool, g, j)
                pool.sem_clear(chain_p)

        @block.scalar
        def _(act):
            act.wait_ge(cT_done, 1)
            nc.scalar.activation(csT[:].rearrange("p k c -> p (k c)"), X[0][:, 0:KD * NC_], ACT.Silu).then_inc(cs_ready, 1)
            act.wait_ge(vT_done, 1)
            nc.scalar.activation(vecT[:], X[1][:, 0:NVEC], ACT.Copy).then_inc(vec_ready, 1)
            for s in range(NSUP + 1):
                n = P if s < NSUP else NS
                act.wait_ge(xT_done, s + 1)
                nc.scalar.activation(xT[:, :, s * P:s * P + n],
                                     ps[s % 2][:, 0:2, :].rearrange("p a (k t) -> p (a k) t", k=4)[:, :, 0:n],
                                     ACT.Copy).then_inc(xT_ready, 1)
            squares_first(act)
            def rows_out(i):
                act.wait_ge(mod_rows_done, i + 1)
                nc.scalar.activation(mod_rows[:, i * 512:(i + 1) * 512], X[i % 2][0:NC_, :], ACT.Copy)\
                    .then_inc(mod_rows_out, 1)

            def upper_rows():
                rows_out(2)
                rows_out(3)
                act.wait_ge(mod_ready, 2)

            rows_out(0)
            rows_out(1)
            act.wait_ge(mod_ready, 1)
            h_scalar(act, 0, mods[0], {12: upper_rows, 20: lambda: rows_out(4)})
            rows_out(5)
            act.sem_inc(mini_free, 1)
            act.sem_inc(hist_evac, 1)
            act.sem_inc(tail_stored[0], 32)
            act.sem_inc(tail_stored[1], 32)

            with act.Fori(0, NG) as g:
                def u_out(i):
                    u = PP.unit[f"U{i}"]
                    act.wait_ge(L0.unit_done, units(PP, g, u + 1))
                    act.wait_ge(pooled, g * KG + i + 1)
                    act.wait_ge(hist_T, g * KG + i + 3)
                    seg = G[:, SE0:SE0 + NB * SEG].rearrange("p (b r) -> p b r", b=NB)
                    nc.scalar.activation(seg[:, :, 0:BUF], X[0][:, 0:NB * BUF].rearrange("p (b r) -> p b r", b=NB),
                                         ACT.Copy).then_inc(hist_evac, 1)
                    for t, n0, _, w in token_parts():
                        nc.scalar.activation(G[:, BUF + n0:BUF + n0 + w], ps[PP.set[u]][:, t, 0:w], ACT.Copy)
                    smp = ps[PP.set[u]][:, 2, N2P:N2P + NS]
                    nc.scalar.activation(seg[:, :, BUF:SEG], smp.rearrange("p (b t) -> p b t", b=NB), ACT.Copy)
                    act.wait_ge(mini_done, g * MINIS + (1 + i) + 1)
                    nc.scalar.activation(tail[:, 0:NS], smp, ACT.Copy)
                    nc.scalar.activation(tail[:, NS:NS + BUF], ps[PP.set[u]][:, 2, N2P - BUF:N2P], ACT.Copy)\
                        .then_inc(L0.evac[PP.set[u]], 1)

                def ada_row(a, mini):
                    act.wait_ge(mini_done, g * MINIS + mini + 2)
                    if mini >= 6:
                        ada_out(a - 1)
                    nc.scalar.activation(mod_row[:], X[1][0:NC_, P:2 * P], ACT.Copy).then_inc(mini_free, 1)

                def ada_out(a):
                    return nc.scalar.activation(
                        mods[1][:].rearrange("p m c -> p (m c)")[:, ds(g * 6 * NC_ + a * NC_, NC_)],
                        X[1][:, 2 * P:2 * P + NC_], ACT.Identity, bias=vecT[:, ds(g * 6 + (V_ADAB + 24 + a), 1)])

                def tail_store(i):
                    act.wait_ge(mini_done, g * MINIS + (1 + i) + 2)
                    if i == 0:
                        ada_out(0)
                    act.wait_ge(tail_stored[i % 2], g * 64 + (i // 2) * 32 + 32)
                    nc.scalar.activation(tail_out[:, i % 2, :], X[1][0:NS + BUF, 0:P], ACT.Copy).then_inc(mini_free, 1)
                    act.wait_ge(mini_free, g * MINIS + (1 + i) + 2)
                    act.dma_start(new_pool_sample[0, :, BUF - TS:BUF, ds(g * GW + i * P, P)],
                                  tail_out[0:NS, i % 2, :]).then_inc(tail_stored[i % 2], 16)
                    act.dma_start(new_pool_prompt[0, 0, :, ds(g * GW + i * P, P)],
                                  tail_out[NS:NS + BUF, i % 2, :]).then_inc(tail_stored[i % 2], 16)

                split_slot(L0, PP, act, g, 0)
                split_slot(L0, PP, act, g, 1)
                def last_ada():
                    act.wait_ge(mini_done, g * MINIS + MINIS + 1)
                    ada_out(5).then_inc(mini_free, 1)

                extra = {0: lambda: ada_row(0, 0), 1: lambda: tail_store(0), 2: lambda: tail_store(1),
                         3: lambda: tail_store(2), 4: lambda: tail_store(3), 5: lambda: ada_row(1, 5),
                         6: lambda: ada_row(2, 6), 7: lambda: ada_row(3, 7), 8: lambda: ada_row(4, 8),
                         9: lambda: ada_row(5, 9), 10: last_ada}
                for j, name in enumerate(PP.names):
                    if name[0] == "U":
                        u_out(int(name[1]))
                    if name[0] == "Z":
                        silu_out(act, L0, PP, g, int(name[1]))
                    if j + 2 < PP.slots:
                        split_slot(L0, PP, act, g, j + 2)
                    if j in extra:
                        extra[j]()
            for i in range(2):
                act.wait_ge(tail_stored[i], 32 + 64 * NG)

            squares_between(act)
            root(act, 1, 0)
            act.wait_ge(wgl_loaded, 16)
            nc.scalar.activation(w_gl_hi[:], w_gl[:], ACT.Copy).then_inc(wgl_hi, 1)
            act.wait_ge(mod_ready, 3)
            h_scalar(act, 1, mods[1], {2: lambda: root(act, 1, 1), 10: lambda: root(act, 1, 2)})

            with act.Fori(0, NG) as g:
                def copy_out(name, dst, scale=1.0, wait=None):
                    u = GP.unit[name]
                    act.wait_ge(L1.unit_done, units(GP, g, u + 1))
                    if wait:
                        wait()
                    for t, (n0, w) in enumerate(NT):
                        last = nc.scalar.activation(dst[:, n0:n0 + w], ps[GP.set[u]][:, t, 0:w], ACT.Copy, scale=scale)
                    last.then_inc(L1.evac[GP.set[u]], 1)

                split_slot(L1, GP, act, g, 0)
                split_slot(L1, GP, act, g, 1)
                copy_out("Q", qT[:], scale=float(P) ** -0.5)
                split_slot(L1, GP, act, g, 2)
                copy_out("K", kT[:])
                split_slot(L1, GP, act, g, 3)
                u = GP.unit["LG"]
                act.wait_ge(L1.unit_done, units(GP, g, u + 1))
                for t, (n0, w) in enumerate(NT):
                    last = nc.scalar.activation(L[:, n0:n0 + w], ps[GP.set[u]][:, t, 0:w], ACT.Identity,
                                                bias=vecT[:, ds(g + V_BG, 1)])
                last.then_inc(L1.evac[GP.set[u]], 1)
                act.wait_ge(L1.evac[GP.set[u]], evacs(GP, g, u))
                nc.scalar.activation(SZ[:], L[:], ACT.Abs).then_inc(chain_a, 1)
                act.wait_ge(chain_a, 1)
                nc.scalar.activation(SZ[:], SZ[:], ACT.Exp, scale=-1.0).then_inc(chain_a, 1)
                act.wait_ge(chain_a, 2)
                nc.scalar.activation(SZ[:], SZ[:], ACT.Ln, bias=1.0).then_inc(sp_ready, 1)
                copy_out("V0", vT[0])
                split_slot(L1, GP, act, g, 4)
                copy_out("V1", vT[1])
                split_slot(L1, GP, act, g, 5)
                copy_out("V2", vT[0])
                split_slot(L1, GP, act, g, 6)
                copy_out("V3", vT[1])
                split_slot(L1, GP, act, g, 7)
                act.wait_ge(lg_ready, g + 2)
                nc.scalar.activation(dec[:, 0:NSUP], L[:, SUP - 1:TP:SUP], ACT.Exp)
                nc.scalar.activation(dec[:, NSUP:NSUP + NB], L[:, TP + TS - 1:T:TS], ACT.Exp).then_inc(dec_ready, 1)
                nc.scalar.activation(qd_s[:], L[:, TP:T], ACT.Exp)
                nc.scalar.activation(ki_s[:], L[:, TP:T], ACT.Exp, scale=-1.0)
                act.wait_ge(smp_arg, g + 1)
                nc.scalar.activation(ks_s[:], ks_s[:], ACT.Exp).then_inc(smp_exp, 1)
                act.wait_ge(kp_zero, g + 1)

                def exps(s):
                    c0 = s * SUP
                    if s >= 1:
                        act.wait_ge(att_done, g * NSUP + s)
                    for b in range(4):
                        kw = {} if b == 0 else {"bias": L[:, c0 + CH * b - 1:c0 + CH * b]}
                        last = nc.scalar.activation(Kp[:, b, 0:CH * (b + 1)], L[:, c0:c0 + CH * (b + 1)], ACT.Exp,
                                                    scale=-1.0, **kw)
                    last.then_inc(kp_exp, 1)
                    act.wait_ge(qd_arg, g * NSUP + s + 1)
                    nc.scalar.activation(qd[:], qd[:], ACT.Exp).then_inc(qd_exp, 1)
                    if s >= 1:
                        act.wait_ge(kT_done, g * NSUP + s)
                    nc.scalar.activation(ks[:], L[:, c0:c0 + SUP], ACT.Exp, scale=-1.0,
                                         bias=L[:, c0 + SUP - 1:c0 + SUP]).then_inc(ks_exp, 1)

                def exp_qs(s):
                    if s >= 1:
                        act.wait_ge(o_done, g * NSUP + s)
                    nc.scalar.activation(qs[:], L[:, s * SUP:(s + 1) * SUP], ACT.Exp).then_inc(qs_exp, 1)

                def ksT_out(s):
                    act.wait_ge(kT_done, g * NSUP + s + 1)
                    if s >= 2:
                        act.wait_ge(upd_done, g * NSUP + s - 1)
                    nc.scalar.activation(ksT[:, s % 2, :], ps[1][:, 1, 0:P], ACT.Copy).then_inc(ksT_ready, 1)

                def o_out(s):
                    if s < NSUP:
                        act.wait_ge(o_done, g * NSUP + s + 1)
                        src, c = ps[1][:, 0, :], slice(s * SUP, (s + 1) * SUP)
                    else:
                        act.wait_ge(smp_o_done, g + 1)
                        src, c = X[1][:, 256:512], slice(TP, T)
                    if s >= 2:
                        act.wait_ge(oms_done, g * (NSUP + 1) + s - 1)
                    nc.scalar.activation(sqo[s % 2][:, 0:src.shape[1]], src, ACT.Square).then_inc(osq_ready, 1)
                    nc.scalar.activation(oT[:, :, c], src.rearrange("p (e t) -> p e t", e=KG), ACT.Copy)\
                        .then_inc(o_evac if s < NSUP else smp_o_evac, 1)

                def gate_in(i):
                    u = GP.unit[f"Z{i}"]
                    act.wait_ge(L1.unit_done, units(GP, g, u + 1))
                    if i == 3:
                        act.wait_ge(gated, g * KG + 1)
                    for t, (n0, w) in enumerate(NT):
                        last = nc.scalar.activation(szT[i][:, n0:n0 + w], ps[GP.set[u]][:, t, 0:w], ACT.Silu)
                    last.then_inc(L1.evac[GP.set[u]], 1)

                def high(i):
                    act.wait_ge(gated, g * KG + i + 1)
                    nc.scalar.activation(a_hi[:, i, :], oT[:, i, :], ACT.Copy).then_inc(gated_hi, 1)

                exps(0)
                exp_qs(0)
                act.wait_ge(smp_kT, g + 1)
                nc.scalar.activation(ksT_s[:], ps[1][0:NS, 1, 0:P], ACT.Copy).then_inc(smp_ksT, 1)
                ksT_out(0)
                exps(1)
                for s in range(NSUP):
                    if s in (0, 4):
                        gate_in(s // 4)
                    if s + 1 < NSUP:
                        ksT_out(s + 1)
                    if s + 2 < NSUP:
                        exps(s + 2)
                    o_out(s)
                    if s + 1 < NSUP:
                        exp_qs(s + 1)
                    if s in (1, 5):
                        split_slot(L1, GP, act, g, GP.slot["Z2"] + s // 4)
                gate_in(2)
                split_slot(L1, GP, act, g, GP.slot["O01"])
                o_out(NSUP)
                act.wait_ge(oms_done, (g + 1) * (NSUP + 1))
                nc.scalar.activation(rms_cols[:, 0:NSUP], X[1][:, 0:NSUP], ACT.Sqrt, bias=eps[:, 0:1],
                                     scale=1.0 / GW)
                nc.scalar.activation(rms_cols[0:NS, NSUP:NSUP + 1], X[1][0:NS, NSUP:NSUP + 1], ACT.Sqrt,
                                     bias=eps[0:NS, 0:1], scale=1.0 / GW).then_inc(orms_ready, 1)
                high(0)
                high(1)
                high(2)
                gate_in(3)
                split_slot(L1, GP, act, g, GP.slot["O23"])
                high(3)
                u = GP.unit["NRM"]
                act.wait_ge(L1.unit_done, units(GP, g, u + 1))
                for t, (n0, w) in enumerate(NT):
                    last = nc.scalar.activation(rms_row[:, n0:n0 + w], ps[GP.set[u]][:, t, 0:w], ACT.Copy)
                last.then_inc(L1.evac[GP.set[u]], 1)
                for j in range(GP.slot["O45"], GP.slots):
                    split_slot(L1, GP, act, g, j)
                act.sem_clear(chain_a)

            for s in range(NSUP + 1):
                n = P if s < NSUP else NS
                act.wait_ge(yT_done, s + 1)
                if s:
                    act.wait_ge(y_sums, s)
                nc.scalar.activation(squares[0:n, :], ps_y[s % 3][0:n].rearrange("p a n -> p (a n)"), ACT.Square,
                                     accum_out=y_sum[0:n, s:s + 1]).then_inc(y_sums, 1)
                act.wait_ge(y_sums, s + 1)
                nc.scalar.activation(y_rms[0:n, s:s + 1], y_sum[0:n, s:s + 1], ACT.Sqrt, bias=eps[0:n, 0:1],
                                     scale=1.0 / D).then_inc(y_root, 1)

        @block.vector
        def _(dve):
            chain = [0]

            def link(ins):
                chain[0] += 1
                ins.then_inc(chain_v, 1)
                dve.wait_ge(chain_v, chain[0])

            def chain_restart():
                dve.wait_ge(chain_v, chain[0])
                dve.sem_clear(chain_v)
                chain[0] = 0

            dve.wait_ge(consts_ready, 1)
            dve.wait_ge(vec_ready, 1)
            def mod_part(part, half, m):
                bias = vecT[:, V_ADAB + m:V_ADAB + m + 4].unsqueeze(2).broadcast_to([P, 4, NC_])
                c = half * 4 * NC_
                return nc.vector.tensor_tensor(mods[0][:, m:m + 4, :],
                                               ps[0][:, part, c:c + 4 * NC_].rearrange("p (m c) -> p m c", c=NC_),
                                               bias, ALU.add)

            def shift_scale(part):
                dve.wait_ge(mod_done, part + 1)
                mod_part(part, 0, 4 * part)
                link(mod_part(part, 1, 8 + 4 * part))
                mod_finish(dve, 0, mods[0], 4 * part, 4 * part + 4)
                dve.wait_ge(mod_ready, part + 1)

            for t in range(3):
                rms_inverse(dve, 0, t)
            h_vector(dve, 0, mods[0], {0: lambda: shift_scale(0), 12: lambda: shift_scale(1)})
            dve.wait_ge(mod_done, 3)
            mod_part(2, 0, 16)
            mod_part(2, 1, 20).then_inc(gate_ready, 1)
            dve.wait_ge(gate_ready, 1)
            dve.wait_ge(h_ready, 13)
            link(nc.vector.memset(G[:, 0:BUF], 0.0))
            chain_restart()
            dve.sem_inc(pooled, 1)

            with dve.Fori(0, NG) as g:
                chain[0] = 0

                def pool_tile(i):
                    u = PP.unit[f"U{i}"]
                    dve.wait_ge(L0.evac[PP.set[u]], evacs(PP, g, u))
                    link(nc.vector.tensor_tensor(s1[:, 1:WE], G[:, 1:WE], G[:, 0:WE - 1], ALU.add))
                    src, dst, have = s1, s2, 1
                    for k in range(3):
                        sh = 2 << k
                        lo = have + sh
                        link(nc.vector.scalar_tensor_tensor(
                            out=dst[:, lo:WE], in0=src[:, lo - sh:WE - sh],
                            scalar=win_on[:].rearrange("p g k -> p (g k)")[:, ds(g * 3 + k, 1)],
                            in1=src[:, lo:WE], op0=ALU.mult, op1=ALU.add))
                        src, dst, have = dst, src, lo
                    diff = s1[:, 0:T]
                    inv = win_inv[:, ds(g, 1)]
                    nc.vector.scalar_tensor_tensor(out=diff[:, 0:TP], in0=src[:, BUF:BUF + TP], scalar=inv,
                                                   in1=G[:, BUF:BUF + TP], op0=ALU.mult, op1=ALU.subtract)
                    seg = src[:, SE0:SE0 + NB * SEG].rearrange("p (b r) -> p b r", b=NB)[:, :, BUF:SEG]
                    useg = G[:, SE0:SE0 + NB * SEG].rearrange("p (b r) -> p b r", b=NB)[:, :, BUF:SEG]
                    link(nc.vector.scalar_tensor_tensor(out=diff[:, TP:T].rearrange("p (b t) -> p b t", b=NB), in0=seg,
                                                        scalar=inv, in1=useg, op0=ALU.mult, op1=ALU.subtract))
                    link(nc.vector.tensor_tensor(diff[:, 0:16], src[:, BUF:BUF + 16],
                                                 cnt_inv[:].rearrange("p g t -> p (g t)")[:, ds(g * 16, 16)], ALU.mult))
                    nc.vector.tensor_tensor(diff[:, 0:16], diff[:, 0:16], G[:, BUF:BUF + 16],
                                            ALU.subtract).then_inc(pooled, 1)
                    dve.wait_ge(pooled, g * KG + i + 2)
                    link(nc.vector.tensor_copy(a_hi[:, i, :], diff))
                    nc.vector.tensor_tensor(a_lo[:, i, :], diff, a_hi[:, i, :].bitcast(f32),
                                            ALU.subtract).then_inc(diff_ready, 1)
                    dve.wait_ge(diff_ready, g * KG + i + 1)

                for i in range(KG):
                    pool_tile(i)
                for m in range(KG):
                    u = PP.unit["G01"] + m
                    dve.wait_ge(L0.unit_done, units(PP, g, u + 1))
                    for t, (n0, w) in enumerate(NT):
                        last = nc.vector.tensor_scalar(oT[:, m, n0:n0 + w], ps[PP.set[u]][:, t, 0:w],
                                                       vecT[:, ds(g * KG + (V_PS + m), 1)], None, ALU.mult)
                    last.then_inc(L0.evac[PP.set[u]], 1)
                for i in range(KG):
                    if i == 0:
                        dve.wait_ge(L0.evac[PP.set[PP.unit["G23"] + 1]], evacs(PP, g, PP.unit["G23"] + 1))
                    gate_tile(dve, L0, PP, g, i, chain)
                for name in ("O01", "O23", "O45", "O67"):
                    add_branch(dve, L0, PP, g, name, mods[0], chain)
                chain_restart()

            dve.wait_ge(mini_free, 1 + MINIS * NG)
            mod_finish(dve, 1, mods[1], 0, KD)
            dve.wait_ge(mod_ready, 3)
            link(nc.vector.memset(gs_tmp[:], 0.0))
            nc.vector.memset(gs_tmp[:], 0.0).then_inc(x_final, 1)
            dve.sem_inc(lg_ready, 1)
            h_vector(dve, 1, mods[1], {8 * t: (lambda t=t: rms_inverse(dve, 1, t)) for t in range(3)})
            dve.wait_ge(gl_done, 1)
            for t, (n0, w) in enumerate(NT):
                last = nc.vector.tensor_copy(glT[32 * t:32 * t + RANK, 0:w], ps[0][0:RANK, t, 0:w])
            last.then_inc(gl_ready, 1)
            link(nc.vector.memset(G[NS:P, TP:T], 0.0))
            link(nc.vector.memset(att_s[:], 0.0))
            link(nc.vector.memset(att[:], 0.0))
            chain_restart()

            with dve.Fori(0, NG) as g:
                chain[0] = 0
                dve.wait_ge(sp_ready, g + 1)
                link(nc.vector.scalar_tensor_tensor(out=L[:], in0=L[:], scalar=0.0, in1=SZ[:], op0=ALU.min,
                                                    op1=ALU.subtract))
                link(nc.vector.tensor_scalar(L[:], L[:], 1.0 / 16.0, None, ALU.mult))
                for s in range(NSUP):
                    c = slice(s * SUP, (s + 1) * SUP)
                    nc.vector.tensor_tensor_scan(L[:, c], ones[:, 0:SUP], L[:, c], 0.0, ALU.mult, ALU.add)
                for b in range(NB):
                    c = slice(TP + b * TS, TP + (b + 1) * TS)
                    last = nc.vector.tensor_tensor_scan(L[:, c], ones[:, 0:TS], L[:, c], 0.0, ALU.mult, ALU.add)
                last.then_inc(lg_ready, 1)
                def v_rows(i):
                    u = GP.unit[f"VT{i}"]
                    dve.wait_ge(L1.unit_done, units(GP, g, u + 1))
                    for half in range(2):
                        nc.vector.tensor_copy(v[:, 4 * half:4 * half + 4, i * P:(i + 1) * P],
                                              ps[1][:, half, :].rearrange("p (s n) -> p s n", s=4))
                    nc.vector.tensor_copy(v[0:NS, NSUP, i * P:(i + 1) * P], ps[1][0:NS, 2, 0:P])\
                        .then_inc(L1.evac[1], 1)

                def qd_args(s):
                    c0 = s * SUP
                    if s >= 1:
                        dve.wait_ge(att_done, g * NSUP + s)
                    nc.vector.tensor_copy(qd[:, 0:CH], L[:, c0:c0 + CH])
                    nc.vector.tensor_tensor(qd[:, CH:SUP].rearrange("p (b t) -> p b t", b=3),
                                            L[:, c0 + CH:c0 + SUP].rearrange("p (b t) -> p b t", b=3),
                                            L[:, c0 + CH - 1:c0 + SUP - 1:CH].unsqueeze(2).broadcast_to([P, 3, CH]),
                                            ALU.subtract).then_inc(qd_arg, 1)

                def scale_qk(s):
                    c = slice(s * SUP, (s + 1) * SUP)
                    dve.wait_ge(qd_exp, g * NSUP + s + 1)
                    nc.vector.tensor_tensor(qd[:], qd[:], qT[:, c], ALU.mult).then_inc(qd_ready, 1)
                    dve.wait_ge(ks_exp, g * NSUP + s + 1)
                    nc.vector.tensor_tensor(ks[:], ks[:], kT[:, c], ALU.mult).then_inc(ks_ready, 1)

                def scale_qs(s):
                    dve.wait_ge(qs_exp, g * NSUP + s + 1)
                    nc.vector.tensor_tensor(qs[:], qs[:], qT[:, s * SUP:(s + 1) * SUP], ALU.mult).then_inc(qs_ready, 1)

                def att_out(s):
                    if s >= 2:
                        wait_apart(dve, o_done, g * NSUP + s - 1)
                    wait_apart(dve, att_done, g * NSUP + s + 1)
                    nc.vector.copy_predicated(att[:, s % 2, :], causal[:], X[0][:, 0:P])\
                        .then_inc(att_ready, 1)

                def state(s):
                    if s == 0:
                        dve.wait_ge(S_stored, g * 16 + 16)
                        dve.wait_ge(upd_done, g * NSUP + s + 1)
                        nc.vector.tensor_copy(S[:], ps[1][:, 2, :]).then_inc(S_ready, 1)
                    else:
                        dve.wait_ge(upd_done, g * NSUP + s + 1)
                        dve.wait_ge(S_ready, g * NSUP + s)
                        nc.vector.scalar_tensor_tensor(out=S[:], in0=S[:], scalar=dec[:, s:s + 1], in1=ps[1][:, 2, :],
                                                       op0=ALU.mult, op1=ALU.add).then_inc(S_ready, 1)

                def ks_rows(b):
                    if b >= 2:
                        dve.wait_ge(smp_upd, g * NB + b - 1)
                    nc.vector.tensor_scalar(ksm[:, b % 2, :], ksT_s[:], seq_rows[:, b:b + 1], None,
                                            ALU.mult).then_inc(ksm_ready, 1)

                def sample_state(b):
                    dve.wait_ge(smp_upd, g * NB + b + 1)
                    nc.vector.scalar_tensor_tensor(
                        out=v[:, b, :], in0=v[:, b, :], scalar=dec[:, NSUP + b:NSUP + b + 1], in1=ps[1][:, 2, :],
                        op0=ALU.mult, op1=ALU.add).then_inc(s0_ready, 1)

                def gate_product(i):
                    u = GP.unit[f"Z{i}"]
                    dve.wait_ge(L1.evac[0], evacs(GP, g, u))
                    nc.vector.scalar_tensor_tensor(out=oT[:, i, :], in0=oT[:, i, :],
                                                   scalar=vecT[:, ds(g * KG + (V_GN + i), 1)], in1=szT[i],
                                                   op0=ALU.mult, op1=ALU.mult).then_inc(gated, 1)

                def low(i):
                    for b in range(4):
                        if i == 0:
                            dve.wait_ge(s0_stored[b], g * 32 + 32)
                    if i >= 1:
                        for b in {1: (4,), 2: (5, 6), 3: (7,)}[i]:
                            dve.wait_ge(s0_stored[b % 4], g * 32 + 48)
                    dve.wait_ge(gated_hi, g * KG + i + 1)
                    nc.vector.tensor_tensor(a_lo[:, i, :], oT[:, i, :], a_hi[:, i, :].bitcast(f32),
                                            ALU.subtract).then_inc(L1.act_ready, 1)

                for i in range(3):
                    v_rows(i)
                dve.wait_ge(lg_ready, g + 2)
                l_end = L[:, TP + TS - 1:T:TS].unsqueeze(2).broadcast_to([P, NB, TS])
                nc.vector.tensor_tensor(ks_s[:].rearrange("p (b t) -> p b t", b=NB), l_end,
                                        L[:, TP:T].rearrange("p (b t) -> p b t", b=NB), ALU.subtract).then_inc(smp_arg, 1)
                qd_args(0)
                v_rows(3)
                dve.wait_ge(smp_exp, g + 1)
                nc.vector.tensor_tensor(qd_s[:], qd_s[:], qT[:, TP:T], ALU.mult)
                nc.vector.tensor_tensor(ki_s[:], ki_s[:], kT[:, TP:T], ALU.mult)
                nc.vector.tensor_tensor(ks_s[:], ks_s[:], kT[:, TP:T], ALU.mult).then_inc(smp_ready, 1)
                dve.wait_ge(dec_ready, g + 1)
                scale_qk(0)
                scale_qs(0)
                wait_apart(dve, smp_att, g + 1)
                nc.vector.copy_predicated(att_s[:], causal_s[:], X[0][0:NS, 0:NS]).then_inc(smp_attr, 1)
                att_out(0)
                dve.wait_ge(smp_ksT, g + 1)
                qd_args(1)
                scale_qk(1)
                for s in range(NSUP + 2):
                    if s >= 2:
                        ks_rows(s - 2)
                    if s + 1 < NSUP:
                        att_out(s + 1)
                    if s + 2 < NSUP:
                        qd_args(s + 2)
                        scale_qk(s + 2)
                    if s < NSUP:
                        state(s)
                    if s + 1 < NSUP:
                        scale_qs(s + 1)
                    if s >= 2:
                        sample_state(s - 2)
                dve.wait_ge(s0_ready, (g + 1) * NB)
                dve.wait_ge(o_evac, (g + 1) * NSUP)
                dve.sem_inc(L1.evac[1], 1)
                dve.wait_ge(smp_o_evac, g + 1)
                gate_product(0)
                gate_product(1)
                dve.wait_ge(orms_ready, g + 1)
                nc.vector.reciprocal(rms_cols[:, 0:NSUP], rms_cols[:, 0:NSUP])
                link(nc.vector.reciprocal(rms_cols[0:NS, NSUP:NSUP + 1], rms_cols[0:NS, NSUP:NSUP + 1]))
                nc.vector.tensor_tensor(rms_diag[:, 0:TP].rearrange("p (s t) -> p s t", s=NSUP),
                                        ident[:].unsqueeze(1).broadcast_to([P, NSUP, P]),
                                        rms_cols[:, 0:NSUP].unsqueeze(2).broadcast_to([P, NSUP, P]), ALU.mult)
                nc.vector.tensor_scalar(rms_diag[0:NS, TP:T], ident[0:NS, 0:NS], rms_cols[0:NS, NSUP:NSUP + 1], None,
                                        ALU.mult).then_inc(odiag_ready, 1)
                low(0)
                gate_product(2)
                low(1)
                low(2)
                gate_product(3)
                low(3)
                u = GP.unit["NRM"]
                dve.wait_ge(L1.evac[GP.set[u]], evacs(GP, g, u))
                for name in ("O01", "O23", "O45", "O67"):
                    add_head(dve, g, name, chain)
                link(nc.vector.memset(G[NS:P, TP:T], 0.0))
                chain_restart()

            nc.vector.memset(gs_tmp[:], 0.0).then_inc(x_final, 1)
            dve.wait_ge(g_rows_loaded, 16)
            for s in range(NSUP + 1):
                n = P if s < NSUP else NS
                dve.wait_ge(y_root, s + 1)
                nc.vector.reciprocal(y_rms[0:n, s:s + 1], y_rms[0:n, s:s + 1]).then_inc(y_inverse, 1)
                dve.wait_ge(y_inverse, s + 1)
                nc.vector.scalar_tensor_tensor(out=y_rows[0:n, s, :], in0=ps_y[s % 3][0:n].rearrange("p a n -> p (a n)"),
                                               scalar=y_rms[0:n, s:s + 1], in1=g_rows[0:n, :], op0=ALU.mult,
                                               op1=ALU.mult).then_inc(y_evac, 1)

        @block.tensor
        def _(pe):
            pe.wait_ge(consts_ready, 1)
            pe.wait_ge(c_loaded, 32)
            for k in range(KD):
                last = nc.tensor.transpose(X[0][:, k * NC_:(k + 1) * NC_], c_rows[:, k * P:(k + 1) * P],
                                           ident[0:NC_, 0:NC_])
            last.then_inc(cT_done, 1)
            pe.wait_ge(vec_loaded, 16 * 6)
            nc.tensor.transpose(X[1][:, 0:NVEC], vec_rows, ident[0:NVEC, 0:NVEC]).then_inc(vT_done, 1)
            pe.wait_ge(vT_done, 1)
            pe.sem_inc(mini_done, 1)
            pe.sem_inc(hist_T, 2)
            for s in range(NSUP + 1):
                n = P if s < NSUP else NS
                pe.wait_ge(x_loaded[s], 16)
                if s >= 2:
                    pe.wait_ge(xT_ready, s - 1)
                for k in range(KD):
                    last = nc.tensor.transpose(ps[s % 2][:, k // 4, (k % 4) * P:(k % 4) * P + n],
                                               xrow[s][0:n, k * P:(k + 1) * P], ident[0:n, 0:n])
                last.then_inc(xT_done, 1)
            pe.wait_ge(cs_ready, 1)
            pe.wait_ge(vec_ready, 1)
            pe.wait_ge(xT_ready, NSUP + 1)
            norm_sums(pe, 0)
            def mod_turn(i):
                pe.wait_ge(mod_rows_out, i + 1)
                for m in range(4):
                    c = (4 * (i % 2) + m) * NC_
                    last = nc.tensor.transpose(ps[0][:, i // 2, c:c + NC_],
                                               mod_rows[:, i * 512 + m * P:i * 512 + (m + 1) * P],
                                               ident[0:NC_, 0:NC_])
                return last

            for i in range(6):
                pe.wait_ge(ada0_loaded[i], 16)
                if i >= 2:
                    pe.wait_ge(mod_rows_out, i - 1)
                src = ada0[i] if i < 4 else ada0_gate[:, i - 4]
                for k in range(KD):
                    last = nc.tensor.matmul(X[i % 2][0:NC_, :], csT[:, k, :], src[:, k, :], start=(k == 0),
                                            stop=(k == KD - 1))
                last.then_inc(mod_rows_done, 1)
                if i % 2:
                    mod_turn(i - 1)
                    mod_turn(i).then_inc(mod_done, 1)
            h_wait(pe, 0)
            pe.wait_ge(gate_ready, 1)
            pe.sem_inc(L0.unit_done, 3)

            def start_sets(lay):
                pe.sem_inc(lay.evac[0], 1)
                pe.sem_inc(lay.evac[1], 1)

            start_sets(L0)
            with pe.Fori(0, NG) as g:
                def hist_mini(i):
                    pe.wait_ge(hist_evac, g * KG + i + 1)
                    pe.wait_ge(hist_loaded[i % 2], g * 32 + (i // 2) * 16 + 16)
                    nc.tensor.transpose(X[0][:, 0:NB * BUF], hist[:, i % 2, :], ident[0:NB * BUF, 0:NB * BUF])\
                        .then_inc(hist_T, 1)

                def ada_turn():
                    return nc.tensor.transpose(X[1][:, 2 * P:2 * P + NC_], mod_row[:], ident[0:NC_, 0:NC_])

                def ada_mini(a, mini):
                    wait_apart(pe, mini_free, g * MINIS + mini + 1)
                    if mini >= 6:
                        ada_turn()
                    pe.wait_ge(ada_loaded, g * 96 + a * 16 + 16)
                    for k in range(KD):
                        last = nc.tensor.matmul(X[1][0:NC_, P:2 * P], csT[:, k, :], ada_stage[:, k, :], start=(k == 0),
                                                stop=(k == KD - 1))
                    last.then_inc(mini_done, 1)

                def tail_mini(i):
                    u = PP.unit[f"U{i}"]
                    wait_apart(pe, L0.evac[PP.set[u]], evacs(PP, g, u))
                    wait_apart(pe, mini_free, g * MINIS + (1 + i) + 1)
                    if i == 0:
                        ada_turn()
                    nc.tensor.transpose(X[1][0:NS + BUF, 0:P], tail[:], ident[:]).then_inc(mini_done, 1)

                for name in PP.names:
                    if name[0] == "U":
                        hist_mini(int(name[1]))
                    if name[0] in "UZ":
                        project(pe, L0, PP, g, name)
                    elif name[0] == "G":
                        project_inner(pe, L0, PP, g, name, diff_ready)
                    else:
                        project_inner(pe, L0, PP, g, name, L0.act_ready)
                    j = PP.slot[name]
                    if j == 0:
                        ada_mini(0, 0)
                    if 1 <= j <= 4:
                        tail_mini(j - 1)
                    if 5 <= j <= 9:
                        ada_mini(j - 4, j)
                    if j == 10:
                        wait_apart(pe, mini_free, g * MINIS + MINIS)
                        ada_turn().then_inc(mini_done, 1)

            norm_sums(pe, 1)
            pe.sem_inc(L1.unit_done, 3)
            pe.wait_ge(wgl_lo, 1)
            for t, (n0, width) in enumerate(NT):
                pe.wait_ge(h_ready, 13 + (13 if t == 2 else 4 * (t + 1)))
                pe.wait_ge(h_odd_ready, 12 + 4 * (t + 1))
                for k in range(KD):
                    for pas, (w, a) in enumerate(((w_gl_hi, h_hi), (w_gl_hi, h_lo), (w_gl_lo, h_hi))):
                        last = nc.tensor.matmul(ps[0][0:RANK, t, 0:width], w[:, k, :], a[:, k, n0:n0 + width],
                                                start=(k == 0 and pas == 0), stop=(k == KD - 1 and pas == 2))
            last.then_inc(gl_done, 1)
            pe.wait_ge(gl_ready, 1)
            start_sets(L1)
            with pe.Fori(0, NG) as g:
                def v_transpose(i):
                    u = GP.unit[f"VT{i}"]
                    src = GP.unit[f"V{i}"]
                    set_ready(pe, L1, GP, g, u)
                    pe.wait_ge(L1.evac[GP.set[src]], evacs(GP, g, src))
                    for s in range(NSUP + 1):
                        n = P if s < NSUP else NS
                        last = nc.tensor.transpose(ps[GP.set[u]][0:n, s // 4, (s % 4) * P:(s % 4 + 1) * P],
                                                   vT[i % 2][:, s * P:s * P + n], ident[:])
                    last.then_inc(L1.unit_done, 1)

                def log_decay():
                    u = GP.unit["LG"]
                    set_ready(pe, L1, GP, g, u)
                    pe.wait_ge(wup_loaded, g * 48 + 48)
                    for t, (n0, width) in enumerate(NT):
                        last = nc.tensor.matmul(ps[GP.set[u]][:, t, 0:width], w_up[32 * t:32 * t + RANK, :],
                                                glT[32 * t:32 * t + RANK, 0:width],
                                                start=True, stop=True)
                    last.then_inc(L1.unit_done, 1)

                filled = [0]

                def fill(n):
                    for f in range(filled[0], filled[0] + n):
                        name, k = f"Z{f // KD}", f % KD
                        u = GP.unit[name]
                        if k == 0:
                            set_ready(pe, L1, GP, g, u)
                            slot_ready(pe, L1, GP, g, name)
                        last = product_step(GP.slot[name] % 2, GP.set[u], k, KD, w8, h_hi, h_lo)
                        if k == KD - 1:
                            last.then_inc(L1.unit_done, 1)
                    filled[0] += n

                def scores(s):
                    pe.wait_ge(kp_ready, g * NSUP + s + 1)
                    pe.wait_ge(qd_ready, g * NSUP + s + 1)
                    if s >= 1:
                        pe.wait_ge(att_ready, g * NSUP + s)
                    else:
                        pe.wait_ge(smp_attr, g + 1)
                    for b in range(4):
                        last = nc.tensor.matmul(X[0][:, b * CH:(b + 1) * CH], Kp[:, b, :], qd[:, b * CH:(b + 1) * CH],
                                                start=True, stop=True)
                    last.then_inc(att_done, 1)

                def key_rows(s):
                    pe.wait_ge(ks_ready, g * NSUP + s + 1)
                    if s >= 1:
                        pe.wait_ge(ksT_ready, g * NSUP + s)
                    else:
                        pe.wait_ge(smp_ksT, g + 1)
                    nc.tensor.transpose(ps[1][:, 1, 0:P], ks[:], ident[:]).then_inc(kT_done, 1)

                def output(s):
                    pe.wait_ge(att_ready, g * NSUP + s + 1)
                    if s >= 1:
                        pe.wait_ge(o_evac, g * NSUP + s)
                    for e in range(KG):
                        last = nc.tensor.matmul(ps[1][:, 0, e * P:(e + 1) * P], v[:, s, e * P:(e + 1) * P],
                                                att[:, s % 2, :], start=(e == 0), stop=(s == 0 and e == KG - 1),
                                                skip_group_check=True)
                    if s:
                        pe.wait_ge(S_ready, g * NSUP + s)
                    pe.wait_ge(qs_ready, g * NSUP + s + 1)
                    if s:
                        for e in range(KG):
                            last = nc.tensor.matmul(ps[1][:, 0, e * P:(e + 1) * P], S[:, e * P:(e + 1) * P],
                                                    qs[:], start=False, stop=(e == KG - 1), skip_group_check=True)
                    last.then_inc(o_done, 1)

                def update(s):
                    pe.wait_ge(ksT_ready, g * NSUP + s + 1)
                    if s >= 3:
                        pe.wait_ge(s0_ready, g * NB + s - 2)
                    nc.tensor.matmul(ps[1][:, 2, :], ksT[:, s % 2, :], v[:, s, :], start=True,
                                     stop=True).then_inc(upd_done, 1)

                def sample_scores():
                    set_ready(pe, L1, GP, g, GP.unit["ATT"])
                    pe.wait_ge(smp_ready, g + 1)
                    nc.tensor.matmul(X[0][0:NS, 0:NS], ki_s[:], qd_s[:], start=True, stop=True).then_inc(smp_att, 1)
                    nc.tensor.transpose(ps[1][0:NS, 1, 0:P], ks_s[:], ident[:]).then_inc(smp_kT, 1)

                def sample_intra():
                    pe.wait_ge(smp_attr, g + 1)
                    for e in range(KG):
                        nc.tensor.matmul(X[1][:, 256 + e * NS:256 + (e + 1) * NS], v[0:NS, NSUP, e * P:(e + 1) * P],
                                         att_s[:], start=(e == 0), stop=False, skip_group_check=True)

                def sample(b):
                    pe.wait_ge(s0_loaded[b % 4], g * 32 + (b // 4) * 16 + 16)
                    for e in range(KG):
                        c = 256 + e * NS + b * TS
                        last = nc.tensor.matmul(X[1][:, c:c + TS], v[:, b, e * P:(e + 1) * P],
                                                qd_s[:, b * TS:(b + 1) * TS], start=False,
                                                stop=(b == NB - 1 and e == KG - 1), skip_group_check=True)
                    if b == NB - 1:
                        last.then_inc(smp_o_done, 1)
                    pe.wait_ge(ksm_ready, g * NB + b + 1)
                    if b + 2 < NSUP:
                        pe.wait_ge(S_ready, g * NSUP + b + 3)
                    else:
                        pe.wait_ge(s0_ready, g * NB + b)
                    nc.tensor.matmul(ps[1][:, 2, :], ksm[:, b % 2, :], v[0:NS, NSUP, :], start=True,
                                     stop=True).then_inc(smp_upd, 1)

                def mean_square(s):
                    n = P if s < NSUP else NS
                    pe.wait_ge(osum_ready, g * (NSUP + 1) + s + 1)
                    nc.tensor.matmul(X[1][0:n, s:s + 1], sqo[s % 2][:, 0:n], ones[:, 0:1], start=False,
                                     stop=True, skip_group_check=True).then_inc(oms_done, 1)

                for name in ("Q", "K"):
                    project(pe, L1, GP, g, name)
                log_decay()
                project(pe, L1, GP, g, "V0")
                project(pe, L1, GP, g, "V1")
                v_transpose(0)
                project(pe, L1, GP, g, "V2")
                v_transpose(1)
                project(pe, L1, GP, g, "V3")
                v_transpose(2)
                fill(3)
                v_transpose(3)
                fill(1)
                sample_scores()
                fill(1)
                scores(0)
                key_rows(0)
                sample_intra()
                fill(FILL_START - 5)
                for s in range(NSUP + 2):
                    if s <= NSUP:
                        fill(1)
                    if s + 1 < NSUP:
                        scores(s + 1)
                        key_rows(s + 1)
                    if s < NSUP:
                        output(s)
                        update(s)
                        fill(FILL_STEP - 1)
                    if 1 <= s <= NSUP:
                        mean_square(s - 1)
                    if s >= 2:
                        sample(s - 2)
                pe.sem_inc(L1.unit_done, 1)
                u = GP.unit["Z3"]
                set_ready(pe, L1, GP, g, u)
                slot_ready(pe, L1, GP, g, "Z3")
                for k in range(KD):
                    last = product_step(GP.slot["Z3"] % 2, GP.set[u], k, KD, w8, h_hi, h_lo)
                    if k == 1:
                        pe.wait_ge(smp_o_evac, g + 1)
                        mean_square(NSUP)
                last.then_inc(L1.unit_done, 1)
                u = GP.unit["NRM"]
                set_ready(pe, L1, GP, g, u)
                pe.wait_ge(odiag_ready, g + 1)
                for t, (n0, width) in enumerate(NT):
                    last = nc.tensor.matmul(ps[GP.set[u]][:, t, 0:width], ones[:], rms_diag[:, n0:n0 + width],
                                            start=True, stop=True)
                last.then_inc(L1.unit_done, 1)
                for name in ("O01", "O23", "O45", "O67"):
                    project_inner(pe, L1, GP, g, name, L1.act_ready)

            pe.wait_ge(x_final, 2)
            for s in range(NSUP + 1):
                n = P if s < NSUP else NS
                if s >= 3:
                    pe.wait_ge(y_evac, s - 2)
                for k in range(KD):
                    last = nc.tensor.transpose(ps_y[s % 3][0:n, k // 4, (k % 4) * P:(k % 4 + 1) * P],
                                               xT[:, k, s * P:s * P + n], ident[:])
                last.then_inc(yT_done, 1)


_INS = ["x_prompt", "x_sample", "c_prompt", "c_sample", "state_pool", "state_gla", "ada_w", "ada_b", "norm_g",
        "pool_w_in", "pool_w_grp", "pool_scale", "pool_w_out", "gla_w_in", "gla_w_gate_up", "gla_b_gate",
        "gla_norm_g", "gla_w_out", "final_g"]
_OUTS = [("y_prompt", (1, TP, D)), ("y_sample", (NB, TS, D)), ("new_pool_prompt", (1, 1, BUF, DI)),
         ("new_gla_prompt", (1, 1, NG, P, GW)), ("new_pool_sample", (1, NB, BUF, DI)),
         ("new_gla_sample", (1, NB, NG, P, GW))]


def kernel(**inputs):
    import numpy as _np
    import concourse.bacc as _bacc
    from concourse import mybir as _mybir
    from concourse.bass_utils import run_bass_kernel_spmd as _run

    nc = _bacc.Bacc("TRN2", target_bir_lowering=False, num_devices=1)
    arrays, args = {}, []
    for name in _INS:
        a = _np.ascontiguousarray(inputs[name])
        arrays[f"in_{name}"] = a
        args.append(nc.dram_tensor(f"in_{name}", a.shape, _mybir.dt.from_np(a.dtype), kind="ExternalInput").ap())
    for name, shape in _OUTS:
        args.append(nc.dram_tensor(f"out_{name}", shape, _mybir.dt.float32, kind="ExternalOutput").ap())
    trunk(nc, *args)
    r = _run(nc, [arrays], core_ids=[0])
    return tuple(r.results[0][f"out_{name}"] for name, _ in _OUTS)
```
